# Optimizing a Trainium2 kernel written in Bass

```python
import math
import jax, jax.numpy as jnp
from jax import lax
import numpy as np

D_MODEL = 1024
BATCH = 1
SEQ = 1024
DEPTH = 1
DEC_BATCH = 8
DEC_SEQ = 1
PAST_LEN = 8192
PAGE_SIZE = 128

MIX_WIDTH = D_MODEL
HEAD_DIM = 64
ATTN_WIDTH = MIX_WIDTH // 2
N_HEADS = ATTN_WIDTH // HEAD_DIM
KV_HEADS = 2
REP = N_HEADS // KV_HEADS
WINDOW = 128
ATTN_BLOCK = WINDOW
ATTN_SCALE = HEAD_DIM ** -0.5
ROPE_THETA = 10000.0
SSM_WIDTH = MIX_WIDTH - ATTN_WIDTH
SSM_HEAD_DIM = 64
SSM_HEADS = SSM_WIDTH // SSM_HEAD_DIM
SSM_GROUPS = 2
HEADS_PER_GROUP = SSM_HEADS // SSM_GROUPS
SSM_STATE = 128
CONV_K = 4
CONV_DIM = SSM_WIDTH + 2 * SSM_GROUPS * SSM_STATE
SSD_CHUNK = 128
N_EGROUPS = 4
EXP_PER_GROUP = 8
N_EXPERTS = N_EGROUPS * EXP_PER_GROUP
TOP_K = 2
EXPERT_FF = D_MODEL // 8
EPS = 1e-6
Q_END = N_HEADS * HEAD_DIM
K_END = Q_END + KV_HEADS * HEAD_DIM
V_END = K_END + KV_HEADS * HEAD_DIM
Z_END = V_END + SSM_WIDTH
XBC_END = Z_END + CONV_DIM
IN_DIM = XBC_END + SSM_HEADS

kernel_name = "hymba_swa_sink_ssd_hiermoe_step"

def rms_norm(x, g):
    xf = x.astype(jnp.float32)
    xf = xf * lax.rsqrt(jnp.mean(xf * xf, axis=-1, keepdims=True) + EPS)
    return (xf * g.astype(jnp.float32)).astype(x.dtype)

def rope(x, pos):
    inv = 1.0 / (ROPE_THETA ** (jnp.arange(0, HEAD_DIM, 2, dtype=jnp.float32) / HEAD_DIM))
    ang = pos.astype(jnp.float32)[:, None] * inv[None, :]
    cos = jnp.cos(ang)[:, None, :]
    sin = jnp.sin(ang)[:, None, :]
    xf = x.astype(jnp.float32)
    x1, x2 = xf[..., :HEAD_DIM // 2], xf[..., HEAD_DIM // 2:]
    return jnp.concatenate([x1 * cos - x2 * sin, x2 * cos + x1 * sin], axis=-1).astype(x.dtype)

def sink_attend(q, k, v, mask, sinks):
    s = jnp.einsum('...qkrd,...skd->...krqs', q, k).astype(jnp.float32) * ATTN_SCALE
    s = jnp.where(mask, s, -jnp.inf)
    sink = sinks.astype(jnp.float32).reshape(KV_HEADS, REP, 1, 1)
    m = jnp.maximum(jnp.max(s, axis=-1, keepdims=True), sink)
    p = jnp.exp(s - m)
    p = p / (jnp.sum(p, axis=-1, keepdims=True) + jnp.exp(sink - m))
    return jnp.einsum('...krqs,...skd->...qkrd', p.astype(v.dtype), v)

def swa_banded(q, k, v, sinks):
    bt, L = q.shape[:2]
    nb = L // ATTN_BLOCK
    qb = q.reshape(bt, nb, ATTN_BLOCK, KV_HEADS, REP, HEAD_DIM)

    def with_prev(t):
        tb = t.reshape(bt, nb, ATTN_BLOCK, KV_HEADS, HEAD_DIM)
        prev = jnp.concatenate([jnp.zeros_like(tb[:, :1]), tb[:, :-1]], axis=1)
        return jnp.concatenate([prev, tb], axis=2)

    kb, vb = with_prev(k), with_prev(v)
    q_off = jnp.arange(ATTN_BLOCK)[:, None]
    k_off = jnp.arange(2 * ATTN_BLOCK)[None, :] - ATTN_BLOCK
    rel = q_off - k_off
    band = (rel >= 0) & (rel < WINDOW)
    in_seq = (jnp.arange(nb)[:, None, None] > 0) | (k_off[None] >= 0)
    mask = (band[None] & in_seq)[:, None, None]
    o = sink_attend(qb, kb, vb, mask, sinks)
    return o.reshape(bt, L, N_HEADS * HEAD_DIM)

def swa_cached(q, k, v, past_k, past_v, pos, sinks):
    bt, L = q.shape[:2]
    wc = past_k.shape[1]
    k_all = jnp.concatenate([past_k.astype(k.dtype), k], axis=1)
    v_all = jnp.concatenate([past_v.astype(v.dtype), v], axis=1)
    k_pos = jnp.concatenate([PAST_LEN - wc + jnp.arange(wc, dtype=jnp.int32), pos])
    rel = pos[:, None] - k_pos[None, :]
    mask = (rel >= 0) & (rel < WINDOW)
    o = sink_attend(q, k_all, v_all, mask, sinks)
    return o.reshape(bt, L, N_HEADS * HEAD_DIM), k_all[:, -wc:], v_all[:, -wc:]

def ssd_scan(x, dt, a, b_in, c_in, d_skip, h0):
    bt, L = x.shape[:2]
    cl = SSD_CHUNK if L % SSD_CHUNK == 0 else L
    nc = L // cl
    xr = x.astype(jnp.float32).reshape(bt, nc, cl, SSM_GROUPS, HEADS_PER_GROUP, SSM_HEAD_DIM)
    dtr = dt.reshape(bt, nc, cl, SSM_GROUPS, HEADS_PER_GROUP)
    xdt = xr * dtr[..., None]
    bc = b_in.astype(jnp.float32).reshape(bt, nc, cl, SSM_GROUPS, SSM_STATE)
    cc = c_in.astype(jnp.float32).reshape(bt, nc, cl, SSM_GROUPS, SSM_STATE)
    a_cum = jnp.cumsum(dtr * a, axis=2)
    seg = a_cum[:, :, :, None] - a_cum[:, :, None, :]
    causal = jnp.tril(jnp.ones((cl, cl), dtype=bool))[:, :, None, None]
    decay = jnp.exp(jnp.where(causal, seg, -jnp.inf))
    cb = jnp.einsum('bclgn,bcsgn->bclsg', cc, bc)
    y_diag = jnp.einsum('bclsge,bcsgep->bclgep', cb[..., None] * decay, xdt)
    decay_to_end = jnp.exp(a_cum[:, :, -1:] - a_cum)
    chunk_states = jnp.einsum('bclgn,bclge,bclgep->bcgepn', bc, decay_to_end, xdt)
    chunk_decay = jnp.exp(a_cum[:, :, -1])

    def step(h, inp):
        s, dcy = inp
        return dcy[..., None, None] * h + s, h

    h_last, h_in = lax.scan(step, h0, (jnp.moveaxis(chunk_states, 1, 0), jnp.moveaxis(chunk_decay, 1, 0)))
    h_in = jnp.moveaxis(h_in, 0, 1)
    y_off = jnp.einsum('bclgn,bcgepn,bclge->bclgep', cc, h_in, jnp.exp(a_cum))
    y = y_diag + y_off + d_skip.astype(jnp.float32)[..., None] * xr
    return y.reshape(bt, L, SSM_WIDTH), h_last

def ssd_mixer(z, xbc, dt_raw, conv_prev, h0, conv_w, conv_b, dt_bias, a_log, d_skip, norm_w):
    bt, L, _ = xbc.shape
    full = jnp.concatenate([conv_prev.astype(xbc.dtype), xbc], axis=1)
    new_conv = full[:, full.shape[1] - (CONV_K - 1):]
    conv = lax.conv_general_dilated(full, conv_w[:, None, :].astype(full.dtype), (1,), 'VALID',
                                    dimension_numbers=('NWC', 'WIO', 'NWC'),
                                    feature_group_count=CONV_DIM)
    xbc = jax.nn.silu(conv + conv_b.astype(conv.dtype))
    xs, bs, cs = jnp.split(xbc, [SSM_WIDTH, SSM_WIDTH + SSM_GROUPS * SSM_STATE], axis=-1)
    xs = xs.reshape(bt, L, SSM_GROUPS, HEADS_PER_GROUP, SSM_HEAD_DIM)
    bs = bs.reshape(bt, L, SSM_GROUPS, SSM_STATE)
    cs = cs.reshape(bt, L, SSM_GROUPS, SSM_STATE)
    dt = jax.nn.softplus(dt_raw.astype(jnp.float32) + dt_bias.astype(jnp.float32))
    dt = dt.reshape(bt, L, SSM_GROUPS, HEADS_PER_GROUP)
    a = -jnp.exp(a_log.astype(jnp.float32)).reshape(SSM_GROUPS, HEADS_PER_GROUP)
    h0 = h0.astype(jnp.float32).reshape(bt, SSM_GROUPS, HEADS_PER_GROUP, SSM_HEAD_DIM, SSM_STATE)
    y, h_last = ssd_scan(xs, dt, a, bs, cs, d_skip.reshape(SSM_GROUPS, HEADS_PER_GROUP), h0)
    g = (y * jax.nn.silu(z.astype(jnp.float32))).reshape(bt, L, SSM_GROUPS, SSM_WIDTH // SSM_GROUPS)
    g = g * lax.rsqrt(jnp.mean(g * g, axis=-1, keepdims=True) + EPS)
    out = (g.reshape(bt, L, SSM_WIDTH) * norm_w.astype(jnp.float32)).astype(z.dtype)
    return out, new_conv, h_last.reshape(bt, SSM_HEADS, SSM_HEAD_DIM, SSM_STATE)

def hier_moe(x, w_grp, b_grp, w_exp, b_exp, w_gate, w_up, w_down):
    bt, L, D = x.shape
    t = x.reshape(bt * L, D)
    g_prob = jax.nn.softmax((t @ w_grp).astype(jnp.float32) + b_grp.astype(jnp.float32), axis=-1)
    g_top, g_idx = lax.top_k(g_prob, 1)
    e_logits = ((t @ w_exp).astype(jnp.float32) + b_exp.astype(jnp.float32)).reshape(-1, N_EGROUPS, EXP_PER_GROUP)
    e_logits = jnp.take_along_axis(e_logits, g_idx[:, :, None], axis=1)[:, 0]
    e_top, e_idx = lax.top_k(jax.nn.softmax(e_logits, axis=-1), TOP_K)
    gate = g_top * (e_top / jnp.sum(e_top, axis=-1, keepdims=True))
    expert = g_idx * EXP_PER_GROUP + e_idx
    combine = jnp.einsum('tk,tke->te', gate, jax.nn.one_hot(expert, N_EXPERTS, dtype=jnp.float32))
    hid = jax.nn.silu(jnp.einsum('td,edf->tef', t, w_gate)) * jnp.einsum('td,edf->tef', t, w_up)
    hid = hid * combine[:, :, None].astype(hid.dtype)
    y = jnp.einsum('tef,efd->td', hid, w_down)
    return y.reshape(bt, L, D).astype(x.dtype)

def trunk_layer(x, pos, past_k, past_v, conv_prev, h0, w):
    bt, L, _ = x.shape
    xn = rms_norm(x, w['norm1'])
    proj = xn @ w['w_in']
    q, k, v, z, xbc, dt_raw = jnp.split(proj, [Q_END, K_END, V_END, Z_END, XBC_END], axis=-1)
    q = rope(rms_norm(q.reshape(bt, L, N_HEADS, HEAD_DIM), w['q_norm']), pos)
    k = rope(rms_norm(k.reshape(bt, L, KV_HEADS, HEAD_DIM), w['k_norm']), pos)
    v = v.reshape(bt, L, KV_HEADS, HEAD_DIM)
    qg = q.reshape(bt, L, KV_HEADS, REP, HEAD_DIM)
    if past_k is None:
        attn = swa_banded(qg, k, v, w['sinks'])
        keep = min(WINDOW, L)
        new_k, new_v = k[:, L - keep:], v[:, L - keep:]
    else:
        attn, new_k, new_v = swa_cached(qg, k, v, past_k, past_v, pos, w['sinks'])
    ssm, new_conv, new_h = ssd_mixer(z, xbc, dt_raw, conv_prev, h0, w['conv_w'], w['conv_b'],
                                     w['dt_bias'], w['a_log'], w['d_skip'], w['ssm_norm'])
    h = x + jnp.concatenate([attn.astype(x.dtype), ssm], axis=-1) @ w['w_out']
    out = h + hier_moe(rms_norm(h, w['norm2']), w['w_grp'], w['b_grp'], w['w_exp'], w['b_exp'],
                       w['w_gate'], w['w_up'], w['w_down'])
    return out, new_k, new_v, new_conv, new_h

def setup_inputs(seed: int = 0) -> dict:
    key = jax.random.key(seed)
    ks = jax.random.split(key, 26)
    f32 = jnp.float32
    nrm = lambda k, s, sc: jax.random.normal(k, s, f32) * sc
    win = min(WINDOW, PAST_LEN)
    dt0 = jnp.exp(jax.random.uniform(ks[14], (DEPTH, SSM_HEADS), f32) * (math.log(0.1) - math.log(0.001)) + math.log(0.001))
    return {
        "x_prompt": nrm(ks[0], (BATCH, SEQ, D_MODEL), 1.0),
        "x_sample": nrm(ks[1], (DEC_BATCH, DEC_SEQ, D_MODEL), 1.0),
        "cache_win_k": nrm(ks[2], (DEPTH, DEC_BATCH, win, KV_HEADS, HEAD_DIM), 1.0),
        "cache_win_v": nrm(ks[3], (DEPTH, DEC_BATCH, win, KV_HEADS, HEAD_DIM), 1.0),
        "state_conv": nrm(ks[4], (DEPTH, DEC_BATCH, CONV_K - 1, CONV_DIM), 1.0),
        "state_ssm": nrm(ks[5], (DEPTH, DEC_BATCH, SSM_HEADS, SSM_HEAD_DIM, SSM_STATE), 0.1),
        "norm1": 1.0 + nrm(ks[6], (DEPTH, D_MODEL), 0.02),
        "w_in": nrm(ks[7], (DEPTH, D_MODEL, IN_DIM), D_MODEL ** -0.5),
        "q_norm": 1.0 + nrm(ks[8], (DEPTH, HEAD_DIM), 0.02),
        "k_norm": 1.0 + nrm(ks[9], (DEPTH, HEAD_DIM), 0.02),
        "sinks": nrm(ks[10], (DEPTH, N_HEADS), 0.5),
        "conv_w": nrm(ks[11], (DEPTH, CONV_K, CONV_DIM), CONV_K ** -0.5),
        "conv_b": nrm(ks[12], (DEPTH, CONV_DIM), 0.02),
        "dt_bias": dt0 + jnp.log(-jnp.expm1(-dt0)),
        "a_log": jnp.log(jax.random.uniform(ks[13], (DEPTH, SSM_HEADS), f32, 1.0, 16.0)),
        "d_skip": 1.0 + nrm(ks[15], (DEPTH, SSM_HEADS), 0.02),
        "ssm_norm": 1.0 + nrm(ks[16], (DEPTH, SSM_WIDTH), 0.02),
        "w_out": nrm(ks[17], (DEPTH, MIX_WIDTH, D_MODEL), MIX_WIDTH ** -0.5),
        "norm2": 1.0 + nrm(ks[18], (DEPTH, D_MODEL), 0.02),
        "w_grp": nrm(ks[19], (DEPTH, D_MODEL, N_EGROUPS), D_MODEL ** -0.5),
        "b_grp": nrm(ks[20], (DEPTH, N_EGROUPS), 0.01),
        "w_exp": nrm(ks[21], (DEPTH, D_MODEL, N_EXPERTS), D_MODEL ** -0.5),
        "b_exp": nrm(ks[22], (DEPTH, N_EXPERTS), 0.01),
        "w_gate": nrm(ks[23], (DEPTH, N_EXPERTS, D_MODEL, EXPERT_FF), D_MODEL ** -0.5),
        "w_up": nrm(ks[24], (DEPTH, N_EXPERTS, D_MODEL, EXPERT_FF), D_MODEL ** -0.5),
        "w_down": nrm(ks[25], (DEPTH, N_EXPERTS, EXPERT_FF, D_MODEL), EXPERT_FF ** -0.5),
    }

def reference(x_prompt, x_sample, cache_win_k, cache_win_v, state_conv, state_ssm, norm1, w_in,
              q_norm, k_norm, sinks, conv_w, conv_b, dt_bias, a_log, d_skip, ssm_norm, w_out,
              norm2, w_grp, b_grp, w_exp, b_exp, w_gate, w_up, w_down):
    bp, lp = x_prompt.shape[:2]
    pos_p = jnp.arange(lp, dtype=jnp.int32)
    pos_s = PAST_LEN + jnp.arange(x_sample.shape[1], dtype=jnp.int32)
    hp, hs = x_prompt, x_sample
    kp_l, vp_l, cp_l, sp_l, ks_l, vs_l, cs_l, ss_l = [], [], [], [], [], [], [], []
    for l in range(DEPTH):
        w = dict(norm1=norm1[l], w_in=w_in[l], q_norm=q_norm[l], k_norm=k_norm[l], sinks=sinks[l],
                 conv_w=conv_w[l], conv_b=conv_b[l], dt_bias=dt_bias[l], a_log=a_log[l],
                 d_skip=d_skip[l], ssm_norm=ssm_norm[l], w_out=w_out[l], norm2=norm2[l],
                 w_grp=w_grp[l], b_grp=b_grp[l], w_exp=w_exp[l], b_exp=b_exp[l],
                 w_gate=w_gate[l], w_up=w_up[l], w_down=w_down[l])
        conv0 = jnp.zeros((bp, CONV_K - 1, CONV_DIM), x_prompt.dtype)
        h0 = jnp.zeros((bp, SSM_HEADS, SSM_HEAD_DIM, SSM_STATE), jnp.float32)
        hp, kp, vp, cp, sp = trunk_layer(hp, pos_p, None, None, conv0, h0, w)
        hs, ks, vs, cs, ss = trunk_layer(hs, pos_s, cache_win_k[l], cache_win_v[l],
                                         state_conv[l], state_ssm[l], w)
        kp_l.append(kp); vp_l.append(vp); cp_l.append(cp); sp_l.append(sp)
        ks_l.append(ks); vs_l.append(vs); cs_l.append(cs); ss_l.append(ss)
    return (hp, hs, jnp.stack(kp_l), jnp.stack(vp_l), jnp.stack(cp_l), jnp.stack(sp_l),
            jnp.stack(ks_l), jnp.stack(vs_l), jnp.stack(cs_l), jnp.stack(ss_l))


_drawn_inputs = setup_inputs


def setup_inputs(seed=0):
    import zlib

    import numpy as np

    out = dict(_drawn_inputs(seed))
    spreads = {}
    factors = {'q_norm': 26.912,
     'sinks': 53.288,
     'd_skip': 43.608,
     'ssm_norm': 2.67,
     'b_grp': 29.202,
     'b_exp': 15.242,
     'norm2': 4.117}
    for name, (base, spread) in spreads.items():
        noise = np.random.default_rng([zlib.crc32(name.encode()), seed]).standard_normal(out[name].shape)
        drawn = base * np.exp(spread * noise) if base else spread * noise
        out[name] = __import__('jax').numpy.asarray(drawn.astype(out[name].dtype))
    for name, factor in factors.items():
        out[name] = (out[name] * factor).astype(out[name].dtype)
    return out
```

```python
from contextlib import ExitStack

import numpy as np

import concourse.bass as bass
from concourse import mybir
from concourse.alu_op_type import AluOpType as ALU

F32 = mybir.dt.float32
I32 = mybir.dt.int32
U32 = mybir.dt.uint32
ACT = mybir.ActivationFunctionType
AX = mybir.AxisListType

P = 128
D = 1024
KC = D // P
SEQ = 1024
TILES = SEQ // P
DEC = 8
TOKENS = SEQ + DEC
NH, NKV, HD = 8, 2, 64
REP = NH // NKV
PAST = 8192
THETA = 10000.0
SCALE = HD ** -0.5
SH, SG, SP_, SN = 8, 2, 64, 128
CK = 4
CD = SH * SP_ + 2 * SG * SN
CC = CD // P
Q_END = NH * HD
K_END = Q_END + NKV * HD
V_END = K_END + NKV * HD
Z_END = V_END + SH * SP_
XBC_END = Z_END + CD
IN_DIM = XBC_END + SH
NG, EPG = 4, 8
NE = NG * EPG
FF = D // 8
EPS = 1e-6
BIG = 1e30
CHOICES = 2 * TOKENS
SLOT_TILES = (CHOICES + NE * (P - 1)) // P
SLOT_TILES += SLOT_TILES % 2
CREDIT = 2

C_ID, C_TRI, C_STRICT, C_ONES, C_BAND, C_IOTA, C_TILE = 0, 128, 256, 384, 512, 768, 800
C_END = C_TILE + SLOT_TILES


def shape_constants():
    c = np.zeros((P, C_END), np.float32)
    r, q = np.arange(P)[:, None], np.arange(P)[None, :]
    c[:, C_ID:C_ID + P] = r == q
    c[:, C_TRI:C_TRI + P] = r <= q
    c[:, C_STRICT:C_STRICT + P] = r < q
    c[:, C_ONES:C_ONES + P] = 1.0
    c[:, C_BAND:C_BAND + P] = np.where(q > r, 0.0, -BIG)
    c[:, C_BAND + P:C_BAND + 2 * P] = np.where(q <= r, 0.0, -BIG)
    c[:, C_IOTA:C_IOTA + NE] = np.arange(NE)
    c[:, C_TILE:C_TILE + SLOT_TILES] = np.arange(SLOT_TILES)
    return c


def rope_table():
    inv = (1.0 / (np.float32(THETA) ** (np.arange(0, HD, 2, dtype=np.float32) / np.float32(HD)))).astype(np.float32)
    pos = np.concatenate([np.arange(SEQ), np.full(P, PAST)]).astype(np.float32)
    ang = pos[:, None] * inv[None, :]
    return np.concatenate([np.cos(ang), np.sin(ang)], axis=1).astype(np.float32)


def layer_kernel(nc, I, O):
    with ExitStack() as ctx:
        def sb(name, shape, dt=F32):
            return ctx.enter_context(nc.sbuf_tensor(name, shape, dt))

        def sem(name):
            return ctx.enter_context(nc.semaphore(name))

        bank = [ctx.enter_context(nc.psum_tensor(f"bank{n}", [P, 512], F32)) for n in range(8)]
        h_dram = nc.dram_tensor("h_dram", (TOKENS, D), F32, kind="Internal").ap()
        t_dram = nc.dram_tensor("t_dram", (TOKENS, D), F32, kind="Internal").ap()
        y_dram = nc.dram_tensor("y_dram", (SLOT_TILES * P, D), F32, kind="Internal").ap()
        slot_dram = nc.dram_tensor("slot_dram", (P * SLOT_TILES, 1), I32, kind="Internal").ap()

        con = sb("con", [P, C_END])
        ident, tri, strict, ones = (con[:, c:c + P] for c in (C_ID, C_TRI, C_STRICT, C_ONES))
        w_arena = sb("w_arena", [P, KC * IN_DIM])
        w_in = w_arena[:, :].rearrange("p (k n) -> p k n", k=KC)
        w_out = sb("w_out_sb", [P, KC, D])
        w_route = sb("w_route", [P, KC, NG + NE])
        b_route = sb("b_route", [P, NG + NE])
        norm1 = sb("norm1_sb", [P, KC])
        norm2 = sb("norm2_sb", [P, D])
        qk_norm = sb("qk_norm", [P, 2, HD])
        sink = sb("sink", [P, NH])
        sink_col = sb("sink_col", [NH, 1])
        conv_w = sb("conv_w_sb", [P, CC, CK])
        conv_b = sb("conv_b_sb", [P, CC])
        dt_bias = sb("dt_bias_sb", [P, SH])
        a_neg = sb("a_neg", [P, SH])
        d_skip = sb("d_skip_sb", [P, SH])
        d_col = sb("d_col", [SH, 1])
        ssm_norm = sb("ssm_norm_sb", [P, 4])
        neg_half = sb("neg_half", [P, 16])
        eps = sb("eps", [P, 16])
        mask = sb("mask", [P, 2, P])

        x = [sb(f"x{u}", [P, D]) for u in range(2)]
        rope = [sb(f"rope{u}", [P, HD]) for u in range(2)]
        xn = sb("xn", [P, D])
        xT = sb("xT", [P, KC, P])
        junk = sb("junk", [P, D])
        stat = sb("stat", [P, 16])
        rstd = sb("rstd", [P, 16])
        qk = sb("qk", [P, 10, HD])
        qkr = sb("qkr", [P, 10, HD])
        v = sb("v", [P, 2, P])
        qT = sb("qT", [P, REP, P])
        kT = sb("kT", [P, 2, P])
        s = sb("s", [P, NH, 2 * P])
        top = sb("top", [P, 4, NH])
        pT = sb("pT", [P, NKV, 2, REP, P])
        aT = sb("aT", [P, REP, P])
        dt = sb("dt", [P, 5, SH])
        zs = sb("zs", [P, SH * SP_])
        raw = sb("raw", [P, CC, P + CK - 1])
        cv = sb("cv", [P, CC, P])
        xc = sb("xc", [P, CC, P])
        xtok = sb("xtok", [P, SH, SP_])
        btok = sb("btok", [P, SG, P])
        xdt = sb("xdt", [P, SH, SP_])
        xde = sb("xde", [P, SH, SP_])
        xd = sb("xd", [P, SH, SP_])
        cum = sb("cum", [P, 3, SH])
        ecum = sb("ecum", [P, 3, SH])
        cbm = sb("cbm", [P, SG, P])
        m = sb("m", [P, SH, P])
        hT = sb("hT", [P, SH, SP_])
        y = sb("y", [P, SH, SP_])
        gT = sb("gT", [P, 4, P])
        t = sb("t", [P, D])
        tT = xT
        lg = sb("lg", [P, 8 + NE])
        le = sb("le", [P, NG, EPG])
        g8 = sb("g8", [P, 8])
        e8 = sb("e8", [P, 8])
        gi = sb("gi", [P, 8], U32)
        ei = sb("ei", [P, 8], U32)
        fi = sb("fi", [P, 16])
        gmask = sb("gmask", [P, 2, NG])
        rt = sb("rt", [P, 8])
        rexp = sb("rexp", [P, NG])
        onehot = sb("onehot", [P, TILES + 1, 2, NE])
        both = sb("both", [P, NE])
        counted = sb("counted", [P, NE])
        rankc = sb("rankc", [P, NE])
        rprod = sb("rprod", [P, 2, NE])
        rank = sb("rank", [P, TILES + 1, 2])
        gate = sb("gate", [P, TILES + 1, 2])

        keys = pT[:, 0, :, :, :].rearrange("p a b c -> p (a b) c")
        vals = pT[:, 1, :, :, :].rearrange("p a b c -> p (a b) c")
        keysT = xT
        q_blk = sb("q_blk", [P, DEC, NKV, REP])
        flat_s = s[:, :, :].rearrange("p a b -> p (a b)")
        ps = flat_s[0:NH, 0:DEC * P].rearrange("p (b s) -> p b s", b=DEC)
        ps_T = sb("ps_T", [P, DEC, NH])
        m_top = sb("m_top", [NH, 4, DEC])
        st_conv = w_arena[0:DEC, 0:3 * CD].rearrange("p (k c) -> p k c", k=CK - 1)
        st_w = w_arena[0:DEC, 3 * CD:7 * CD].rearrange("p (k c) -> p k c", k=CK)
        st_b = w_arena[0:DEC, 7 * CD:8 * CD]
        st_raw = w_arena[0:DEC, 8 * CD:9 * CD]
        st_acc = w_arena[0:DEC, 9 * CD:10 * CD]
        st_tmp = w_arena[0:DEC, 10 * CD:11 * CD]
        st_xc = w_arena[0:DEC, 11 * CD:12 * CD]
        st_h = w_arena[:, 12 * CD:16 * CD].rearrange("p (b c n) -> p b c n", b=DEC, c=4)
        head_sel = w_arena[0:SH, 16 * CD:16 * CD + SH * SP_]
        flat_cv = cv[:, :, :].rearrange("p a b -> p (a b)")
        st_bx = flat_cv[:, 0:512].rearrange("p (c n) -> p c n", c=4)
        st_ch = flat_cv[:, 512:1024].rearrange("p (c n) -> p c n", c=4)
        st_xT = sb("st_xT", [P, 4, DEC])
        st_zT = sb("st_zT", [P, 4, DEC])
        st_da = sb("st_da", [SH, 2 * DEC + 1])
        st_sc = sb("st_sc", [P, 4, 2 * DEC + 1])
        st_dx = sb("st_dx", [P, 4, DEC])
        st_y = sb("st_y", [P, 4, DEC])
        st_g2 = sb("st_g2", [P, 4, DEC])
        st_n = sb("st_n", [P, SG, DEC])
        st_r = sb("st_r", [P, SG, DEC])

        PAIRS = 2 * (TILES + 1)
        nt = w_arena[:, 17500:17500 + 4 * NE].rearrange("p (a e) -> p a e", a=4)
        pair_prod = w_arena[:, 17700:17700 + PAIRS * NE].rearrange("p (a e) -> p a e", e=NE)
        quo = w_arena[:, 17000:17000 + 4 * PAIRS].rearrange("p (a e) -> p a e", a=4)
        addr = sb("addr", [P, 2, PAIRS], I32)
        tok = sb("tok", [P, TILES + 1], I32)
        zero_i = sb("zero_i", [P, SLOT_TILES], I32)
        slot_tok = sb("slot_tok", [P, SLOT_TILES], I32)
        etile = sb("etile", [1, SLOT_TILES])
        etile_i = sb("etile_i", [1, SLOT_TILES], I32)
        ecmp = w_arena[0:1, 8192:8192 + SLOT_TILES * NE].rearrange("p (j e) -> p j e", e=NE)

        def arena(at, n):
            return w_arena[:, at:at + n]
        wgu = [arena(u * 3072, 2048).rearrange("p (a k f) -> p a k f", a=2, k=KC) for u in range(2)]
        wd = [arena(u * 3072 + 2048, 1024) for u in range(2)]
        xg = [arena(6144 + u * D, D) for u in range(2)]
        xgT = [arena(8192 + u * D, D).rearrange("p (k f) -> p k f", k=KC) for u in range(2)]
        sil = [arena(10240 + u * 256, P) for u in range(2)]
        hid = [arena(10368 + u * 256, P) for u in range(2)]
        hidT = [arena(10752 + u * P, P) for u in range(2)]
        yo = [arena(11008 + u * D, D) for u in range(2)]
        c_h = [arena(13056 + u * 2560, D) for u in range(2)]
        c_y1 = [x[0][:, :], x[1][:, :]]
        c_y2 = [xn[:, :], t[:, :]]
        tok_now = [sb(f"tok_now{u}", [P, 1], I32) for u in range(2)]

        loaded = sem("loaded")
        S = {}
        for name in ("ssq xs xn xm xT projq projz projc qkv dtp dl dta z rawc cumm cum ecd qsq qs qkr qkt qkc sc0 sc1 sc2 sc3 "
                     "se smax pexp prob ptm pta ptb pv at convd xcs xtm xtk xdt xde xd rmm rmin rexpd cbt cbm md ydm yf "
                     "stm std ysq ys yg ytm gt wom hres hsq hs td ttm tt lgm sel gex rsel rankm rankd").split():
            S[name] = sem("s_" + name)
        T = {}
        for name in ("init aneg kT0 kT1 q1 q2 sc1 sc2 sx sp ptm pT pv aT cv1 cv2 dt1 dt2 dt3 xz1 xz2 bc hst yT g sq nrm nr rs gT "
                     "cnt nt slots et zero ssmT ssmC").split():
            T[name] = sem("m_" + name)
        E_ = {}
        for name in ("xT xTe gu sil hid hT hTe dn ya yd tokc").split():
            E_[name] = sem("e_" + name)
        x_in = [sem(f"x_in{u}") for u in range(2)]
        h_out = [sem(f"h_out{u}") for u in range(2)]
        t_out = [sem(f"t_out{u}") for u in range(2)]
        cache_in = sem("cache_in")
        state_in = sem("state_in")
        rows_in = sem("rows_in")
        scattered = sem("scattered")
        zeroed = sem("zeroed")
        slots_in = sem("slots_in")
        e_w = [sem(f"e_w{u}") for u in range(2)]
        e_x = [sem(f"e_x{u}") for u in range(2)]
        e_y = [sem(f"e_y{u}") for u in range(2)]
        e_out = [sem(f"e_out{u}") for u in range(2)]
        c_in = [sem(f"c_in{u}") for u in range(2)]
        c_in1 = [sem(f"c_in1{u}") for u in range(2)]
        c_done = sem("c_done")
        c_out = [sem(f"c_out{u}") for u in range(2)]
        kv_out = sem("kv_out")
        outs = sem("outs")
        block = ctx.enter_context(nc.Block())

        def now(eng, names, tile):
            for name in names.split():
                eng.wait_ge(S[name], tile + (CREDIT + 1))

        def last(eng, names, tile):
            for name in names.split():
                eng.wait_ge(S[name], tile + CREDIT)

        def credit(eng, names):
            for name in names.split():
                eng.sem_inc(S[name], CREDIT)

        flat_x = I["x_prompt"].rearrange("a s d -> (a s) d")
        n_loaded = [0]

        @block.sync
        def _(sp):
            def load(dst, src):
                sp.dma_start(dst, src).then_inc(loaded, 16)
                n_loaded[0] += 16

            def row(name, n):
                return I[name].rearrange("a n -> (a n)").rearrange("(a n) -> a n", a=1).broadcast_to([n, I[name].shape[-1]])

            for u in range(2):
                sp.sem_inc(x_in[u], 32)
            load(con[:, :], I["constants"])
            load(norm1[:, :], I["norm1"].rearrange("a (p k) -> (a p) k", k=KC))
            load(w_in, I["w_in"].rearrange("a (p k) n -> (a p) k n", k=KC))
            load(qk_norm[:, 0, :], row("q_norm", P))
            load(qk_norm[:, 1, :], row("k_norm", P))
            load(sink[:, :], row("sinks", P))
            load(sink_col[:, :], I["sinks"].rearrange("a (n b) -> (a n) b", b=1))
            load(d_col[:, :], I["d_skip"].rearrange("a (n b) -> (a n) b", b=1))
            load(conv_w[:, :, :], I["conv_w_by_channel"])
            load(conv_b[:, :], I["conv_b_by_channel"])
            load(dt_bias[:, :], row("dt_bias", P))
            load(a_neg[:, :], row("a_log", P))
            load(d_skip[:, :], row("d_skip", P))
            load(ssm_norm[:, :], I["ssm_norm_by_channel"])
            for kv in range(NKV):
                load(w_out[kv * HD:(kv + 1) * HD, 0:REP, :],
                     I["w_out"][0, kv * REP * HD:(kv + 1) * REP * HD].rearrange("(r d) n -> d r n", d=HD))
            load(w_out[:, REP:KC, :], I["w_out"][0, NH * HD:].rearrange("(c p) n -> p c n", p=P))
            load(norm2[:, :], row("norm2", P))
            load(w_route[:, :, 0:NG], I["w_grp"].rearrange("a (p k) n -> (a p) k n", k=KC))
            load(w_route[:, :, NG:NG + NE], I["w_exp"].rearrange("a (p k) n -> (a p) k n", k=KC))
            load(b_route[:, 0:NG], row("b_grp", P))
            load(b_route[:, NG:NG + NE], row("b_exp", P))

            with sp.Fori(0, TILES // 2) as pair:
                t0 = pair * 2
                for u in range(2):
                    sp.wait_ge(S["td"], t0 + (u + CREDIT - 1))
                    sp.dma_start(rope[u][:, :], I["rope"][bass.ds(t0 * P + u * P, P), :]).then_inc(x_in[u], 16)
                    sp.wait_ge(h_out[u], 8 * t0 + 16)
                    sp.dma_start(x[u][:, :], flat_x[bass.ds(t0 * P + u * P, P), :]).then_inc(x_in[u], 16)
            sp.wait_ge(h_out[0], 8 * TILES + 16)
            sp.wait_ge(S["td"], TILES + CREDIT - 1)
            sp.dma_start(x[0][0:DEC, :], I["x_sample"].rearrange("b s d -> (b s) d")).then_inc(x_in[0], 16)
            sp.dma_start(rope[0][0:DEC, :], I["rope"][SEQ:SEQ + DEC, :]).then_inc(x_in[0], 16)
            last(sp, "convd pv", TILES)
            sp.dma_start(O["conv_prompt"], raw[:, :, 0:CK - 1]).then_inc(outs, 16)
            ck = I["cache_win_k"].rearrange("a b s k d -> (a s) b (k d)")
            cw = I["cache_win_v"].rearrange("a b s k d -> (a s) b (k d)")
            sp.dma_start(keys[0:P - 1, :, :], ck[1:P]).then_inc(cache_in, 16)
            sp.dma_start(vals[0:P - 1, :, :], cw[1:P]).then_inc(cache_in, 16)
            for name in ("k", "v"):
                o = O[f"win_{name}_sample"].rearrange("a b s k d -> (a b) s (k d)")
                i = I[f"cache_win_{name}"].rearrange("a b s k d -> (a b) s (k d)")
                sp.dma_start(o[:, 0:P - 1, :], i[:, 1:P, :]).then_inc(outs, 16)
            sp.dma_start(O["conv_sample"][0, :, 0:CK - 2, :], I["state_conv"][0, :, 1:CK - 1, :]).then_inc(outs, 16)
            now(sp, "qkr qkv", TILES)
            new_k = qkr[0:DEC, 8:10, :].rearrange("p a b -> p (a b)")
            new_v = v[0:DEC, 1, :]
            sp.dma_start(keys[P - 1:P, :, :], new_k).then_inc(cache_in, 16)
            sp.dma_start(vals[P - 1:P, :, :], new_v).then_inc(cache_in, 16)
            sp.dma_start(O["win_k_sample"].rearrange("a b s k d -> (a b) s (k d)")[:, P - 1, :], new_k).then_inc(outs, 16)
            sp.dma_start(O["win_v_sample"].rearrange("a b s k d -> (a b) s (k d)")[:, P - 1, :], new_v).then_inc(outs, 16)
            now(sp, "projc", TILES)
            sp.dma_start(st_conv, I["state_conv"][0]).then_inc(state_in, 16)
            sp.dma_start(st_w, I["conv_w"].broadcast_to([DEC, CK, CD])).then_inc(state_in, 16)
            sp.dma_start(st_b, row("conv_b", DEC)).then_inc(state_in, 16)
            for b in range(DEC):
                sp.dma_start(st_h[:, b], I["state_ssm"][0, b].rearrange("(c l) p n -> (l p) c n", l=2)).then_inc(state_in, 16)
            now(sp, "rawc", TILES)
            sp.dma_start(O["conv_sample"][0, :, CK - 2, :], st_raw).then_inc(outs, 16)
            sp.wait_ge(T["ssmC"], 1)
            sp.dma_start(O["ssm_prompt"].rearrange("a b (c l) p n -> (a b l p) c n", l=2),
                         flat_cv[:, 0:512].rearrange("p (c n) -> p c n", c=4)).then_inc(outs, 16)
            sp.wait_ge(T["hst"], DEC)
            for b in range(DEC):
                sp.dma_start(O["ssm_sample"][0, b].rearrange("(c l) p n -> (l p) c n", l=2), st_h[:, b]).then_inc(outs, 16)

            sp.wait_ge(outs, N_OUTS)
            sp.wait_ge(T["et"], 1)
            with sp.Fori(0, SLOT_TILES // 2) as pair:
                j0 = pair * 2
                for u in range(2):
                    e = sp.value_load(etile_i[0:1, bass.ds(j0 + u, 1)], min_val=0, max_val=NE - 1)
                    sp.wait_ge(T["et"], 1)
                    sp.wait_ge(E_["dn"], j0 + u + 1)
                    sp.dma_start(wgu[u][:, 0], I["w_gate"][0, bass.ds(e, 1)].rearrange("a (p k) f -> (a p) k f", k=KC)).then_inc(e_w[u], 16)
                    sp.dma_start(wgu[u][:, 1], I["w_up"][0, bass.ds(e, 1)].rearrange("a (p k) f -> (a p) k f", k=KC)).then_inc(e_w[u], 16)
                    sp.dma_start(wd[u], I["w_down"][0, bass.ds(e, 1)].rearrange("a f n -> (a f) n")).then_inc(e_w[u], 16)
            for c in range(TILES + 1):
                n, u = (P, c % 2) if c < TILES else (DEC, c % 2)
                if c >= 2:
                    sp.wait_ge(c_done, c - 1)
                    sp.wait_ge(c_out[u], 16 * (c // 2))
                sp.dma_start(c_h[u][0:n, :], h_dram[c * P:c * P + n, :]).then_inc(c_in[u], 16)
            for u in range(2):
                sp.wait_ge(c_out[u], 16 * ((TILES + 2 - u) // 2))
            sp.wait_ge(outs, N_OUTS)

        def rows(ap, n):
            return ap[0:n]

        def act_front(act, tile, u, n, x_need):
            act.wait_ge(x_in[u], x_need)
            last(act, "xs hs", tile)
            act.activation(junk[0:n, :], x[u][0:n, :], ACT.Square, scale=D ** -0.5, accum_out=stat[0:n, 0:1]).then_inc(S["ssq"], 1)
            now(act, "xs", tile)
            last(act, "xm", tile)
            act.activation(xn[0:n, :], x[u][0:n, :], ACT.Copy, scale=rstd[0:n, 0:1]).then_inc(S["xn"], 1)
            now(act, "projq", tile)
            last(act, "qkr pv dta", tile)
            act.activation(qk[0:n, 0:8, :].rearrange("p a b -> p (a b)"), bank[0][0:n, :], ACT.Copy)
            act.activation(qk[0:n, 8:10, :].rearrange("p a b -> p (a b)"), bank[1][0:n, 0:P], ACT.Copy)
            if n == P:
                act.activation(v[:, 0, :], v[:, 1, :], ACT.Copy)
                act.drain()
            act.activation(v[0:n, 1, :], bank[1][0:n, P:2 * P], ACT.Copy)
            act.activation(dt[0:n, 0, :], bank[1][0:n, 2 * P:2 * P + SH], ACT.Copy).then_inc(S["qkv"], 1)
            now(act, "dtp", tile)
            act.activation(dt[0:n, 2, :], dt[0:n, 1, :], ACT.Exp, scale=-1.0)
            act.drain()
            act.activation(dt[0:n, 2, :], dt[0:n, 2, :], ACT.Ln, bias=1.0).then_inc(S["dl"], 1)

        def act_tail(act, tile, u, n, dram_rows):
            now(act, "hres", tile)
            act.dma_start(h_dram[dram_rows, :], x[u][0:n, :]).then_inc(h_out[u], 16)
            act.drain()
            act.activation(junk[0:n, :], x[u][0:n, :], ACT.Square, scale=D ** -0.5, accum_out=stat[0:n, 13:14]).then_inc(S["hsq"], 1)
            now(act, "td", tile)
            act.dma_start(t_dram[dram_rows, :], t[0:n, :]).then_inc(t_out[u], 16)
            now(act, "ttm", tile)
            act.activation(tT[:, 0:4, 0:n], bank[4][:, 0:4 * n].rearrange("p (k n) -> p k n", k=4), ACT.Copy)
            act.activation(tT[:, 4:8, 0:n], bank[5][:, 0:4 * n].rearrange("p (k n) -> p k n", k=4), ACT.Copy).then_inc(S["tt"], 1)
            now(act, "sel", tile)
            act.activation(rexp[0:n, :], lg[0:n, 0:NG], ACT.Exp, bias=rt[0:n, 0:1], accum_out=rt[0:n, 1:2])
            act.activation(rt[0:n, 3:4], e8[0:n, 1:2], ACT.Exp, bias=rt[0:n, 2:3]).then_inc(S["gex"], 1)

        @block.scalar
        def _(act):
            credit(act, "ssq xn qkv dl z rawc ecd pexp pta at xcs xtk rexpd ysq hsq tt gex")
            for u in range(2):
                act.sem_inc(h_out[u], 16)
                act.sem_inc(t_out[u], 16)
            act.wait_ge(loaded, n_loaded[0])
            act.activation(a_neg[:, :], a_neg[:, :], ACT.Exp).then_inc(T["aneg"], 1)
            act.wait_ge(T["init"], 1)
            with act.Fori(0, TILES // 2) as pair:
                t0 = pair * 2
                for u in range(2):
                    tile = t0 + u
                    act_front(act, tile, u, P, 16 * t0 + 64)
                    now(act, "cum", tile)
                    last(act, "yf std xde", tile)
                    act.activation(ecum[:, :, :], cum[:, :, :], ACT.Exp).then_inc(S["ecd"], 1)
                    now(act, "projz", tile)
                    act.activation(zs[:, :], bank[2][:, :], ACT.Silu).then_inc(S["z"], 1)
                    now(act, "projc", tile)
                    last(act, "convd", tile)
                    for c in range(2):
                        ins = act.activation(raw[:, 4 * c:4 * c + 4, CK - 1:], bank[3 + c][:, :].rearrange("p (c n) -> p c n", c=4), ACT.Copy)
                    ins.then_inc(S["rawc"], 1)
                    now(act, "convd", tile)
                    last(act, "ydm", tile)
                    act.activation(xc[:, :, :], cv[:, :, :], ACT.Silu).then_inc(S["xcs"], 1)
                    now(act, "xtm", tile)
                    last(act, "stm yf xd xdt", tile)
                    act.activation(xtok[:, :, :].rearrange("p a b -> p (a b)"), bank[3][:, :], ACT.Copy)
                    act.activation(btok[:, :, :].rearrange("p a b -> p (a b)"), bank[4][:, 0:2 * P], ACT.Copy).then_inc(S["xtk"], 1)
                    now(act, "smax", tile)
                    for hh in range(NH):
                        act.activation(s[:, hh, :], s[:, hh, :], ACT.Exp, bias=top[:, 1, hh:hh + 1], accum_out=top[:, 2, hh:hh + 1])
                    act.activation(top[:, 3, :], top[:, 3, :], ACT.Exp).then_inc(S["pexp"], 1)
                    now(act, "rmin", tile)
                    act.activation(m[:, :, :], m[:, :, :], ACT.Exp).then_inc(S["rexpd"], 1)
                    now(act, "ptm", tile)
                    last(act, "pv", tile)
                    act.activation(pT[:, 0, 0].rearrange("p a b -> p (a b)"), bank[0][:, :], ACT.Copy)
                    act.activation(pT[:, 0, 1].rearrange("p a b -> p (a b)"), bank[1][:, :], ACT.Copy).then_inc(S["pta"], 1)
                    now(act, "pv", tile)
                    last(act, "wom", tile)
                    act.activation(aT[:, :, :].rearrange("p a b -> p (a b)"), bank[4][:, :], ACT.Copy).then_inc(S["at"], 1)
                    now(act, "yf", tile)
                    last(act, "ys", tile)
                    for g in range(SG):
                        ins = act.activation(junk[:, 256 * g:256 * g + 256], y[:, 4 * g:4 * g + 4, :].rearrange("p a b -> p (a b)"),
                                             ACT.Square, scale=256 ** -0.5, accum_out=stat[:, 11 + g:12 + g])
                    ins.then_inc(S["ysq"], 1)
                    act_tail(act, tile, u, P, bass.ds(t0 * P + u * P, P))
            act.wait_ge(kv_out, 32)
            act_front(act, TILES, 0, DEC, 8 * TILES * 2 + 64)
            now(act, "projz", TILES)
            act.activation(zs[0:DEC, :], bank[2][0:DEC, :], ACT.Silu).then_inc(S["z"], 1)
            now(act, "projc", TILES)
            for c in range(2):
                ins = act.activation(st_raw[:, 512 * c:512 * c + 512], bank[3 + c][0:DEC, :], ACT.Copy)
            ins.then_inc(S["rawc"], 1)
            act.wait_ge(T["dt1"], 1)
            act.activation(dt[0:DEC, 4, :], dt[0:DEC, 4, :], ACT.Exp).then_inc(T["dt2"], 1)
            act.wait_ge(T["cv1"], 1)
            act.activation(st_xc, st_acc, ACT.Silu).then_inc(T["cv2"], 1)
            act.wait_ge(T["sx"], 1)
            act.activation(ps, ps, ACT.Exp)
            act.activation(m_top[:, 3, :], m_top[:, 3, :], ACT.Exp).then_inc(T["sp"], 1)
            act_tail(act, TILES, 0, DEC, slice(SEQ, TOKENS))

            for u in range(2):
                act.sem_inc(e_out[u], 16)
            act.sem_inc(E_["sil"], 2)
            act.sem_inc(E_["ya"], 2)
            act.sem_inc(E_["xTe"], 2)
            act.wait_ge(outs, N_OUTS)
            with act.Fori(0, SLOT_TILES // 2) as pair:
                j0 = pair * 2
                for u in range(2):
                    j = j0 + u
                    act.wait_ge(E_["xT"], j + 3)
                    act.activation(xgT[u][:, 0:4, :].rearrange("p a b -> p (a b)"), bank[0 + 2 * u][:, :], ACT.Copy)
                    act.activation(xgT[u][:, 4:8, :].rearrange("p a b -> p (a b)"), bank[1 + 2 * u][:, :], ACT.Copy).then_inc(E_["xTe"], 1)
                    act.wait_ge(E_["gu"], j + 1)
                    act.wait_ge(E_["hid"], j + 1)
                    act.activation(sil[u], bank[4][:, 0:P], ACT.Silu).then_inc(E_["sil"], 1)
                    act.wait_ge(E_["dn"], j + 3)
                    act.wait_ge(e_out[u], 8 * j0 + 16)
                    act.activation(yo[u][:, 0:512], bank[6][:, :], ACT.Copy).then_inc(E_["ya"], 1)
                    act.wait_ge(E_["ya"], j + 3)
                    act.wait_ge(E_["yd"], j + 3)
                    act.dma_start(y_dram[bass.ds(j0 * P + u * P, P), :], yo[u]).then_inc(e_out[u], 16)
            for c in range(TILES + 1):
                n, u = (P, c % 2) if c < TILES else (DEC, c % 2)
                act.wait_ge(c_done, c + 1)
                dst = O["y_prompt"][0, c * P:(c + 1) * P, :] if c < TILES else O["y_sample"].rearrange("b s d -> (b s) d")
                act.dma_start(dst, c_h[u][0:n, :]).then_inc(c_out[u], 16)

        def dve_front(dve, tile, u, n, x_need):
            now(dve, "xm", tile)
            last(dve, "lgm", tile)
            for c, b in enumerate((5, 6)):
                ins = dve.tensor_tensor(xT[:, 4 * c:4 * c + 4, 0:n], bank[b][:, 0:4 * n].rearrange("p (k n) -> p k n", k=4),
                                        norm1[:, 4 * c:4 * c + 4].unsqueeze(2).to_broadcast([P, 4, n]), ALU.mult)
            ins.then_inc(S["xT"], 1)
            now(dve, "qkv", tile)
            dve.tensor_tensor(dt[0:n, 0, :], dt[0:n, 0, :], dt_bias[0:n, :], ALU.add)
            dve.drain()
            dve.tensor_scalar(dt[0:n, 1, :], dt[0:n, 0, :], -1.0, None, ALU.mult)
            dve.drain()
            dve.tensor_tensor(dt[0:n, 1, :], dt[0:n, 0, :], dt[0:n, 1, :], ALU.max).then_inc(S["dtp"], 1)
            last(dve, "ptm qs", tile)
            sq = flat_s[0:n, 0:640].rearrange("p (a b) -> p a b", a=10)
            dve.scalar_tensor_tensor(out=sq, in0=qk[0:n, :, :], scalar=1.0 / HD, in1=qk[0:n, :, :], op0=ALU.mult, op1=ALU.mult)
            dve.drain()
            dve.tensor_reduce(stat[0:n, 1:11], sq, AX.X, ALU.add).then_inc(S["qsq"], 1)
            now(dve, "dl", tile)
            last(dve, "rmm xdt", tile)
            dve.tensor_scalar(dt[0:n, 0, :], dt[0:n, 0, :], 0.0, None, ALU.max)
            dve.drain()
            dve.tensor_tensor(dt[0:n, 3, :], dt[0:n, 0, :], dt[0:n, 2, :], ALU.add)
            dve.drain()
            dve.tensor_tensor(dt[0:n, 4, :], dt[0:n, 3, :], a_neg[0:n, :], ALU.mult).then_inc(S["dta"], 1)
            now(dve, "qs", tile)
            last(dve, "qkt", tile)
            dve.wait_ge(x_in[u], x_need)
            w = flat_s[0:n, 1280:1920].rearrange("p (a b) -> p a b", a=10)
            dve.tensor_tensor(w, qk[0:n, :, :], rstd[0:n, 1:11].unsqueeze(2).to_broadcast([n, 10, HD]), ALU.mult)
            dve.drain()
            dve.tensor_tensor(w[:, 0:8, :], w[:, 0:8, :], qk_norm[0:n, 0:1, :].to_broadcast([n, 8, HD]), ALU.mult)
            dve.tensor_tensor(w[:, 8:10, :], w[:, 8:10, :], qk_norm[0:n, 1:2, :].to_broadcast([n, 2, HD]), ALU.mult)
            dve.drain()
            H2 = HD // 2
            tmp = [flat_s[0:n, 320 * a:320 * a + 320].rearrange("p (a b) -> p a b", a=10) for a in range(4)]
            cos = rope[u][0:n, 0:H2].unsqueeze(1).to_broadcast([n, 10, H2])
            sin = rope[u][0:n, H2:HD].unsqueeze(1).to_broadcast([n, 10, H2])
            dve.tensor_tensor(tmp[0], w[:, :, 0:H2], cos, ALU.mult)
            dve.tensor_tensor(tmp[1], w[:, :, H2:HD], sin, ALU.mult)
            dve.tensor_tensor(tmp[2], w[:, :, H2:HD], cos, ALU.mult)
            dve.tensor_tensor(tmp[3], w[:, :, 0:H2], sin, ALU.mult)
            dve.drain()
            q_out = qkr[0:n, 0:8, :].rearrange("p (r k) d -> p k r d", k=NKV)
            for half, (a, b, op) in enumerate(((0, 1, ALU.subtract), (2, 3, ALU.add))):
                at = slice(half * H2, half * H2 + H2)
                for kv in range(NKV):
                    hs_ = slice(kv * REP, kv * REP + REP)
                    dve.tensor_tensor(q_out[:, kv, :, at], tmp[a][:, hs_, :], tmp[b][:, hs_, :], op)
                ins = dve.tensor_tensor(qkr[0:n, 8:10, at], tmp[a][:, 8:10, :], tmp[b][:, 8:10, :], op)
            ins.then_inc(S["qkr"], 1)

        def dve_tail(dve, tile, u, n, t_free, slot):
            now(dve, "wom", tile)
            for c in range(2):
                ins = dve.tensor_tensor(x[u][0:n, 512 * c:512 * c + 512], x[u][0:n, 512 * c:512 * c + 512], bank[2 + c][0:n, :], ALU.add)
            ins.then_inc(S["hres"], 1)
            now(dve, "hs", tile)
            last(dve, "ttm", tile)
            dve.wait_ge(*t_free)
            dve.scalar_tensor_tensor(out=t[0:n, :], in0=x[u][0:n, :], scalar=rstd[0:n, 13:14], in1=norm2[0:n, :],
                                     op0=ALU.mult, op1=ALU.mult).then_inc(S["td"], 1)
            now(dve, "lgm", tile)
            last(dve, "gex", tile)
            dve.tensor_tensor(lg[0:n, 0:NG], bank[7][0:n, 0:NG], b_route[0:n, 0:NG], ALU.add)
            dve.tensor_tensor(lg[0:n, 8:8 + NE], bank[7][0:n, NG:NG + NE], b_route[0:n, NG:NG + NE], ALU.add)
            dve.drain()
            dve.max(g8[0:n, :], lg[0:n, 0:8])
            dve.drain()
            dve.max_index(gi[0:n, :], g8[0:n, :], lg[0:n, 0:8])
            dve.tensor_scalar(rt[0:n, 0:1], g8[0:n, 0:1], -1.0, None, ALU.mult)
            dve.drain()
            dve.tensor_copy(fi[0:n, 0:1], gi[0:n, 0:1])
            dve.drain()
            dve.tensor_scalar(gmask[0:n, 0, :], con[0:n, C_IOTA:C_IOTA + NG], fi[0:n, 0:1], None, ALU.is_equal)
            dve.drain()
            dve.tensor_scalar(gmask[0:n, 1, :], gmask[0:n, 0, :], 1.0, BIG, ALU.subtract, ALU.mult)
            dve.tensor_tensor(le[0:n, :, :], lg[0:n, 8:8 + NE].rearrange("p (g e) -> p g e", g=NG),
                              gmask[0:n, 0, :].unsqueeze(2).to_broadcast([n, NG, EPG]), ALU.mult)
            dve.drain()
            dve.tensor_tensor(le[0:n, :, :], le[0:n, :, :], gmask[0:n, 1, :].unsqueeze(2).to_broadcast([n, NG, EPG]), ALU.add)
            dve.drain()
            fl = le[0:n, :, :].rearrange("p g e -> p (g e)")
            dve.max(e8[0:n, :], fl)
            dve.drain()
            dve.max_index(ei[0:n, :], e8[0:n, :], fl)
            dve.tensor_scalar(rt[0:n, 2:3], e8[0:n, 0:1], -1.0, None, ALU.mult).then_inc(S["sel"], 1)
            dve.drain()
            dve.tensor_copy(fi[0:n, 2:4], ei[0:n, 0:2])
            dve.drain()
            for k in range(2):
                dve.tensor_scalar(slot("onehot", n)[:, k], con[0:n, C_IOTA:C_IOTA + NE], fi[0:n, 2 + k:3 + k], None, ALU.is_equal)
            dve.drain()
            last(dve, "rankm", tile)
            dve.tensor_tensor(both[0:n, :], slot("onehot", n)[:, 0], slot("onehot", n)[:, 1], ALU.add).then_inc(S["rsel"], 1)
            now(dve, "gex", tile)
            dve.tensor_scalar(rt[0:n, 4:5], rt[0:n, 3:4], 1.0, None, ALU.add)
            dve.drain()
            dve.tensor_tensor(rt[0:n, 4:5], rt[0:n, 4:5], rt[0:n, 1:2], ALU.mult)
            dve.drain()
            dve.reciprocal(slot("gate", n)[:, 0:1], rt[0:n, 4:5])
            dve.drain()
            dve.tensor_tensor(slot("gate", n)[:, 1:2], slot("gate", n)[:, 0:1], rt[0:n, 3:4], ALU.mult)
            now(dve, "rankm", tile)
            dve.tensor_copy(rankc[0:n, :], bank[7][0:n, 0:NE])
            dve.tensor_tensor(counted[0:n, :], counted[0:n, :], both[0:n, :], ALU.add)
            dve.drain()
            dve.tensor_tensor(rprod[0:n, :, :], slot("onehot", n), rankc[0:n, :].unsqueeze(1).to_broadcast([n, 2, NE]), ALU.mult)
            dve.drain()
            dve.tensor_reduce(slot("rank", n), rprod[0:n, :, :], AX.X, ALU.add).then_inc(S["rankd"], 1)

        @block.vector
        def _(dve):
            credit(dve, "xT dtp qsq dta cum qkr qkc se smax prob ptb convd xdt rmin cbm md yf std yg gt hres td sel rsel rankd")
            dve.memset(v[:, :, :], 0.0)
            dve.memset(kT[:, :, :], 0.0)
            dve.memset(raw[:, :, 0:CK - 1], 0.0)
            dve.memset(hT[:, :, :], 0.0)
            dve.memset(counted[:, :], 0.0)
            dve.memset(onehot[:, TILES], 0.0)
            dve.memset(rank[:, TILES], 0.0)
            dve.memset(q_blk[:, :, :, :], 0.0)
            dve.memset(mask[:, 0, :], -BIG)
            dve.memset(lg[:, :], -BIG)
            dve.drain().then_inc(T["init"], 1)
            dve.wait_ge(loaded, n_loaded[0])
            dve.wait_ge(T["aneg"], 1)
            dve.tensor_scalar(a_neg[:, :], a_neg[:, :], -1.0, None, ALU.mult)
            dve.tensor_copy(mask[:, 1, :], con[:, C_BAND + P:C_BAND + 2 * P])
            dve.drain()
            with dve.Fori(0, TILES // 2) as pair:
                t0 = pair * 2
                for u in range(2):
                    tile = t0 + u
                    dve_front(dve, tile, u, P, 16 * t0 + 64)
                    now(dve, "cumm", tile)
                    last(dve, "ecd", tile)
                    dve.tensor_copy(cum[:, 0, :], bank[7][:, 0:SH])
                    dve.tensor_copy(cum[:, 2, :], bank[7][:, SH:2 * SH])
                    dve.drain()
                    dve.tensor_tensor(cum[:, 1, :], cum[:, 2, :], cum[:, 0, :], ALU.subtract).then_inc(S["cum"], 1)
                    now(dve, "qkt", tile)
                    last(dve, "sc3", tile)
                    dve.tensor_copy(kT[:, 0, :], kT[:, 1, :])
                    dve.drain()
                    dve.tensor_copy(kT[:, 1, :], bank[7][:, 0:P])
                    dve.tensor_copy(qT[:, :, :].rearrange("p a b -> p (a b)"), bank[2][:, :]).then_inc(S["qkc"], 1)
                    now(dve, "rawc", tile)
                    last(dve, "xcs", tile)
                    for c in range(CC):
                        dve.tensor_scalar(cv[:, c, :], raw[:, c, 0:P], conv_w[:, c, 0:1], conv_b[:, c:c + 1], ALU.mult, ALU.add)
                    for k in range(1, CK):
                        dve.drain()
                        for c in range(CC):
                            dve.scalar_tensor_tensor(out=cv[:, c, :], in0=raw[:, c, k:k + P], scalar=conv_w[:, c, k:k + 1],
                                                     in1=cv[:, c, :], op0=ALU.mult, op1=ALU.add)
                    dve.drain()
                    dve.tensor_copy(raw[:, :, 0:CK - 1], raw[:, :, P:P + CK - 1]).then_inc(S["convd"], 1)
                    for i, b in enumerate((5, 6, 0, 1)):
                        now(dve, f"sc{i}", tile)
                        ins = dve.scalar_tensor_tensor(
                            out=s[:, 2 * i:2 * i + 2, :], in0=bank[b][:, :].rearrange("p (a b) -> p a b", a=2), scalar=SCALE,
                            in1=mask[:, :, :].rearrange("p a b -> p (a b)").unsqueeze(1).to_broadcast([P, 2, 2 * P]),
                            op0=ALU.mult, op1=ALU.add)
                    ins.then_inc(S["se"], 1)
                    dve.drain()
                    dve.tensor_copy(mask[:, 0, :], con[:, C_BAND:C_BAND + P])
                    dve.tensor_reduce(top[:, 0, :], s[:, :, :], AX.X, ALU.max)
                    dve.drain()
                    dve.tensor_tensor(top[:, 0, :], top[:, 0, :], sink[:, :], ALU.max)
                    dve.drain()
                    dve.tensor_scalar(top[:, 1, :], top[:, 0, :], -1.0, None, ALU.mult)
                    dve.tensor_tensor(top[:, 3, :], sink[:, :], top[:, 0, :], ALU.subtract).then_inc(S["smax"], 1)
                    now(dve, "rmm", tile)
                    last(dve, "ydm", tile)
                    for hh in range(SH):
                        ins = dve.tensor_scalar(m[:, hh, :], bank[5 + hh // 4][:, (hh % 4) * P:(hh % 4 + 1) * P],
                                                cum[:, 0, hh:hh + 1], 0.0, ALU.subtract, ALU.min)
                    ins.then_inc(S["rmin"], 1)
                    now(dve, "cbt", tile)
                    dve.tensor_tensor(cbm[:, :, :], bank[7][:, 0:2 * P].rearrange("p (g l) -> p g l", g=SG),
                                      tri.unsqueeze(1).to_broadcast([P, SG, P]), ALU.mult).then_inc(S["cbm"], 1)
                    now(dve, "xtk", tile)
                    last(dve, "xde", tile)
                    dve.tensor_tensor(xdt[:, :, :], xtok[:, :, :], dt[:, 3, :].unsqueeze(2).to_broadcast([P, SH, SP_]), ALU.mult).then_inc(S["xdt"], 1)
                    now(dve, "pexp", tile)
                    dve.tensor_tensor(top[:, 2, :], top[:, 2, :], top[:, 3, :], ALU.add)
                    dve.drain()
                    dve.reciprocal(top[:, 2, :], top[:, 2, :])
                    dve.drain()
                    for hh in range(NH):
                        ins = dve.tensor_scalar(s[:, hh, :], s[:, hh, :], top[:, 2, hh:hh + 1], None, ALU.mult)
                    ins.then_inc(S["prob"], 1)
                    now(dve, "rexpd", tile)
                    for g in range(SG):
                        ins = dve.tensor_tensor(m[:, 4 * g:4 * g + 4, :], m[:, 4 * g:4 * g + 4, :],
                                                cbm[:, g:g + 1, :].to_broadcast([P, 4, P]), ALU.mult)
                    ins.then_inc(S["md"], 1)
                    now(dve, "ptm", tile)
                    last(dve, "pv", tile)
                    dve.tensor_copy(pT[:, 1, 0].rearrange("p a b -> p (a b)"), bank[2][:, :])
                    dve.tensor_copy(pT[:, 1, 1].rearrange("p a b -> p (a b)"), bank[3][:, :]).then_inc(S["ptb"], 1)
                    now(dve, "ydm ecd xd z", tile)
                    fy = y[:, :, :].rearrange("p a b -> p (a b)")
                    dve.tensor_tensor(y[:, :, :], bank[6][:, :].rearrange("p (a b) -> p a b", a=SH),
                                      ecum[:, 0, :].unsqueeze(2).to_broadcast([P, SH, SP_]), ALU.mult)
                    dve.drain()
                    dve.tensor_tensor(fy, fy, bank[5][:, :], ALU.add)
                    dve.drain()
                    dve.tensor_tensor(y[:, :, :], y[:, :, :], xd[:, :, :], ALU.add)
                    dve.drain()
                    dve.tensor_tensor(fy, fy, zs[:, :], ALU.mult).then_inc(S["yf"], 1)
                    dve.tensor_tensor(hT[:, :, :], hT[:, :, :], ecum[:, 2, :].unsqueeze(2).to_broadcast([P, SH, SP_]), ALU.mult)
                    dve.drain()
                    now(dve, "stm", tile)
                    dve.tensor_tensor(hT[:, :, :].rearrange("p a b -> p (a b)"), hT[:, :, :].rearrange("p a b -> p (a b)"),
                                      bank[0][:, :], ALU.add).then_inc(S["std"], 1)
                    now(dve, "ys", tile)
                    for g in range(SG):
                        ins = dve.tensor_scalar(y[:, 4 * g:4 * g + 4, :], y[:, 4 * g:4 * g + 4, :], rstd[:, 11 + g:12 + g], None, ALU.mult)
                    ins.then_inc(S["yg"], 1)
                    now(dve, "ytm", tile)
                    last(dve, "wom", tile)
                    dve.tensor_tensor(gT[:, :, :], bank[1][:, :].rearrange("p (c n) -> p c n", c=4),
                                      ssm_norm[:, :].unsqueeze(2).to_broadcast([P, 4, P]), ALU.mult).then_inc(S["gt"], 1)

                    def slot(name, n, t0=t0, u=u):
                        return {"onehot": onehot, "rank": rank, "gate": gate}[name][0:n, bass.ds(t0 + u, 1)].squeeze(1)
                    dve_tail(dve, tile, u, P, (t_out[1 - u], 8 * t0 + (16, 32)[u]), slot)

            dve.wait_ge(kv_out, 32)
            dve_front(dve, TILES, 0, DEC, 8 * TILES * 2 + 64)
            dve.drain()
            dve.tensor_copy(dt[0:DEC, 1, :], dt[0:DEC, 3, :]).then_inc(T["dt1"], 1)
            dve.wait_ge(T["q1"], 1)
            for b in range(DEC):
                for kv in range(NKV):
                    r = slice(kv * HD, kv * HD + HD)
                    ins = dve.tensor_copy(q_blk[r, b, kv, :], bank[7][r, 0:REP * DEC].rearrange("p (r b) -> p r b", b=DEC)[:, :, b])
            ins.then_inc(T["q2"], 1)
            dve.wait_ge(T["kT0"], 1)
            for c in range(2):
                ins = dve.tensor_copy(keysT[:, 4 * c:4 * c + 4, :].rearrange("p a b -> p (a b)"), bank[5 + c][:, :])
            ins.then_inc(T["kT1"], 1)
            dve.wait_ge(state_in, 16 * 11)
            now(dve, "rawc", TILES)
            dve.tensor_tensor(st_acc, st_raw, st_w[:, CK - 1, :], ALU.mult)
            dve.drain()
            dve.tensor_tensor(st_acc, st_acc, st_b, ALU.add)
            for k in range(CK - 1):
                dve.tensor_tensor(st_tmp, st_conv[:, k, :], st_w[:, k, :], ALU.mult)
                dve.drain()
                dve.tensor_tensor(st_acc, st_acc, st_tmp, ALU.add)
                dve.drain()
            dve.drain().then_inc(T["cv1"], 1)
            dve.wait_ge(T["sc1"], 1)
            for c in range(2):
                dve.tensor_scalar(ps[:, 4 * c:4 * c + 4, :].rearrange("p a b -> p (a b)"), bank[c][0:NH, :], SCALE, None, ALU.mult)
            dve.drain()
            dve.tensor_reduce(m_top[:, 0, :], ps, AX.X, ALU.max)
            dve.drain()
            dve.tensor_scalar(m_top[:, 0, :], m_top[:, 0, :], sink_col[:, 0:1], None, ALU.max)
            dve.drain()
            dve.tensor_tensor(ps, ps, m_top[:, 0, :].unsqueeze(2).to_broadcast([NH, DEC, P]), ALU.subtract)
            dve.tensor_scalar(m_top[:, 3, :], m_top[:, 0, :], -1.0, sink_col[:, 0:1], ALU.mult, ALU.add)
            dve.drain().then_inc(T["sx"], 1)
            dve.wait_ge(T["sp"], 1)
            dve.tensor_reduce(m_top[:, 2, :], ps, AX.X, ALU.add)
            dve.drain()
            dve.tensor_tensor(m_top[:, 2, :], m_top[:, 2, :], m_top[:, 3, :], ALU.add)
            dve.drain()
            dve.reciprocal(m_top[:, 2, :], m_top[:, 2, :])
            dve.drain()
            dve.tensor_tensor(ps, ps, m_top[:, 2, :].unsqueeze(2).to_broadcast([NH, DEC, P]), ALU.mult)
            dve.drain().then_inc(T["sc2"], 1)
            dve.wait_ge(T["ptm"], 1)
            dve.tensor_copy(ps_T[:, :, :].rearrange("p b h -> p (b h)"), bank[2][:, 0:DEC * NH]).then_inc(T["pT"], 1)
            dve.wait_ge(T["pv"], 1)
            for kv in range(NKV):
                r = slice(kv * HD, kv * HD + HD)
                ins = dve.tensor_copy(aT[r, :, 0:DEC], bank[3][r, 0:DEC * NH].rearrange("p (b k r) -> p k r b", b=DEC, k=NKV)[:, kv])
            ins.then_inc(T["aT"], 1)
            dve.wait_ge(T["dt3"], 1)
            dve.tensor_copy(st_da[:, 0:2 * DEC], bank[6][0:SH, 0:2 * DEC])
            dve.tensor_copy(st_da[:, 2 * DEC:], d_col[:, :])
            dve.tensor_copy(head_sel.rearrange("p (h d) -> p h d", h=SH), ident[0:SH, 0:SH].unsqueeze(2).to_broadcast([SH, SH, SP_]))
            dve.drain().then_inc(T["xz1"], 1)
            dve.wait_ge(T["xz2"], 1)
            dve.tensor_copy(st_sc[:, :, :], bank[7][:, 0:4 * (2 * DEC + 1)].rearrange("p (c n) -> p c n", c=4))
            dve.tensor_copy(st_xT[:, :, :], bank[4][:, 0:4 * DEC].rearrange("p (c n) -> p c n", c=4))
            dve.tensor_copy(st_zT[:, :, :], bank[4][:, 4 * DEC:8 * DEC].rearrange("p (c n) -> p c n", c=4))
            dve.drain()
            dve.tensor_tensor(st_dx[:, :, :], st_xT[:, :, :], st_sc[:, :, 0:DEC], ALU.mult)
            dve.drain()
            dve.wait_ge(T["ssmT"], 1)
            dve.tensor_copy(flat_cv[:, 0:512], bank[5][:, :]).then_inc(T["ssmC"], 1)
            dve.wait_ge(outs, N_SSM)
            for b in range(DEC):
                dve.wait_ge(T["bc"], b + 1)
                bc = bank[b % 2][:, :].rearrange("p (w g n) -> p w g n", w=2, g=SG)
                for g in range(SG):
                    dve.tensor_tensor(st_bx[:, 2 * g:2 * g + 2, :], bc[:, 0, g:g + 1, :].to_broadcast([P, 2, P]),
                                      st_dx[:, 2 * g:2 * g + 2, b:b + 1].to_broadcast([P, 2, P]), ALU.mult)
                dve.tensor_tensor(st_h[:, b], st_h[:, b], st_sc[:, :, DEC + b:DEC + b + 1].to_broadcast([P, 4, P]), ALU.mult)
                dve.drain()
                dve.tensor_tensor(st_h[:, b], st_h[:, b], st_bx, ALU.add)
                dve.drain()
                for g in range(SG):
                    dve.tensor_tensor(st_ch[:, 2 * g:2 * g + 2, :], st_h[:, b, 2 * g:2 * g + 2, :],
                                      bc[:, 1, g:g + 1, :].to_broadcast([P, 2, P]), ALU.mult)
                dve.drain()
                dve.tensor_reduce(st_y[:, :, b], st_ch, AX.X, ALU.add)
                dve.drain().then_inc(T["hst"], 1)
            dve.tensor_tensor(st_g2[:, :, :], st_xT[:, :, :], st_sc[:, :, 2 * DEC:].to_broadcast([P, 4, DEC]), ALU.mult)
            dve.drain()
            dve.tensor_tensor(st_y[:, :, :], st_y[:, :, :], st_g2[:, :, :], ALU.add)
            dve.drain()
            dve.tensor_tensor(st_y[:, :, :], st_y[:, :, :], st_zT[:, :, :], ALU.mult)
            dve.drain()
            dve.tensor_tensor(st_g2[:, :, :], st_y[:, :, :], st_y[:, :, :], ALU.mult)
            dve.drain().then_inc(T["sq"], 1)
            dve.wait_ge(T["nrm"], 1)
            dve.tensor_copy(st_g2[:, :, :].rearrange("p a b -> p (a b)"), bank[6][:, 0:4 * DEC])
            dve.drain()
            for g in range(SG):
                ins = dve.tensor_tensor(st_n[:, g, :], st_g2[:, 2 * g, :], st_g2[:, 2 * g + 1, :], ALU.add)
            ins.then_inc(T["nr"], 1)
            dve.wait_ge(T["rs"], 1)
            for g in range(SG):
                dve.tensor_tensor(st_y[:, 2 * g:2 * g + 2, :], st_y[:, 2 * g:2 * g + 2, :], st_r[:, g:g + 1, :].to_broadcast([P, 2, DEC]), ALU.mult)
            dve.drain()
            dve.tensor_tensor(gT[:, :, 0:DEC], st_y[:, :, :], ssm_norm[:, :].unsqueeze(2).to_broadcast([P, 4, DEC]), ALU.mult).then_inc(T["gT"], 1)
            dve_tail(dve, TILES, 0, DEC, (t_out[1], 8 * TILES + 16),
                     lambda name, n: {"onehot": onehot, "rank": rank, "gate": gate}[name][0:n, TILES])

            dve.drain().then_inc(T["cnt"], 1)
            dve.wait_ge(T["cnt"], 2)
            dve.tensor_copy(nt[:, 0, :], bank[0][:, 0:NE])
            dve.drain()
            dve.tensor_scalar(nt[:, 1, :], nt[:, 0, :], 0.0, None, ALU.is_gt)
            dve.drain()
            for j in range(1, (TOKENS + P - 1) // P):
                dve.scalar_tensor_tensor(out=nt[:, 1, :], in0=nt[:, 0, :], scalar=float(P * j), in1=nt[:, 1, :], op0=ALU.is_gt, op1=ALU.add)
                dve.drain()
            dve.tensor_tensor_scan(nt[:, 2, :], con[:, C_ONES:C_ONES + NE], nt[:, 1, :], 0.0, ALU.mult, ALU.add)
            dve.drain()
            dve.tensor_tensor(nt[:, 3, :], nt[:, 2, :], nt[:, 1, :], ALU.subtract)
            dve.tensor_tensor(ecmp, nt[0:1, 2:3, :].to_broadcast([1, SLOT_TILES, NE]),
                              con[0:1, C_TILE:C_TILE + SLOT_TILES].unsqueeze(2).to_broadcast([1, SLOT_TILES, NE]), ALU.is_le)
            dve.drain()
            dve.tensor_reduce(etile[:, :], ecmp, AX.X, ALU.add)
            dve.drain()
            dve.tensor_scalar(etile[:, :], etile[:, :], float(NE - 1), None, ALU.min)
            dve.drain()
            dve.tensor_copy(etile_i[:, :], etile[:, :]).then_inc(T["et"], 1)
            rk = rank[:, :, :].rearrange("p a b -> p (a b)")
            dve.tensor_scalar(quo[:, 0, :], rk, float(P), None, ALU.is_ge)
            dve.drain()
            for j in range(2, (TOKENS + P - 1) // P):
                dve.scalar_tensor_tensor(out=quo[:, 0, :], in0=rk, scalar=float(P * j), in1=quo[:, 0, :], op0=ALU.is_ge, op1=ALU.add)
                dve.drain()
            dve.scalar_tensor_tensor(out=quo[:, 1, :], in0=quo[:, 0, :], scalar=-float(P), in1=rk, op0=ALU.mult, op1=ALU.add)
            dve.tensor_tensor(pair_prod, onehot[:, :, :, :].rearrange("p a b e -> p (a b) e"), nt[:, 3:4, :].to_broadcast([P, PAIRS, NE]), ALU.mult)
            dve.drain()
            dve.tensor_reduce(quo[:, 3, :], pair_prod, AX.X, ALU.add)
            dve.drain()
            dve.tensor_tensor(quo[:, 2, :], quo[:, 3, :], quo[:, 0, :], ALU.add)
            dve.drain()
            dve.scalar_tensor_tensor(out=addr[:, 0, :], in0=quo[:, 1, :], scalar=float(SLOT_TILES), in1=quo[:, 2, :], op0=ALU.mult, op1=ALU.add)
            dve.scalar_tensor_tensor(out=addr[:, 1, :], in0=quo[:, 2, :], scalar=float(P), in1=quo[:, 1, :], op0=ALU.mult, op1=ALU.add)
            dve.drain().then_inc(T["slots"], 1)

            dve.sem_inc(E_["hid"], 1)
            dve.sem_inc(E_["hTe"], 1)
            dve.sem_inc(E_["yd"], 2)
            dve.wait_ge(outs, N_OUTS)

            def expert_hidden(j, u):
                dve.wait_ge(E_["sil"], j + 3)
                dve.tensor_tensor(hid[u], sil[u], bank[4][:, P:2 * P], ALU.mult).then_inc(E_["hid"], 1)
                dve.wait_ge(E_["hT"], j + 1)
                dve.tensor_copy(hidT[u], bank[5][:, 0:P]).then_inc(E_["hTe"], 1)

            with dve.Fori(0, SLOT_TILES // 2) as pair:
                j0 = pair * 2
                for u in range(2):
                    j = j0 + u
                    expert_hidden(j, u)
                    dve.wait_ge(E_["dn"], j + 3)
                    dve.wait_ge(e_out[u], 8 * j0 + 16)
                    dve.tensor_copy(yo[u][:, 512:D], bank[7][:, :]).then_inc(E_["yd"], 1)

            for c in range(TILES + 1):
                n, u = (P, c % 2) if c < TILES else (DEC, c % 2)
                dve.wait_ge(c_in[u], 16 * (c // 2 + 1))
                dve.wait_ge(c_in1[u], 32 * (c // 2 + 1))
                for k, yk in enumerate((c_y1[u], c_y2[u])):
                    ins = dve.scalar_tensor_tensor(out=c_h[u][0:n, :], in0=yk[0:n, :], scalar=gate[0:n, c, k:k + 1], in1=c_h[u][0:n, :],
                                                   op0=ALU.mult, op1=ALU.add)
                    if k == 0:
                        dve.drain()
                ins.then_inc(c_done, 1)

        def root_mean(pool, col, count, n, done):
            pool.tensor_tensor(stat[0:n, col:col + count], stat[0:n, col:col + count], eps[0:n, 0:count], ALU.add)
            pool.drain()
            pool.tensor_tensor(rstd[0:n, col:col + count], stat[0:n, col:col + count], neg_half[0:n, 0:count], ALU.pow).then_inc(S[done], 1)

        @block.gpsimd
        def _(pool):
            credit(pool, "xs qs xde xd ys hs")
            pool.memset(neg_half[:, :], -0.5)
            pool.memset(eps[:, :], EPS)
            pool.memset(zero_i[:, :], 0).then_inc(T["zero"], 1)
            pool.iota(tok[:, :], pattern=[[P, TILES + 1]], base=0, channel_multiplier=1).then_inc(T["zero"], 1)
            pool.wait_ge(T["zero"], 2)
            pool.dma_start(slot_dram.rearrange("(p j) a -> p (j a)", p=P), zero_i[:, :]).then_inc(zeroed, 16)
            with pool.Fori(0, TILES // 2) as pair:
                t0 = pair * 2
                for u in range(2):
                    tile = t0 + u
                    now(pool, "ssq", tile)
                    last(pool, "xn", tile)
                    root_mean(pool, 0, 1, P, "xs")
                    now(pool, "qsq", tile)
                    last(pool, "qkr", tile)
                    root_mean(pool, 1, 10, P, "qs")
                    now(pool, "xtk", tile)
                    last(pool, "yf", tile)
                    pool.tensor_tensor(xd[:, :, :], xtok[:, :, :], d_skip[:, :].unsqueeze(2).to_broadcast([P, SH, SP_]), ALU.mult).then_inc(S["xd"], 1)
                    now(pool, "xdt ecd", tile)
                    last(pool, "stm", tile)
                    pool.tensor_tensor(xde[:, :, :], xdt[:, :, :], ecum[:, 1, :].unsqueeze(2).to_broadcast([P, SH, SP_]), ALU.mult).then_inc(S["xde"], 1)
                    now(pool, "ysq", tile)
                    last(pool, "yg", tile)
                    root_mean(pool, 11, 2, P, "ys")
                    now(pool, "hsq", tile)
                    last(pool, "td", tile)
                    root_mean(pool, 13, 1, P, "hs")
                    if u == 1:
                        pass
            now(pool, "qkr", TILES - 1)
            pool.dma_start(O["win_k_prompt"].rearrange("a b s k d -> (a b s) (k d)"), qkr[:, 8:10, :].rearrange("p a b -> p (a b)")).then_inc(kv_out, 16)
            pool.dma_start(O["win_v_prompt"].rearrange("a b s k d -> (a b s) (k d)"), v[:, 1, :]).then_inc(kv_out, 16)
            now(pool, "ssq", TILES)
            root_mean(pool, 0, 1, DEC, "xs")
            now(pool, "qsq", TILES)
            root_mean(pool, 1, 10, DEC, "qs")
            pool.wait_ge(T["nr"], 1)
            pool.tensor_scalar(st_n[:, :, :], st_n[:, :, :], 1.0 / 256, EPS, ALU.mult, ALU.add)
            pool.drain()
            pool.tensor_tensor(st_r[:, :, :].rearrange("p a b -> p (a b)"), st_n[:, :, :].rearrange("p a b -> p (a b)"), neg_half[:, 0:SG * DEC], ALU.pow).then_inc(T["rs"], 1)
            now(pool, "hsq", TILES)
            root_mean(pool, 13, 1, DEC, "hs")

            pool.wait_ge(T["slots"], 1)
            pool.wait_ge(zeroed, 16)
            for c in range(TILES + 1):
                n = P if c < TILES else DEC
                for k in range(2):
                    i = 2 * c + k
                    pool.indirect_dma_start(slot_dram, bass.IndirectOffsetOnAxis(ap=addr[0:n, 0, i:i + 1].bitcast(U32), axis=0),
                                            tok[0:n, c:c + 1], None).then_inc(scattered, 16)
            pool.wait_ge(scattered, 16 * PAIRS)
            pool.dma_start(slot_tok[:, :], slot_dram.rearrange("(p j) a -> p (j a)", p=P)).then_inc(slots_in, 16)
            pool.wait_ge(slots_in, 16)
            for u in range(2):
                pool.wait_ge(t_out[u], 16 + 16 * ((TILES + 2 - u) // 2))
            pool.wait_ge(outs, N_OUTS)
            with pool.Fori(0, SLOT_TILES // 2) as pair:
                j0 = pair * 2
                for u in range(2):
                    pool.wait_ge(E_["xT"], j0 + u + 1)
                    pool.tensor_copy(tok_now[u][:, :], slot_tok[:, bass.ds(j0 + u, 1)]).then_inc(E_["tokc"], 1)
                    pool.wait_ge(t_out[0], 16 + 16 * (TILES // 2 + 1))
                    pool.wait_ge(E_["tokc"], j0 + u + 1)
                    pool.indirect_dma_start(xg[u], None, t_dram, bass.IndirectOffsetOnAxis(ap=tok_now[u][:, :].bitcast(U32), axis=0)).then_inc(e_x[u], 16)
            for u in range(2):
                pool.wait_ge(e_out[u], 16 + 16 * (SLOT_TILES // 2))
                pool.wait_ge(h_out[u], 16 + 16 * ((TILES + 2 - u) // 2))
            for c in range(TILES + 1):
                n, u = (P, c % 2) if c < TILES else (DEC, c % 2)
                if c >= 2:
                    pool.wait_ge(c_done, c - 1)
                for k, yk in enumerate((c_y1[u], c_y2[u])):
                    pool.indirect_dma_start(yk[0:n, :], None, y_dram,
                                            bass.IndirectOffsetOnAxis(ap=addr[0:n, 1, 2 * c + k:2 * c + k + 1].bitcast(U32), axis=0)).then_inc(c_in1[u], 16)

        def pe_turn_x(pe, src, ids, n, banks, done):
            for k in range(KC):
                cols = src.rearrange("t (p k) -> t k p", k=KC)[:, k, :]
                ins = pe.transpose(bank[banks[k // 4]][:, (k % 4) * n:(k % 4 + 1) * n], cols, ids)
            ins.then_inc(done, 1)

        def pe_front(pe, tile, n):
            ids = ident[0:n, 0:n]
            now(pe, "xn", tile)
            last(pe, "tt yf", tile)
            pe_turn_x(pe, xn[0:n, :], ids, n, (5, 6), S["xm"])
            now(pe, "xT", tile)
            last(pe, "std gt", tile)
            for out, cols in ((bank[0][0:n, :], slice(0, Q_END)), (bank[1][0:n, 0:256], slice(Q_END, V_END)),
                              (bank[1][0:n, 256:256 + SH], slice(XBC_END, IN_DIM))):
                for k in range(KC):
                    ins = pe.matmul(out, xT[:, k, 0:n], w_in[:, k, cols], start=k == 0, stop=k == KC - 1)
            ins.then_inc(S["projq"], 1)
            last(pe, "hres", tile)
            for k in range(KC):
                ins = pe.matmul(bank[2][0:n, :], xT[:, k, 0:n], w_in[:, k, V_END:Z_END], start=k == 0, stop=k == KC - 1)
            ins.then_inc(S["projz"], 1)

        def pe_tail(pe, tile, n):
            for c in range(2):
                for k in range(KC):
                    lhs = aT[:, k, 0:n] if k < REP else gT[:, k - REP, 0:n]
                    ins = pe.matmul(bank[2 + c][0:n, :], lhs, w_out[:, k, 512 * c:512 * c + 512], start=k == 0, stop=k == KC - 1)
            ins.then_inc(S["wom"], 1)
            now(pe, "td", tile)
            pe_turn_x(pe, t[0:n, :], ident[0:n, 0:n], n, (4, 5), S["ttm"])
            now(pe, "tt", tile)
            for k in range(KC):
                ins = pe.matmul(bank[7][0:n, 0:NG + NE], tT[:, k, 0:n], w_route[:, k, :], start=k == 0, stop=k == KC - 1)
            ins.then_inc(S["lgm"], 1)
            now(pe, "rsel", tile)
            pe.matmul(bank[7][0:n, 0:NE], strict[0:n, 0:n], both[0:n, :], start=True, stop=False)
            pe.matmul(bank[7][0:n, 0:NE], ones[:, 0:n], counted[:, :], start=False, stop=True).then_inc(S["rankm"], 1)

        @block.tensor
        def _(pe):
            credit(pe, "xm projq projz projc cumm qkt sc0 sc1 sc2 sc3 ptm pv xtm rmm cbt ydm stm ytm wom ttm lgm rankm")
            pe.wait_ge(loaded, n_loaded[0])
            pe.wait_ge(T["init"], 1)
            with pe.Fori(0, TILES // 2) as pair:
                t0 = pair * 2
                for u in range(2):
                    tile = t0 + u
                    pe_front(pe, tile, P)
                    for c in range(CC):
                        at = Z_END + c * P
                        for k in range(KC):
                            ins = pe.matmul(bank[3 + c // 4][:, (c % 4) * P:(c % 4 + 1) * P], w_in[:, k, at:at + P], xT[:, k, :],
                                            start=k == 0, stop=k == KC - 1)
                    ins.then_inc(S["projc"], 1)
                    now(pe, "dta", tile)
                    last(pe, "rankd", tile)
                    pe.matmul(bank[7][:, 0:SH], tri, dt[:, 4, :], start=True, stop=True)
                    pe.matmul(bank[7][:, SH:2 * SH], ones, dt[:, 4, :], start=True, stop=True).then_inc(S["cumm"], 1)
                    now(pe, "qkr z cum", tile)
                    for r in range(REP):
                        pe.transpose(bank[2][:, r * P:(r + 1) * P], qkr[:, 2 * r:2 * r + 2, :].rearrange("p a b -> p (a b)"), ident)
                    pe.transpose(bank[7][:, 0:P], qkr[:, 8:10, :].rearrange("p a b -> p (a b)"), ident).then_inc(S["qkt"], 1)
                    now(pe, "qkc qkv", tile)
                    for i, b in enumerate((5, 6, 0, 1)):
                        for j in range(2):
                            kv, r = (2 * i + j) // REP, (2 * i + j) % REP
                            rr = slice(kv * HD, kv * HD + HD)
                            ins = pe.matmul(bank[b][:, j * 256:(j + 1) * 256], qT[rr, r, :], kT[rr, :, :].rearrange("p a b -> p (a b)"),
                                            start=True, stop=True)
                        ins.then_inc(S[f"sc{i}"], 1)
                    now(pe, "xcs rawc", tile)
                    for c in range(6):
                        ins = pe.transpose(bank[3 + c // 4][:, (c % 4) * P:(c % 4 + 1) * P], xc[:, c, :], ident)
                    ins.then_inc(S["xtm"], 1)
                    now(pe, "se", tile)
                    for hh in range(SH):
                        ins = pe.matmul(bank[5 + hh // 4][:, (hh % 4) * P:(hh % 4 + 1) * P], dt[:, 4, hh:hh + 1].to_broadcast([P, P]), tri,
                                        start=True, stop=True)
                    ins.then_inc(S["rmm"], 1)
                    for g in range(SG):
                        ins = pe.matmul(bank[7][:, g * P:(g + 1) * P], xc[:, 4 + g, :], xc[:, 6 + g, :], start=True, stop=True)
                    ins.then_inc(S["cbt"], 1)
                    now(pe, "prob xtk", tile)
                    for kv in range(NKV):
                        for blk in range(2):
                            for r in range(REP):
                                ins = pe.transpose(bank[kv * 2 + blk][:, r * P:(r + 1) * P], s[:, kv * REP + r, blk * P:(blk + 1) * P], ident)
                    ins.then_inc(S["ptm"], 1)
                    now(pe, "md xdt rmin", tile)
                    last(pe, "std", tile)
                    for hh in range(SH):
                        pe.matmul(bank[5][:, hh * SP_:(hh + 1) * SP_], m[:, hh, :], xdt[:, hh, :], start=True, stop=True)
                    for g in range(SG):
                        ins = pe.matmul(bank[6][:, g * 256:(g + 1) * 256], xc[:, 6 + g, :], hT[:, 4 * g:4 * g + 4, :].rearrange("p a b -> p (a b)"),
                                        start=True, stop=True)
                    ins.then_inc(S["ydm"], 1)
                    now(pe, "pta ptb", tile)
                    for kv in range(NKV):
                        for blk in range(2):
                            ins = pe.matmul(bank[4][kv * HD:(kv + 1) * HD, :], v[:, blk, kv * HD:(kv + 1) * HD],
                                            pT[:, kv, blk].rearrange("p a b -> p (a b)"), start=blk == 0, stop=blk == 1)
                    ins.then_inc(S["pv"], 1)
                    now(pe, "xde", tile)
                    for g in range(SG):
                        ins = pe.matmul(bank[0][:, g * 256:(g + 1) * 256], btok[:, g, :], xde[:, 4 * g:4 * g + 4, :].rearrange("p a b -> p (a b)"),
                                        start=True, stop=True)
                    ins.then_inc(S["stm"], 1)
                    now(pe, "yg", tile)
                    for c in range(4):
                        ins = pe.transpose(bank[1][:, c * P:(c + 1) * P], y[:, 2 * c:2 * c + 2, :].rearrange("p a b -> p (a b)"), ident)
                    ins.then_inc(S["ytm"], 1)
                    now(pe, "at gt", tile)
                    pe_tail(pe, tile, P)
            i8 = ident[0:DEC, 0:DEC]
            pe_front(pe, TILES, DEC)
            for c in range(2):
                for k in range(KC):
                    ins = pe.matmul(bank[3 + c][0:DEC, :], xT[:, k, 0:DEC], w_in[:, k, Z_END + 512 * c:Z_END + 512 * c + 512],
                                    start=k == 0, stop=k == KC - 1)
            ins.then_inc(S["projc"], 1)
            now(pe, "qkr", TILES)
            last(pe, "rankd", TILES)
            for r in range(REP):
                ins = pe.transpose(bank[7][:, r * DEC:(r + 1) * DEC], qkr[0:DEC, 2 * r:2 * r + 2, :].rearrange("p a b -> p (a b)"), i8)
            ins.then_inc(T["q1"], 1)
            pe.wait_ge(cache_in, 64)
            for b in range(DEC):
                ins = pe.transpose(bank[5 + b // 4][:, (b % 4) * P:(b % 4 + 1) * P], keys[:, b, :], ident)
            ins.then_inc(T["kT0"], 1)
            pe.wait_ge(T["q2"], 1)
            pe.wait_ge(T["kT1"], 1)
            now(pe, "qkv", TILES)
            for b in range(DEC):
                ins = pe.matmul(bank[b // 4][0:NH, (b % 4) * P:(b % 4 + 1) * P], q_blk[:, b].rearrange("p k r -> p (k r)"), keysT[:, b, :],
                                start=True, stop=True)
            ins.then_inc(T["sc1"], 1)
            last(pe, "std", TILES)
            for c in range(4):
                ins = pe.transpose(bank[5][:, c * P:(c + 1) * P], hT[:, 2 * c:2 * c + 2, :].rearrange("p a b -> p (a b)"), ident)
            ins.then_inc(T["ssmT"], 1)
            pe.wait_ge(T["dt2"], 1)
            now(pe, "z", TILES)
            pe.transpose(bank[6][0:SH, 0:DEC], dt[0:DEC, 3, :], i8)
            pe.transpose(bank[6][0:SH, DEC:2 * DEC], dt[0:DEC, 4, :], i8).then_inc(T["dt3"], 1)
            pe.wait_ge(T["cv2"], 1)
            pe.wait_ge(T["sc2"], 1)
            for b in range(DEC):
                ins = pe.transpose(bank[2][:, b * NH:(b + 1) * NH], ps[:, b, :], i8)
            ins.then_inc(T["ptm"], 1)
            pe.wait_ge(T["pT"], 1)
            now(pe, "rawc", TILES)
            for b in range(DEC):
                ins = pe.matmul(bank[3][:, b * NH:(b + 1) * NH], vals[:, b, :], ps_T[:, b, :], start=True, stop=True)
            ins.then_inc(T["pv"], 1)
            for c in range(4):
                pe.transpose(bank[4][:, c * DEC:(c + 1) * DEC], st_xc[:, c * P:(c + 1) * P], i8)
            for c in range(4):
                pe.transpose(bank[4][:, (4 + c) * DEC:(5 + c) * DEC], zs[0:DEC, c * P:(c + 1) * P], i8)
            pe.wait_ge(T["xz1"], 1)
            for c in range(4):
                ins = pe.matmul(bank[7][:, c * (2 * DEC + 1):(c + 1) * (2 * DEC + 1)],
                                head_sel[:, c * P:(c + 1) * P], st_da[:, :], start=True, stop=True)
            ins.then_inc(T["xz2"], 1)
            for b in range(DEC):
                if b >= 2:
                    pe.wait_ge(T["hst"], b - 1)
                pe.matmul(bank[b % 2][:, :], ident[0:DEC, b:b + 1].to_broadcast([DEC, P]), st_xc[:, 512:1024],
                          start=True, stop=True).then_inc(T["bc"], 1)
            pe.wait_ge(T["sq"], 1)
            pe.matmul(bank[6][:, 0:4 * DEC], ones, st_g2[:, :, :].rearrange("p a b -> p (a b)"), start=True, stop=True).then_inc(T["nrm"], 1)
            pe.wait_ge(T["aT"], 1)
            pe.wait_ge(T["gT"], 1)
            pe_tail(pe, TILES, DEC)
            pe.wait_ge(T["cnt"], 1)
            pe.matmul(bank[0][:, 0:NE], ones, counted[:, :], start=True, stop=True).then_inc(T["cnt"], 1)

            pe.sem_inc(E_["dn"], 2)
            pe.sem_inc(E_["xT"], 2)

            def expert_down(j, u):
                pe.wait_ge(E_["hid"], j + 2)
                pe.transpose(bank[5][:, 0:P], hid[u], ident).then_inc(E_["hT"], 1)
                pe.wait_ge(E_["hTe"], j + 2)
                pe.wait_ge(E_["ya"], j + 2)
                pe.wait_ge(E_["yd"], j + 2)
                for c in range(2):
                    ins = pe.matmul(bank[6 + c][:, :], hidT[u], wd[u][:, 512 * c:512 * c + 512], start=True, stop=True)
                ins.then_inc(E_["dn"], 1)

            with pe.Fori(0, SLOT_TILES // 2) as pair:
                j0 = pair * 2
                for u in range(2):
                    j = j0 + u
                    pe.wait_ge(e_x[u], 8 * j0 + 16)
                    pe.wait_ge(E_["xTe"], j + 1)
                    pe_turn_x(pe, xg[u], ident, P, (2 * u, 2 * u + 1), E_["xT"])
                    pe.wait_ge(E_["xTe"], j + 3)
                    pe.wait_ge(e_w[u], 24 * j0 + 48)
                    for k in range(KC):
                        ins = pe.matmul(bank[4][:, 0:256], xgT[u][:, k, :], wgu[u][:, :, k, :], start=k == 0, stop=k == KC - 1)
                    ins.then_inc(E_["gu"], 1)
                    expert_down(j, u)


OUTS = [("y_prompt", (1, SEQ, D)), ("y_sample", (DEC, 1, D)), ("win_k_prompt", (1, 1, P, NKV, HD)), ("win_v_prompt", (1, 1, P, NKV, HD)),
        ("conv_prompt", (P, CC, CK - 1)), ("ssm_prompt", (1, 1, SH, SP_, SN)), ("win_k_sample", (1, DEC, P, NKV, HD)),
        ("win_v_sample", (1, DEC, P, NKV, HD)), ("conv_sample", (1, DEC, CK - 1, CD)), ("ssm_sample", (1, DEC, SH, SP_, SN))]
N_SSM = 16 * (0 + 1 + 3 + 2 + 1 + 1)
N_OUTS = N_SSM + 16 * DEC


def kernel(**inputs):
    import concourse.bacc as bacc
    from concourse.bass_utils import run_bass_kernel_spmd

    nc = bacc.Bacc("TRN2", target_bir_lowering=False, num_devices=1)
    arrays, ins, outs = {}, {}, {}
    given = dict(inputs, constants=shape_constants(), rope=rope_table())
    given["conv_w_by_channel"] = np.asarray(inputs["conv_w"])[0].reshape(CK, CC, P).transpose(2, 1, 0)
    given["conv_b_by_channel"] = np.asarray(inputs["conv_b"])[0].reshape(CC, P).T
    given["ssm_norm_by_channel"] = np.asarray(inputs["ssm_norm"])[0].reshape(4, P).T
    for name, a in given.items():
        a = np.ascontiguousarray(a)
        arrays[f"in_{name}"] = a
        ins[name] = nc.dram_tensor(f"in_{name}", a.shape, mybir.dt.from_np(a.dtype), kind="ExternalInput").ap()
    for name, shape in OUTS:
        outs[name] = nc.dram_tensor(f"out_{name}", shape, F32, kind="ExternalOutput").ap()
    layer_kernel(nc, ins, outs)
    r = run_bass_kernel_spmd(nc, [arrays], core_ids=[0])
    got = {name: r.results[0][f"out_{name}"] for name, _ in OUTS}
    got["conv_prompt"] = got["conv_prompt"].transpose(2, 1, 0).reshape(1, 1, CK - 1, CD)
    return tuple(got[name] for name, _ in OUTS)
```

```python
from contextlib import ExitStack

import numpy as np

import concourse.bass as bass
from concourse import mybir
from concourse.alu_op_type import AluOpType as ALU

F32 = mybir.dt.float32
BF16 = mybir.dt.bfloat16
I32 = mybir.dt.int32
U32 = mybir.dt.uint32
ACT = mybir.ActivationFunctionType
AX = mybir.AxisListType

P = 128
D = 1024
KC = D // P
SEQ = 1024
TILES = SEQ // P
DEC = 8
TOKENS = SEQ + DEC
NH, NKV, HD = 8, 2, 64
REP = NH // NKV
PAST = 8192
THETA = 10000.0
SCALE = HD ** -0.5
SH, SG, SP_, SN = 8, 2, 64, 128
CK = 4
CD = SH * SP_ + 2 * SG * SN
CC = CD // P
Q_END = NH * HD
K_END = Q_END + NKV * HD
V_END = K_END + NKV * HD
Z_END = V_END + SH * SP_
XBC_END = Z_END + CD
IN_DIM = XBC_END + SH
NG, EPG = 4, 8
NE = NG * EPG
FF = D // 8
EPS = 1e-6
BIG = 1e30
CHOICES = 2 * TOKENS
ROWS = P
OVER_TILES = CHOICES // (ROWS + 1)
SLOT_TILES = NE + OVER_TILES
EMPTY = 8192
RING = 4
CREDIT = 2

C_ID, C_TRI, C_STRICT, C_ONES, C_BAND, C_IOTA, C_CHOICE = 0, 128, 256, 384, 512, 768, 896
C_END = C_CHOICE + 2 * (TILES + 1)


def shape_constants():
    c = np.zeros((P, C_END), np.float32)
    r, q = np.arange(P)[:, None], np.arange(P)[None, :]
    c[:, C_ID:C_ID + P] = r == q
    c[:, C_TRI:C_TRI + P] = r <= q
    c[:, C_STRICT:C_STRICT + P] = r < q
    c[:, C_ONES:C_ONES + P] = 1.0
    c[:, C_BAND:C_BAND + P] = np.where(q > r, 0.0, -BIG)
    c[:, C_BAND + P:C_BAND + 2 * P] = np.where(q <= r, 0.0, -BIG)
    c[:, C_IOTA:C_IOTA + P] = np.arange(P)
    i = np.arange(2 * (TILES + 1))
    c[:, C_CHOICE:C_END] = i % 2 * TOKENS + i // 2 * P + r - EMPTY
    return c


def rope_table():
    inv = np.float32(1.0) / np.power(THETA, np.arange(0, HD, 2) / HD).astype(np.float32)
    pos = np.concatenate([np.arange(SEQ), np.full(P, PAST)]).astype(np.float32)
    ang = pos[:, None] * inv[None, :]
    ang = ang.astype(np.float64)
    return np.concatenate([np.cos(ang), np.sin(ang)], axis=1).astype(np.float32)


def layer_kernel(nc, I, O):
    with ExitStack() as ctx:
        def sb(name, shape, dt=F32):
            return ctx.enter_context(nc.sbuf_tensor(name, shape, dt))

        def sem(name):
            return ctx.enter_context(nc.semaphore(name))

        bank = [ctx.enter_context(nc.psum_tensor(f"bank{n}", [P, 512], F32)) for n in range(8)]
        h_dram = nc.dram_tensor("h_dram", (TOKENS, D), F32, kind="Internal").ap()
        t_dram = nc.dram_tensor("t_dram", (TOKENS, D), F32, kind="Internal").ap()
        y_dram = nc.dram_tensor("y_dram", (CHOICES, D), F32, kind="Internal").ap()

        con = sb("con", [P, C_END])
        ident, tri, strict, ones = (con[:, c:c + P] for c in (C_ID, C_TRI, C_STRICT, C_ONES))
        w_arena = sb("w_arena", [P, KC * IN_DIM])
        w_in = w_arena[:, :].rearrange("p (k n) -> p k n", k=KC)
        w_out = sb("w_out_sb", [P, KC, D])
        w_route = sb("w_route", [P, KC, NG + NE])
        b_route = sb("b_route", [P, NG + NE])
        norm1 = sb("norm1_sb", [P, KC])
        norm2 = sb("norm2_sb", [P, D])
        qk_norm = sb("qk_norm", [P, 2, HD])
        sink = sb("sink", [P, NH])
        sink_col = sb("sink_col", [NH, 1])
        conv_w = sb("conv_w_sb", [P, CC, CK])
        conv_b = sb("conv_b_sb", [P, CC])
        dt_bias = sb("dt_bias_sb", [P, SH])
        a_neg = sb("a_neg", [P, SH])
        d_skip = sb("d_skip_sb", [P, SH])
        d_col = sb("d_col", [SH, 1])
        ssm_norm = sb("ssm_norm_sb", [P, 4])
        neg_half = sb("neg_half", [P, 16])
        eps = sb("eps", [P, 16])
        mask = sb("mask", [P, 2, P])

        x = [sb(f"x{u}", [P, D]) for u in range(2)]
        rope = [sb(f"rope{u}", [P, HD]) for u in range(2)]
        xn = sb("xn", [P, D])
        xT = sb("xT", [P, KC, P])
        junk = sb("junk", [P, D], BF16)
        stat = sb("stat", [P, 16])
        rstd = sb("rstd", [P, 16])
        qk = sb("qk", [P, 10, HD])
        qkr = sb("qkr", [P, 10, HD])
        v_new = sb("v_new", [P, P])
        v = sb("v", [P, 2, P])
        qT = sb("qT", [P, REP, P])
        kT = sb("kT", [P, 2, P])
        s = sb("s", [P, NH, 2 * P])
        top = sb("top", [P, 4, NH])
        pT = sb("pT", [P, NKV, 2, REP, P])
        aT = sb("aT", [P, REP, P])
        dt = sb("dt", [P, 5, SH])
        zs = sb("zs", [P, SH * SP_])
        raw = sb("raw", [P, CC, P + CK - 1])
        cv = sb("cv", [P, CC, P])
        xc = sb("xc", [P, CC, P])
        xtok = sb("xtok", [P, SH, SP_])
        btok = sb("btok", [P, SG, P])
        xdt = sb("xdt", [P, SH, SP_])
        xde = sb("xde", [P, SH, SP_])
        xd = sb("xd", [P, SH, SP_])
        cum = sb("cum", [P, 3, SH])
        ecum = sb("ecum", [P, 3, SH])
        cbm = sb("cbm", [P, SG, P])
        m = cv
        hT = sb("hT", [P, SH, SP_])
        y = sb("y", [P, SH, SP_])
        gT = sb("gT", [P, 4, P])
        t = sb("t", [P, D])
        tT = sb("tT", [P, KC, P])
        lg = sb("lg", [P, 8 + NE])
        le = sb("le", [P, NG, EPG])
        g8 = sb("g8", [P, 8])
        e8 = sb("e8", [P, 8])
        gi = sb("gi", [P, 8], U32)
        ei = sb("ei", [P, 8], U32)
        fi = sb("fi", [P, 16])
        gmask = sb("gmask", [P, 2, NG])
        rt = sb("rt", [P, 8])
        rexp = sb("rexp", [P, NG])
        onehot = sb("onehot", [P, TILES + 1, 2, NE])
        both = sb("both", [P, NE])
        counted = sb("counted", [P, NE])
        rankc = sb("rankc", [P, NE])
        rprod = sb("rprod", [P, 2, NE])
        rank = sb("rank", [P, TILES + 1, 2])
        gate = sb("gate", [P, TILES + 1, 2])

        keys = pT[:, 0, :, :, :].rearrange("p a b c -> p (a b) c")
        vals = pT[:, 1, :, :, :].rearrange("p a b c -> p (a b) c")
        keysT = xT
        q_blk = sb("q_blk", [P, DEC, NKV, REP])
        flat_s = s[:, :, :].rearrange("p a b -> p (a b)")
        ps = flat_s[0:NH, 0:DEC * P].rearrange("p (b s) -> p b s", b=DEC)
        ps_T = sb("ps_T", [P, DEC, NH])
        m_top = sb("m_top", [NH, 4, DEC])
        st_conv = w_arena[0:DEC, 0:3 * CD].rearrange("p (k c) -> p k c", k=CK - 1)
        st_w = w_arena[0:DEC, 3 * CD:7 * CD].rearrange("p (k c) -> p k c", k=CK)
        st_b = w_arena[0:DEC, 7 * CD:8 * CD]
        st_raw = xn[0:DEC, :]
        st_acc = w_arena[0:DEC, 9 * CD:10 * CD]
        st_tmp = w_arena[0:DEC, 10 * CD:11 * CD]
        st_xc = flat_s[0:DEC, CD:2 * CD]
        st_h = w_arena[:, 12 * CD:16 * CD].rearrange("p (b c n) -> p b c n", b=DEC, c=4)
        head_sel = w_arena[0:SH, 16 * CD:16 * CD + SH * SP_]
        flat_cv = cv[:, :, :].rearrange("p a b -> p (a b)")
        st_bx = [flat_cv[:, u * 512:(u + 1) * 512].rearrange("p (c n) -> p c n", c=4) for u in range(2)]
        st_ch = hT[:, :, :].rearrange("p a b -> p (a b)").rearrange("p (c n) -> p c n", c=4)
        st_turned = y[:, :, :].rearrange("p a b -> p (a b)").rearrange("p (c n) -> p c n", c=4)
        st_xT = sb("st_xT", [P, 4, DEC])
        st_zT = sb("st_zT", [P, 4, DEC])
        st_da = sb("st_da", [SH, 2 * DEC + 1])
        st_sc = sb("st_sc", [P, 4, 2 * DEC + 1])
        st_dx = sb("st_dx", [P, 4, DEC])
        st_y = sb("st_y", [P, 4, DEC])
        st_g2 = sb("st_g2", [P, 4, DEC])
        st_n = sb("st_n", [P, SG, DEC])
        st_r = sb("st_r", [P, SG, DEC])

        PAIRS = 2 * (TILES + 1)
        slot_tab = sb("slot_tab", [P, SLOT_TILES, 2], I32)
        slot_f = sb("slot_f", [P, 3, NE])
        etile_i = sb("etile_i", [1, OVER_TILES], I32)
        over_i = sb("over_i", [1, 1], I32)
        flat_raw = raw[:, :, :].rearrange("p c n -> p (c n)")
        flat_pT = pT[:, :, :, :, :].rearrange("p a b c d -> p (a b c d)")
        flat_xc = xc[:, :, :].rearrange("p a b -> p (a b)")
        chosen = flat_raw[:, 0:PAIRS * NE].rearrange("p (i e) -> p i e", e=NE)
        THIRD = PAIRS // 3
        row_sel = [half[:, :].rearrange("p (i r) -> p i r", r=P)
                   for half in (flat_s[:, 0:THIRD * P], flat_s[:, THIRD * P:2 * THIRD * P], flat_xc[:, 0:THIRD * P])]
        over_sel = [half[:, :].rearrange("p (i r) -> p i r", r=P)
                    for half in (flat_pT[:, 0:THIRD * P], flat_pT[:, THIRD * P:2 * THIRD * P], flat_xc[:, 0:THIRD * P])]
        flat_onehot = onehot[:, :, :, :].rearrange("p a b e -> p (a b) e")
        flat_rank = rank[:, :, :].rearrange("p a b -> p (a b)")
        quo = w_arena[:, 17000:17000 + 4 * PAIRS].rearrange("p (a e) -> p a e", a=4)
        nt = w_arena[:, 17500:17500 + 4 * NE].rearrange("p (a e) -> p a e", a=4)
        pair_prod = w_arena[:, 17700:17700 + PAIRS * NE].rearrange("p (a e) -> p a e", e=NE)
        ecmp = flat_cv[0:1, 0:OVER_TILES * NE].rearrange("p (j e) -> p j e", e=NE)
        etile = flat_cv[0:1, OVER_TILES * NE:OVER_TILES * (NE + 1)]

        def arena(at, n):
            return w_arena[:, at:at + n]
        wgu = [arena(w * 3 * D, 2 * D).rearrange("p (a k f) -> p a k f", a=2, k=KC) for w in range(RING)]
        wd = [arena(w * 3 * D + 2 * D, D) for w in range(RING)]
        xg = [x[1][:, :], xn[:, :], xT[:, :, :].rearrange("p a b -> p (a b)"), tT[:, :, :].rearrange("p a b -> p (a b)")]
        xgT = [arena((12 + u) * D, D).rearrange("p (k f) -> p k f", k=KC) for u in range(2)]
        sil = [arena(14 * D + u * P, P) for u in range(2)]
        hidT = [arena(14 * D + (2 + u) * P, P) for u in range(2)]
        yo = [flat_s[:, u * D:(u + 1) * D] for u in range(2)]
        idx_in = [sb(f"idx_in{w}", [P, 1], I32) for w in range(RING)]
        idx_out = [sb(f"idx_out{w}", [P, 1], I32) for w in range(RING)]
        c_h = [w_out[:, c, :] for c in range(TILES)] + [x[0][:, :]]
        c_y = [[arena((2 * w + k) * D, D) for k in range(2)] for w in range(4)]

        loaded = sem("loaded")
        S = {}
        for name in ("ssq xs xn xm xT projq projk projz proja projc qe qkv vc rawa dtp dl dta z rawc cumm cum ecd qsq qs qkr qkt qkc sc0 sc1 sc2 sc3 "
                     "se smax pexp prob ptm pta ptb pv at convd xcs xtm xtk xdt xde xd rmm rmin rexpd cbm md ydm yf "
                     "stm std ysq ys yg ytm gt conva wom hres hsq hs td ttm tt lgm sel gex rsel rankm rankd").split():
            S[name] = sem("s_" + name)
        T = {}
        for name in "init aneg q kT att cv dt dx xz bc bx hst norm ssmT ssmC cnt slots et over".split():
            T[name] = sem("m_" + name)
        E_ = {}
        for name in ("turn xa xd up sil hid dn ya yd idx").split():
            E_[name] = sem("e_" + name)
        V = {}
        for name in ("turn xe up sil hid dn ye idx").split():
            V[name] = sem("o_" + name)
        x_in = [sem(f"x_in{u}") for u in range(2)]
        h_out = [sem(f"h_out{u}") for u in range(2)]
        t_out = [sem(f"t_out{u}") for u in range(2)]
        cache_in = sem("cache_in")
        state_in = sem("state_in")
        e_w = [sem(f"e_w{w}") for w in range(RING)]
        e_x = [sem(f"e_x{w}") for w in range(4)]
        e_out = [sem(f"e_out{u}") for u in range(2)]
        o_w, o_x, o_out = sem("o_w"), sem("o_x"), sem("o_out")
        c_in = sem("c_in")
        c_in1 = [sem(f"c_in1{w}") for w in range(4)]
        c_done = sem("c_done")
        c_out = sem("c_out")
        kv_out = sem("kv_out")
        first_in, params, w_q, w_x, w_z = (sem(name) for name in ("first_in", "params", "w_q", "w_x", "w_z"))
        outs = sem("outs")
        block = ctx.enter_context(nc.Block())

        def now(eng, names, tile):
            for name in names.split():
                eng.wait_ge(S[name], tile + (CREDIT + 1))

        def last(eng, names, tile):
            for name in names.split():
                eng.wait_ge(S[name], tile + CREDIT)

        def credit(eng, names):
            for name in names.split():
                eng.sem_inc(S[name], CREDIT)

        flat_x = I["x_prompt"].rearrange("a s d -> (a s) d")
        n_loaded = [0]
        N_PARAMS = 16 * 11

        def row(name, n):
            return I[name].rearrange("a n -> (a n)").rearrange("(a n) -> a n", a=1).broadcast_to([n, I[name].shape[-1]])

        @block.sync
        def _(sp):
            def load(dst, src):
                sp.dma_start(dst, src).then_inc(loaded, 16)
                n_loaded[0] += 16

            sp.dma_start(norm1[:, :], I["norm1"].rearrange("a (p k) -> (a p) k", k=KC)).then_inc(first_in, 16)
            sp.dma_start(con[:, :], I["constants"]).then_inc(first_in, 16)
            for u in range(2):
                sp.dma_start(x[u][:, :], flat_x[u * P:(u + 1) * P, :]).then_inc(x_in[u], 16)
                sp.dma_start(rope[u][:, :], I["rope"][u * P:(u + 1) * P, :]).then_inc(x_in[u], 16)
            w_rows = I["w_in"].rearrange("a (p k) n -> (a p) k n", k=KC)
            for cols, landed in ((slice(0, V_END), w_q), (slice(Z_END, IN_DIM), w_x), (slice(V_END, Z_END), w_z)):
                sp.dma_start(w_in[:, :, cols], w_rows[:, :, cols]).then_inc(landed, 16)
            for kv in range(NKV):
                load(w_out[kv * HD:(kv + 1) * HD, 0:REP, :],
                     I["w_out"][0, kv * REP * HD:(kv + 1) * REP * HD].rearrange("(r d) n -> d r n", d=HD))
            load(w_out[:, REP:KC, :], I["w_out"][0, NH * HD:].rearrange("(c p) n -> p c n", p=P))
            load(norm2[:, :], row("norm2", P))
            load(w_route[:, :, 0:NG], I["w_grp"].rearrange("a (p k) n -> (a p) k n", k=KC))
            load(w_route[:, :, NG:NG + NE], I["w_exp"].rearrange("a (p k) n -> (a p) k n", k=KC))
            load(b_route[:, 0:NG], row("b_grp", P))
            load(b_route[:, NG:NG + NE], row("b_exp", P))

            with sp.Fori(0, TILES // 2 - 1) as pair:
                t0 = pair * 2
                for u in range(2):
                    sp.wait_ge(first_in, 32)
                    sp.wait_ge(S["td"], t0 + (u + CREDIT + 1))
                    sp.dma_start(rope[u][:, :], I["rope"][bass.ds(t0 * P + (u + 2) * P, P), :]).then_inc(x_in[u], 16)
                    sp.wait_ge(h_out[u], 8 * t0 + 32)
                    sp.dma_start(x[u][:, :], flat_x[bass.ds(t0 * P + (u + 2) * P, P), :]).then_inc(x_in[u], 16)
            now(sp, "td", TILES - 2)
            sp.wait_ge(h_out[0], 16 + 16 * (TILES // 2))
            sp.dma_start(x[0][0:DEC, :], I["x_sample"].rearrange("b s d -> (b s) d")).then_inc(x_in[0], 16)
            sp.dma_start(rope[0][0:DEC, :], I["rope"][SEQ:SEQ + DEC, :]).then_inc(x_in[0], 16)
            now(sp, "qkr", TILES - 1)
            sp.dma_start(O["win_k_prompt"].rearrange("a b s k d -> (a b s) (k d)"), qkr[:, 8:10, :].rearrange("p a b -> p (a b)")).then_inc(kv_out, 16)
            last(sp, "convd pv", TILES)
            sp.dma_start(O["win_v_prompt"].rearrange("a b s k d -> (a b s) (k d)"), v[:, 1, :]).then_inc(outs, 16)
            sp.dma_start(O["conv_prompt"], raw[:, :, 0:CK - 1]).then_inc(outs, 16)
            ck = I["cache_win_k"].rearrange("a b s k d -> (a s) b (k d)")
            cw = I["cache_win_v"].rearrange("a b s k d -> (a s) b (k d)")
            sp.dma_start(keys[0:P - 1, :, :], ck[1:P]).then_inc(cache_in, 16)
            sp.dma_start(vals[0:P - 1, :, :], cw[1:P]).then_inc(cache_in, 16)
            for name in ("k", "v"):
                o = O[f"win_{name}_sample"].rearrange("a b s k d -> (a b) s (k d)")
                i = I[f"cache_win_{name}"].rearrange("a b s k d -> (a b) s (k d)")
                sp.dma_start(o[:, 0:P - 1, :], i[:, 1:P, :]).then_inc(outs, 16)
            sp.dma_start(O["conv_sample"][0, :, 0:CK - 2, :], I["state_conv"][0, :, 1:CK - 1, :]).then_inc(outs, 16)
            now(sp, "qkr qkv", TILES)
            new_k = qkr[0:DEC, 8:10, :].rearrange("p a b -> p (a b)")
            new_v = v_new[0:DEC, :]
            sp.dma_start(keys[P - 1:P, :, :], new_k).then_inc(cache_in, 16)
            sp.dma_start(vals[P - 1:P, :, :], new_v).then_inc(cache_in, 16)
            sp.dma_start(O["win_k_sample"].rearrange("a b s k d -> (a b) s (k d)")[:, P - 1, :], new_k).then_inc(outs, 16)
            sp.dma_start(O["win_v_sample"].rearrange("a b s k d -> (a b) s (k d)")[:, P - 1, :], new_v).then_inc(outs, 16)
            now(sp, "projz", TILES)
            sp.dma_start(st_conv, I["state_conv"][0]).then_inc(state_in, 16)
            sp.dma_start(st_w, I["conv_w"].broadcast_to([DEC, CK, CD])).then_inc(state_in, 16)
            sp.dma_start(st_b, row("conv_b", DEC)).then_inc(state_in, 16)
            for b in range(DEC):
                sp.dma_start(st_h[:, b], I["state_ssm"][0, b].rearrange("(c l) p n -> (l p) c n", l=2)).then_inc(state_in, 16)
            now(sp, "rawc", TILES)
            sp.dma_start(O["conv_sample"][0, :, CK - 2, :], st_raw).then_inc(outs, 16)
            def expert_weights(e, w):
                one = bass.ds(e, 1)
                return (sp.dma_start(wgu[w][:, 0], I["w_gate"][0, one].rearrange("a (p k) f -> (a p) k f", k=KC)),
                        sp.dma_start(wgu[w][:, 1], I["w_up"][0, one].rearrange("a (p k) f -> (a p) k f", k=KC)),
                        sp.dma_start(wd[w], I["w_down"][0, one].rearrange("a f n -> (a f) n")))

            sp.wait_ge(T["cv"], 2)
            for w in range(RING):
                for one in expert_weights(w, w):
                    one.then_inc(e_w[w], 16)
            sp.wait_ge(T["ssmC"], 1)
            sp.dma_start(O["ssm_prompt"].rearrange("a b (c l) p n -> (a b l p) c n", l=2), st_turned).then_inc(outs, 16)
            for b in range(DEC):
                sp.wait_ge(T["hst"], b + 1)
                sp.dma_start(O["ssm_sample"][0, b].rearrange("(c l) p n -> (l p) c n", l=2), st_h[:, b]).then_inc(outs, 16)
            now(sp, "wom", TILES)
            for u in range(2):
                sp.wait_ge(h_out[u], 16 + 16 * ((TILES + 1 - u) // 2))
            for c in range(TILES):
                sp.dma_start(c_h[c], h_dram[c * P:(c + 1) * P, :]).then_inc(c_in, 16)
            with sp.Fori(1, NE // RING) as group:
                for w in range(RING):
                    sp.wait_ge(first_in, 32)
                    sp.wait_ge(E_["dn"], RING * group + (w - RING + 2))
                    for one in expert_weights(RING * group + w, w):
                        one.then_inc(e_w[w], 16)
            sp.wait_ge(T["et"], 1)
            over = sp.value_load(over_i[0:1, 0:1], min_val=0, max_val=OVER_TILES)
            with sp.If(over > 0):
                sp.wait_ge(E_["dn"], NE + 1)
                with sp.Fori(0, OVER_TILES) as j:
                    e = sp.value_load(etile_i[0:1, bass.ds(j, 1)], min_val=0, max_val=NE - 1)
                    sp.wait_ge(T["et"], 1)
                    sp.wait_ge(V["dn"], j + 1)
                    for one in expert_weights(e, 0):
                        one.then_inc(o_w, 16)
                sp.wait_ge(o_out, 16 * OVER_TILES)
                sp.wait_ge(V["dn"], OVER_TILES + 1)
            sp.wait_ge(E_["dn"], NE + 1)
            for u in range(2):
                sp.wait_ge(e_out[u], 16 * NE // 2)
            for c in range(TILES + 1):
                n, w = (P if c < TILES else DEC), c % 4
                if c >= 4:
                    sp.wait_ge(c_done, c - 3)
                for k in range(2):
                    at = k * TOKENS + c * P
                    sp.dma_start(c_y[w][k][0:n, :], y_dram[at:at + n, :]).then_inc(c_in1[w], 16)
            sp.wait_ge(c_out, 16 * (TILES + 1))
            sp.wait_ge(outs, N_OUTS)

        def rows(ap, n):
            return ap[0:n]

        def act_rows(act, tile, u, n, x_need):
            act.wait_ge(x_in[u], x_need)
            last(act, "xs", tile)
            act.activation(junk[0:n, :], x[u][0:n, :], ACT.Square, scale=D ** -0.5, accum_out=stat[0:n, 0:1]).then_inc(S["ssq"], 1)
            now(act, "xs", tile)
            last(act, "xm", tile)
            act.activation(xn[0:n, :], x[u][0:n, :], ACT.Copy, scale=rstd[0:n, 0:1]).then_inc(S["xn"], 1)

        def act_q(act, tile, n):
            now(act, "projq", tile)
            last(act, "qkr", tile)
            act.activation(qk[0:n, 0:8, :].rearrange("p a b -> p (a b)"), bank[0][0:n, :], ACT.Copy).then_inc(S["qe"], 1)

        def act_kv(act, tile, n):
            now(act, "projk", tile)
            last(act, "qkr dta vc", tile)
            act.activation(qk[0:n, 8:10, :].rearrange("p a b -> p (a b)"), bank[1][0:n, 0:P], ACT.Copy)
            act.activation(v_new[0:n, :], bank[1][0:n, P:2 * P], ACT.Copy)
            act.activation(dt[0:n, 0, :], bank[1][0:n, 2 * P:2 * P + SH], ACT.Copy).then_inc(S["qkv"], 1)

        def act_raw(act, tile, n, half):
            now(act, ("proja", "projc")[half], tile)
            last(act, ("conva", "convd")[half], tile)
            if n == P:
                out = raw[:, 4 * half:4 * half + 4, CK - 1:]
                act.activation(out, bank[half][:, :].rearrange("p (c n) -> p c n", c=4), ACT.Copy).then_inc(S[("rawa", "rawc")[half]], 1)
            else:
                act.activation(st_raw[:, 512 * half:512 * half + 512], bank[half][0:n, :], ACT.Copy).then_inc(S[("rawa", "rawc")[half]], 1)

        def act_softplus(act, tile, n):
            now(act, "dtp", tile)
            act.activation(dt[0:n, 2, :], dt[0:n, 1, :], ACT.Exp, scale=-1.0)
            act.drain()
            act.activation(dt[0:n, 2, :], dt[0:n, 2, :], ACT.Ln, bias=1.0).then_inc(S["dl"], 1)

        def act_z(act, tile, n):
            now(act, "projz", tile)
            last(act, "yf", tile)
            act.activation(zs[0:n, :], bank[0][0:n, :], ACT.Silu).then_inc(S["z"], 1)

        def act_residual(act, tile, u, n, dram_rows):
            now(act, "hres", tile)
            act.dma_start(h_dram[dram_rows, :], x[u][0:n, :]).then_inc(h_out[u], 16)
            act.activation(junk[0:n, :], x[u][0:n, :], ACT.Square, scale=D ** -0.5, accum_out=stat[0:n, 13:14]).then_inc(S["hsq"], 1)

        def act_store_t(act, tile, u, n, dram_rows):
            now(act, "td", tile)
            act.dma_start(t_dram[dram_rows, :], t[0:n, :]).then_inc(t_out[u], 16)

        def act_turned_t(act, tile, n):
            now(act, "ttm", tile)
            act.activation(tT[:, 0:4, 0:n], bank[5][:, 0:4 * n].rearrange("p (k n) -> p k n", k=4), ACT.Copy)
            act.activation(tT[:, 4:8, 0:n], bank[6][:, 0:4 * n].rearrange("p (k n) -> p k n", k=4), ACT.Copy).then_inc(S["tt"], 1)

        def act_conv(act, tile):
            now(act, "convd", tile)
            last(act, "ydm", tile)
            act.activation(xc[:, :, :], cv[:, :, :], ACT.Silu).then_inc(S["xcs"], 1)

        def act_router(act, tile, n):
            now(act, "sel", tile)
            act.activation(rexp[0:n, :], lg[0:n, 0:NG], ACT.Exp, bias=rt[0:n, 0:1], accum_out=rt[0:n, 1:2])
            act.activation(rt[0:n, 3:4], e8[0:n, 1:2], ACT.Exp, bias=rt[0:n, 2:3]).then_inc(S["gex"], 1)

        @block.scalar
        def _(act):
            credit(act, "ssq xn qe qkv vc dl z rawa rawc ecd pexp pta at xcs xtk rexpd ysq hsq tt gex")
            for u in range(2):
                act.sem_inc(h_out[u], 16)
                act.sem_inc(t_out[u], 16)
            for dst, src in (
                    (qk_norm[:, 0, :], row("q_norm", P)),
                    (qk_norm[:, 1, :], row("k_norm", P)),
                    (sink[:, :], row("sinks", P)),
                    (sink_col[:, :], I["sinks"].rearrange("a (n b) -> (a n) b", b=1)),
                    (d_col[:, :], I["d_skip"].rearrange("a (n b) -> (a n) b", b=1)),
                    (conv_w[:, :, :], I["conv_w_by_channel"]),
                    (conv_b[:, :], I["conv_b_by_channel"]),
                    (dt_bias[:, :], row("dt_bias", P)),
                    (a_neg[:, :], row("a_log", P)),
                    (d_skip[:, :], row("d_skip", P)),
                    (ssm_norm[:, :], I["ssm_norm_by_channel"]),
            ):
                act.dma_start(dst, src).then_inc(params, 16)
            act_rows(act, 0, 0, P, 32)
            act_q(act, 0, P)
            act_kv(act, 0, P)
            act_raw(act, 0, P, 0)
            act_raw(act, 0, P, 1)
            act.wait_ge(params, N_PARAMS)
            act.activation(a_neg[:, :], a_neg[:, :], ACT.Exp).then_inc(T["aneg"], 1)
            act_softplus(act, 0, P)
            act_z(act, 0, P)
            act_conv(act, 0)
            act.wait_ge(T["init"], 1)

            def act_tile(tile, u, n_next, x_need, dram_rows, first=False):
                if not first:
                    act_turned_t(act, tile - 1, P)
                act_rows(act, tile + 1, 1 - u, n_next, x_need)
                last(act, "pv", tile)
                act.activation(v[:, 0, :], v[:, 1, :], ACT.Copy)
                act.drain()
                act.activation(v[:, 1, :], v_new[:, :], ACT.Copy).then_inc(S["vc"], 1)
                now(act, "cum", tile)
                last(act, "yf std xde", tile)
                act.activation(ecum[:, :, :], cum[:, :, :], ACT.Exp).then_inc(S["ecd"], 1)
                now(act, "xtm", tile)
                last(act, "stm yf xd xdt", tile)
                act.activation(xtok[:, :, :].rearrange("p a b -> p (a b)"), bank[2][:, :], ACT.Copy)
                act.activation(btok[:, :, :].rearrange("p a b -> p (a b)"), bank[3][:, 0:2 * P], ACT.Copy).then_inc(S["xtk"], 1)
                now(act, "smax", tile)
                for hh in range(NH):
                    act.activation(s[:, hh, :], s[:, hh, :], ACT.Exp, bias=top[:, 1, hh:hh + 1], accum_out=top[:, 2, hh:hh + 1])
                act.activation(top[:, 3, :], top[:, 3, :], ACT.Exp).then_inc(S["pexp"], 1)
                now(act, "rmin", tile)
                act.activation(m[:, :, :], m[:, :, :], ACT.Exp).then_inc(S["rexpd"], 1)
                if not first:
                    act_router(act, tile - 1, P)
                act_q(act, tile + 1, n_next)
                act_kv(act, tile + 1, n_next)
                now(act, "ptm", tile)
                last(act, "pv", tile)
                act.activation(pT[:, 0, 0].rearrange("p a b -> p (a b)"), bank[4][:, :], ACT.Copy)
                act.activation(pT[:, 0, 1].rearrange("p a b -> p (a b)"), bank[2][:, :], ACT.Copy).then_inc(S["pta"], 1)
                now(act, "pv", tile)
                last(act, "wom", tile)
                act.activation(aT[:, :, :].rearrange("p a b -> p (a b)"), bank[4][:, :], ACT.Copy).then_inc(S["at"], 1)
                now(act, "yf", tile)
                last(act, "ys", tile)
                for g in range(SG):
                    ins = act.activation(junk[:, 256 * g:256 * g + 256], y[:, 4 * g:4 * g + 4, :].rearrange("p a b -> p (a b)"),
                                         ACT.Square, scale=256 ** -0.5, accum_out=stat[:, 11 + g:12 + g])
                ins.then_inc(S["ysq"], 1)
                act_raw(act, tile + 1, n_next, 0)
                act_softplus(act, tile + 1, n_next)
                act_raw(act, tile + 1, n_next, 1)
                act.drain()
                act_residual(act, tile, u, P, dram_rows)
                act_store_t(act, tile, u, P, dram_rows)
                act_z(act, tile + 1, n_next)
                if n_next == P:
                    act_conv(act, tile + 1)

            act_tile(0, 0, P, 32, slice(0, P), first=True)
            with act.Fori(0, TILES // 2 - 1) as pair:
                t0 = pair * 2 + 1
                for u in range(2):
                    act_tile(t0 + u, 1 - u, P, 32 * pair + 64, bass.ds(t0 * P + u * P, P))
            act_tile(TILES - 1, 1, DEC, 16 * TILES + 32, slice((TILES - 1) * P, TILES * P))
            act_turned_t(act, TILES - 1, P)
            act_router(act, TILES - 1, P)
            act.wait_ge(T["dt"], 1)
            act.activation(dt[0:DEC, 4, :], dt[0:DEC, 4, :], ACT.Exp).then_inc(T["dt"], 1)
            act.wait_ge(T["cv"], 1)
            act.activation(st_xc, st_acc, ACT.Silu).then_inc(T["cv"], 1)
            act.wait_ge(T["att"], 2)
            act.activation(ps, ps, ACT.Exp)
            act.activation(m_top[:, 3, :], m_top[:, 3, :], ACT.Exp).then_inc(T["att"], 1)
            act.wait_ge(T["dx"], 1)
            for b in range(DEC):
                act.wait_ge(T["bc"], b + 1)
                if b >= 2:
                    act.wait_ge(T["hst"], b - 1)
                for c in range(4):
                    ins = act.activation(st_bx[b % 2][:, c, :], bank[b % 2][:, (c // 2) * P:(c // 2 + 1) * P], ACT.Copy,
                                         scale=st_dx[:, c, b:b + 1])
                ins.then_inc(T["bx"], 1)
            act.drain()
            act_residual(act, TILES, 0, DEC, slice(SEQ, TOKENS))
            act_store_t(act, TILES, 0, DEC, slice(SEQ, TOKENS))
            act_turned_t(act, TILES, DEC)
            act_router(act, TILES, DEC)

            act.sem_inc(E_["ya"], 1)
            act.sem_inc(V["ye"], 1)
            act.wait_ge(outs, N_OUTS)

            def act_turned(j, w):
                act.wait_ge(E_["turn"], j + 1)
                act.activation(xgT[w % 2][:, 0:4, :].rearrange("p a b -> p (a b)"), bank[w % 2 * 2][:, :], ACT.Copy).then_inc(E_["xa"], 1)

            def act_expert(j, w, stored, more=True):
                u = w % 2
                act.wait_ge(E_["up"], j + 1)
                act.activation(sil[u], bank[4 + u][:, 0:P], ACT.Silu).then_inc(E_["sil"], 1)
                if more:
                    act_turned(j + 1, (w + 1) % RING)
                act.wait_ge(E_["dn"], j + 2)
                if stored is not None:
                    act.wait_ge(e_out[u], stored)
                act.activation(yo[u][:, 0:512], bank[6][:, :], ACT.Copy).then_inc(E_["ya"], 1)

            act_turned(0, 0)
            for w in range(RING):
                act_expert(w, w, 16 * (w // 2) if w >= 2 else None)
            with act.Fori(1, NE // RING - 1) as group:
                for w in range(RING):
                    act_expert(RING * group + w, w, 32 * group + 16 * (w // 2))
            for w in range(RING):
                j = NE - RING + w
                act_expert(j, w, 16 * (j // 2), w < RING - 1)
            act.wait_ge(T["et"], 1)
            over = act.value_load(over_i[0:1, 0:1], min_val=0, max_val=OVER_TILES)
            with act.If(over > 0):
                act.wait_ge(e_out[0], 16 * NE // 2)
                with act.Fori(0, OVER_TILES) as j:
                    act.wait_ge(V["turn"], j + 1)
                    act.activation(xgT[0][:, 0:4, :].rearrange("p a b -> p (a b)"), bank[0][:, :], ACT.Copy)
                    act.activation(xgT[0][:, 4:8, :].rearrange("p a b -> p (a b)"), bank[1][:, :], ACT.Copy).then_inc(V["xe"], 1)
                    act.wait_ge(V["up"], j + 1)
                    act.activation(sil[0], bank[4][:, 0:P], ACT.Silu).then_inc(V["sil"], 1)
                    act.wait_ge(V["dn"], j + 2)
                    act.activation(yo[0][:, 0:512], bank[6][:, :], ACT.Copy)
                    act.activation(yo[0][:, 512:D], bank[7][:, :], ACT.Copy).then_inc(V["ye"], 1)
            for c in range(TILES + 1):
                n = P if c < TILES else DEC
                act.wait_ge(c_done, c + 1)
                dst = O["y_prompt"][0, c * P:(c + 1) * P, :] if c < TILES else O["y_sample"].rearrange("b s d -> (b s) d")
                act.dma_start(dst, c_h[c][0:n, :]).then_inc(c_out, 16)

        def dve_xT(dve, tile, n):
            now(dve, "xm", tile)
            last(dve, "projz", tile)
            for c, b in enumerate((0, 1)):
                ins = dve.tensor_tensor(xT[:, 4 * c:4 * c + 4, 0:n], bank[b][:, 0:4 * n].rearrange("p (k n) -> p k n", k=4),
                                        norm1[:, 4 * c:4 * c + 4].unsqueeze(2).to_broadcast([P, 4, n]), ALU.mult)
            ins.then_inc(S["xT"], 1)

        def dve_front(dve, tile, u, n, x_need):
            now(dve, "qkv", tile)
            dve.tensor_tensor(dt[0:n, 0, :], dt[0:n, 0, :], dt_bias[0:n, :], ALU.add)
            dve.drain()
            dve.tensor_scalar(dt[0:n, 1, :], dt[0:n, 0, :], -1.0, None, ALU.mult)
            dve.drain()
            dve.tensor_tensor(dt[0:n, 1, :], dt[0:n, 0, :], dt[0:n, 1, :], ALU.max).then_inc(S["dtp"], 1)
            last(dve, "ptm qs", tile)
            sq = flat_s[0:n, 0:640].rearrange("p (a b) -> p a b", a=10)
            dve.scalar_tensor_tensor(out=sq, in0=qk[0:n, :, :], scalar=1.0 / HD, in1=qk[0:n, :, :], op0=ALU.mult, op1=ALU.mult)
            dve.drain()
            dve.tensor_reduce(stat[0:n, 1:11], sq, AX.X, ALU.add).then_inc(S["qsq"], 1)
            now(dve, "dl", tile)
            last(dve, "rmm xdt", tile)
            dve.tensor_scalar(dt[0:n, 0, :], dt[0:n, 0, :], 0.0, None, ALU.max)
            dve.drain()
            dve.tensor_tensor(dt[0:n, 3, :], dt[0:n, 0, :], dt[0:n, 2, :], ALU.add)
            dve.drain()
            dve.tensor_tensor(dt[0:n, 4, :], dt[0:n, 3, :], a_neg[0:n, :], ALU.mult).then_inc(S["dta"], 1)
            now(dve, "qs", tile)
            last(dve, "qkt", tile)
            dve.wait_ge(x_in[u], x_need)
            w = flat_s[0:n, 1280:1920].rearrange("p (a b) -> p a b", a=10)
            dve.tensor_tensor(w, qk[0:n, :, :], rstd[0:n, 1:11].unsqueeze(2).to_broadcast([n, 10, HD]), ALU.mult)
            dve.drain()
            dve.tensor_tensor(w[:, 0:8, :], w[:, 0:8, :], qk_norm[0:n, 0:1, :].to_broadcast([n, 8, HD]), ALU.mult)
            dve.tensor_tensor(w[:, 8:10, :], w[:, 8:10, :], qk_norm[0:n, 1:2, :].to_broadcast([n, 2, HD]), ALU.mult)
            dve.drain()
            H2 = HD // 2
            tmp = [flat_s[0:n, 320 * a:320 * a + 320].rearrange("p (a b) -> p a b", a=10) for a in range(4)]
            cos = rope[u][0:n, 0:H2].unsqueeze(1).to_broadcast([n, 10, H2])
            sin = rope[u][0:n, H2:HD].unsqueeze(1).to_broadcast([n, 10, H2])
            dve.tensor_tensor(tmp[0], w[:, :, 0:H2], cos, ALU.mult)
            dve.tensor_tensor(tmp[1], w[:, :, H2:HD], sin, ALU.mult)
            dve.tensor_tensor(tmp[2], w[:, :, H2:HD], cos, ALU.mult)
            dve.tensor_tensor(tmp[3], w[:, :, 0:H2], sin, ALU.mult)
            dve.drain()
            q_out = qkr[0:n, 0:8, :].rearrange("p (r k) d -> p k r d", k=NKV)
            for half, (a, b, op) in enumerate(((0, 1, ALU.subtract), (2, 3, ALU.add))):
                at = slice(half * H2, half * H2 + H2)
                for kv in range(NKV):
                    hs_ = slice(kv * REP, kv * REP + REP)
                    dve.tensor_tensor(q_out[:, kv, :, at], tmp[a][:, hs_, :], tmp[b][:, hs_, :], op)
                ins = dve.tensor_tensor(qkr[0:n, 8:10, at], tmp[a][:, 8:10, :], tmp[b][:, 8:10, :], op)
            ins.then_inc(S["qkr"], 1)

        def dve_residual(dve, tile, u, n):
            now(dve, "wom", tile)
            for c in range(2):
                ins = dve.tensor_tensor(x[u][0:n, 512 * c:512 * c + 512], x[u][0:n, 512 * c:512 * c + 512], bank[4 - c][0:n, :], ALU.add)
            ins.then_inc(S["hres"], 1)

        def dve_norm2(dve, tile, u, n, t_free):
            now(dve, "hs", tile)
            last(dve, "ttm", tile)
            dve.wait_ge(*t_free)
            dve.scalar_tensor_tensor(out=t[0:n, :], in0=x[u][0:n, :], scalar=rstd[0:n, 13:14], in1=norm2[0:n, :],
                                     op0=ALU.mult, op1=ALU.mult).then_inc(S["td"], 1)

        def dve_router(dve, tile, n, slot):
            now(dve, "lgm", tile)
            last(dve, "gex", tile)
            dve.tensor_tensor(lg[0:n, 0:NG], bank[7][0:n, 0:NG], b_route[0:n, 0:NG], ALU.add)
            dve.tensor_tensor(lg[0:n, 8:8 + NE], bank[7][0:n, NG:NG + NE], b_route[0:n, NG:NG + NE], ALU.add)
            dve.drain()
            dve.max(g8[0:n, :], lg[0:n, 0:8])
            dve.drain()
            dve.max_index(gi[0:n, :], g8[0:n, :], lg[0:n, 0:8])
            dve.tensor_scalar(rt[0:n, 0:1], g8[0:n, 0:1], -1.0, None, ALU.mult)
            dve.drain()
            dve.tensor_copy(fi[0:n, 0:1], gi[0:n, 0:1])
            dve.drain()
            dve.tensor_scalar(gmask[0:n, 0, :], con[0:n, C_IOTA:C_IOTA + NG], fi[0:n, 0:1], None, ALU.is_equal)
            dve.drain()
            dve.tensor_scalar(gmask[0:n, 1, :], gmask[0:n, 0, :], 1.0, BIG, ALU.subtract, ALU.mult)
            dve.tensor_tensor(le[0:n, :, :], lg[0:n, 8:8 + NE].rearrange("p (g e) -> p g e", g=NG),
                              gmask[0:n, 0, :].unsqueeze(2).to_broadcast([n, NG, EPG]), ALU.mult)
            dve.drain()
            dve.tensor_tensor(le[0:n, :, :], le[0:n, :, :], gmask[0:n, 1, :].unsqueeze(2).to_broadcast([n, NG, EPG]), ALU.add)
            dve.drain()
            fl = le[0:n, :, :].rearrange("p g e -> p (g e)")
            dve.max(e8[0:n, :], fl)
            dve.drain()
            dve.max_index(ei[0:n, :], e8[0:n, :], fl)
            dve.tensor_scalar(rt[0:n, 2:3], e8[0:n, 0:1], -1.0, None, ALU.mult).then_inc(S["sel"], 1)
            dve.drain()
            dve.tensor_copy(fi[0:n, 2:4], ei[0:n, 0:2])
            dve.drain()
            for k in range(2):
                dve.tensor_scalar(slot("onehot", n)[:, k], con[0:n, C_IOTA:C_IOTA + NE], fi[0:n, 2 + k:3 + k], None, ALU.is_equal)
            dve.drain()
            last(dve, "rankm", tile)
            dve.tensor_tensor(both[0:n, :], slot("onehot", n)[:, 0], slot("onehot", n)[:, 1], ALU.add).then_inc(S["rsel"], 1)

        def dve_rank(dve, tile, n, slot):
            now(dve, "gex", tile)
            dve.tensor_scalar(rt[0:n, 4:5], rt[0:n, 3:4], 1.0, None, ALU.add)
            dve.drain()
            dve.tensor_tensor(rt[0:n, 4:5], rt[0:n, 4:5], rt[0:n, 1:2], ALU.mult)
            dve.drain()
            dve.reciprocal(slot("gate", n)[:, 0:1], rt[0:n, 4:5])
            dve.drain()
            dve.tensor_tensor(slot("gate", n)[:, 1:2], slot("gate", n)[:, 0:1], rt[0:n, 3:4], ALU.mult)
            now(dve, "rankm", tile)
            dve.tensor_copy(rankc[0:n, :], bank[7][0:n, 0:NE])
            dve.tensor_tensor(counted[0:n, :], counted[0:n, :], both[0:n, :], ALU.add)
            dve.drain()
            dve.tensor_tensor(rprod[0:n, :, :], slot("onehot", n), rankc[0:n, :].unsqueeze(1).to_broadcast([n, 2, NE]), ALU.mult)
            dve.drain()
            dve.tensor_reduce(slot("rank", n), rprod[0:n, :, :], AX.X, ALU.add).then_inc(S["rankd"], 1)

        @block.vector
        def _(dve):
            credit(dve, "conva xT dtp qsq dta cum qkr qkc se smax prob ptb convd xdt rmin cbm md yf std yg gt hres td sel rsel rankd")
            dve.memset(v[:, :, :], 0.0)
            dve.memset(kT[:, :, :], 0.0)
            dve.memset(raw[:, :, 0:CK - 1], 0.0)
            dve.memset(hT[:, :, :], 0.0)
            dve.memset(counted[:, :], 0.0)
            dve.memset(onehot[:, TILES], 0.0)
            dve.memset(rank[:, TILES], 0.0)
            dve.memset(q_blk[:, :, :, :], 0.0)
            dve.memset(mask[:, 0, :], -BIG)
            dve.memset(lg[:, :], -BIG)
            dve.drain().then_inc(T["init"], 1)
            dve.wait_ge(first_in, 32)
            dve.tensor_copy(mask[:, 1, :], con[:, C_BAND + P:C_BAND + 2 * P])
            dve_xT(dve, 0, P)
            dve.wait_ge(params, N_PARAMS)
            dve.wait_ge(T["aneg"], 1)
            dve.tensor_scalar(a_neg[:, :], a_neg[:, :], -1.0, None, ALU.mult)
            dve.drain()
            dve_front(dve, 0, 0, P, 32)

            def dve_conv(tile, half):
                now(dve, ("rawa", "rawc")[half], tile)
                last(dve, "xcs ydm", tile)
                cc = range(4 * half, 4 * half + 4)
                for c in cc:
                    dve.tensor_scalar(cv[:, c, :], raw[:, c, 0:P], conv_w[:, c, 0:1], conv_b[:, c:c + 1], ALU.mult, ALU.add)
                for k in range(1, CK):
                    dve.drain()
                    for c in cc:
                        dve.scalar_tensor_tensor(out=cv[:, c, :], in0=raw[:, c, k:k + P], scalar=conv_w[:, c, k:k + 1],
                                                 in1=cv[:, c, :], op0=ALU.mult, op1=ALU.add)
                dve.drain()
                dve.tensor_copy(raw[:, cc[0]:cc[0] + 4, 0:CK - 1], raw[:, cc[0]:cc[0] + 4, P:P + CK - 1]).then_inc(S[("conva", "convd")[half]], 1)

            def dve_keys(tile):
                now(dve, "cumm", tile)
                last(dve, "ecd", tile)
                dve.tensor_copy(cum[:, 0, :], bank[7][:, 0:SH])
                dve.tensor_copy(cum[:, 2, :], bank[7][:, SH:2 * SH])
                dve.drain()
                dve.tensor_tensor(cum[:, 1, :], cum[:, 2, :], cum[:, 0, :], ALU.subtract).then_inc(S["cum"], 1)
                now(dve, "qkt", tile)
                last(dve, "sc3", tile)
                dve.tensor_copy(kT[:, 0, :], kT[:, 1, :])
                dve.drain()
                dve.tensor_copy(kT[:, 1, :], bank[6][:, 0:P])
                dve.tensor_copy(qT[:, :, :].rearrange("p a b -> p (a b)"), bank[2][:, :]).then_inc(S["qkc"], 1)

            dve_conv(0, 0)
            dve_conv(0, 1)
            dve_keys(0)
            dve.wait_ge(loaded, n_loaded[0])

            def dve_tile(tile, u, n_next, x_need, t_free, slot):
                for i, b in enumerate((3, 4, 5, 6)):
                    now(dve, f"sc{i}", tile)
                    ins = dve.scalar_tensor_tensor(
                        out=s[:, 2 * i:2 * i + 2, :], in0=bank[b][:, :].rearrange("p (a b) -> p a b", a=2), scalar=SCALE,
                        in1=mask[:, :, :].rearrange("p a b -> p (a b)").unsqueeze(1).to_broadcast([P, 2, 2 * P]),
                        op0=ALU.mult, op1=ALU.add)
                ins.then_inc(S["se"], 1)
                dve_xT(dve, tile + 1, n_next)
                dve.drain()
                if slot is None:
                    dve.tensor_copy(mask[:, 0, :], con[:, C_BAND:C_BAND + P])
                dve.tensor_reduce(top[:, 0, :], s[:, :, :], AX.X, ALU.max)
                dve.drain()
                dve.tensor_tensor(top[:, 0, :], top[:, 0, :], sink[:, :], ALU.max)
                dve.drain()
                dve.tensor_scalar(top[:, 1, :], top[:, 0, :], -1.0, None, ALU.mult)
                dve.tensor_tensor(top[:, 3, :], sink[:, :], top[:, 0, :], ALU.subtract).then_inc(S["smax"], 1)
                now(dve, "rmm", tile)
                last(dve, "ydm", tile)
                for hh in range(SH):
                    ins = dve.tensor_scalar(m[:, hh, :], bank[5 + hh // 4][:, (hh % 4) * P:(hh % 4 + 1) * P],
                                            cum[:, 0, hh:hh + 1], 0.0, ALU.subtract, ALU.min)
                ins.then_inc(S["rmin"], 1)
                now(dve, "xtk", tile)
                dve.tensor_tensor(cbm[:, :, :], bank[3][:, 2 * P:4 * P].rearrange("p (g l) -> p g l", g=SG),
                                  tri.unsqueeze(1).to_broadcast([P, SG, P]), ALU.mult).then_inc(S["cbm"], 1)
                last(dve, "xde", tile)
                dve.tensor_tensor(xdt[:, :, :], xtok[:, :, :], dt[:, 3, :].unsqueeze(2).to_broadcast([P, SH, SP_]), ALU.mult).then_inc(S["xdt"], 1)
                if slot is not None:
                    dve_router(dve, tile - 1, P, slot)
                now(dve, "pexp", tile)
                dve.tensor_tensor(top[:, 2, :], top[:, 2, :], top[:, 3, :], ALU.add)
                dve.drain()
                dve.reciprocal(top[:, 2, :], top[:, 2, :])
                dve.drain()
                for hh in range(NH):
                    ins = dve.tensor_scalar(s[:, hh, :], s[:, hh, :], top[:, 2, hh:hh + 1], None, ALU.mult)
                ins.then_inc(S["prob"], 1)
                if slot is not None:
                    dve_rank(dve, tile - 1, P, slot)
                now(dve, "rexpd", tile)
                for g in range(SG):
                    ins = dve.tensor_tensor(m[:, 4 * g:4 * g + 4, :], m[:, 4 * g:4 * g + 4, :],
                                            cbm[:, g:g + 1, :].to_broadcast([P, 4, P]), ALU.mult)
                ins.then_inc(S["md"], 1)
                now(dve, "ptm", tile)
                last(dve, "pv", tile)
                dve.tensor_copy(pT[:, 1, 0].rearrange("p a b -> p (a b)"), bank[3][:, :])
                dve.tensor_copy(pT[:, 1, 1].rearrange("p a b -> p (a b)"), bank[7][:, :]).then_inc(S["ptb"], 1)
                now(dve, "ydm ecd xd z", tile)
                fy = y[:, :, :].rearrange("p a b -> p (a b)")
                dve.tensor_tensor(y[:, :, :], bank[6][:, :].rearrange("p (a b) -> p a b", a=SH),
                                  ecum[:, 0, :].unsqueeze(2).to_broadcast([P, SH, SP_]), ALU.mult)
                dve.drain()
                dve.tensor_tensor(fy, fy, bank[5][:, :], ALU.add)
                dve.drain()
                dve.tensor_tensor(y[:, :, :], y[:, :, :], xd[:, :, :], ALU.add)
                dve.drain()
                dve.tensor_tensor(fy, fy, zs[:, :], ALU.mult).then_inc(S["yf"], 1)
                dve.tensor_tensor(hT[:, :, :], hT[:, :, :], ecum[:, 2, :].unsqueeze(2).to_broadcast([P, SH, SP_]), ALU.mult)
                dve.drain()
                now(dve, "stm", tile)
                dve.tensor_tensor(hT[:, :, :].rearrange("p a b -> p (a b)"), hT[:, :, :].rearrange("p a b -> p (a b)"),
                                  bank[2][:, :], ALU.add).then_inc(S["std"], 1)
                now(dve, "ys", tile)
                for g in range(SG):
                    ins = dve.tensor_scalar(y[:, 4 * g:4 * g + 4, :], y[:, 4 * g:4 * g + 4, :], rstd[:, 11 + g:12 + g], None, ALU.mult)
                ins.then_inc(S["yg"], 1)
                now(dve, "ytm", tile)
                last(dve, "wom", tile)
                dve.tensor_tensor(gT[:, :, :], bank[3][:, :].rearrange("p (c n) -> p c n", c=4),
                                  ssm_norm[:, :].unsqueeze(2).to_broadcast([P, 4, P]), ALU.mult).then_inc(S["gt"], 1)

                if n_next == DEC:
                    dve.wait_ge(kv_out, 16)
                dve_front(dve, tile + 1, 1 - u, n_next, x_need)
                if n_next == P:
                    dve_conv(tile + 1, 0)
                dve_residual(dve, tile, u, P)
                if n_next == P:
                    dve_keys(tile + 1)
                dve_norm2(dve, tile, u, P, t_free)
                if n_next == P:
                    dve_conv(tile + 1, 1)

            routed = {"onehot": onehot, "rank": rank, "gate": gate}
            dve_tile(0, 0, P, 32, (t_out[1], 16), None)
            with dve.Fori(0, TILES // 2 - 1) as pair:
                t0 = pair * 2
                for u in range(2):
                    dve_tile(t0 + (u + 1), 1 - u, P, 32 * pair + 64, (t_out[u], 16 * pair + 32),
                             lambda name, n: routed[name][0:n, bass.ds(t0 + u, 1)].squeeze(1))
            dve_tile(TILES - 1, 1, DEC, 16 * TILES + 32, (t_out[0], 8 * TILES + 16), lambda name, n: routed[name][0:n, TILES - 2])
            last_slot = lambda name, n: routed[name][0:n, TILES - 1]
            dve_router(dve, TILES - 1, P, last_slot)
            dve_rank(dve, TILES - 1, P, last_slot)

            dve.drain()
            dve.tensor_copy(dt[0:DEC, 1, :], dt[0:DEC, 3, :]).then_inc(T["dt"], 1)
            dve.wait_ge(T["q"], 1)
            for b in range(DEC):
                for kv in range(NKV):
                    r = slice(kv * HD, kv * HD + HD)
                    ins = dve.tensor_copy(q_blk[r, b, kv, :], bank[7][r, 0:REP * DEC].rearrange("p (r b) -> p r b", b=DEC)[:, :, b])
            ins.then_inc(T["q"], 1)
            dve.wait_ge(T["kT"], 1)
            for c in range(2):
                ins = dve.tensor_copy(keysT[:, 4 * c:4 * c + 4, :].rearrange("p a b -> p (a b)"), bank[5 + c][:, :])
            ins.then_inc(T["kT"], 1)
            dve.wait_ge(state_in, 16 * 11)
            now(dve, "rawc", TILES)
            dve.tensor_tensor(st_acc, st_raw, st_w[:, CK - 1, :], ALU.mult)
            dve.drain()
            dve.tensor_tensor(st_acc, st_acc, st_b, ALU.add)
            for k in range(CK - 1):
                dve.tensor_tensor(st_tmp, st_conv[:, k, :], st_w[:, k, :], ALU.mult)
                dve.drain()
                dve.tensor_tensor(st_acc, st_acc, st_tmp, ALU.add)
                dve.drain()
            dve.drain().then_inc(T["cv"], 1)
            dve.wait_ge(T["att"], 1)
            for c in range(2):
                dve.tensor_scalar(ps[:, 4 * c:4 * c + 4, :].rearrange("p a b -> p (a b)"), bank[c][0:NH, :], SCALE, None, ALU.mult)
            dve.drain()
            dve.tensor_reduce(m_top[:, 0, :], ps, AX.X, ALU.max)
            dve.drain()
            dve.tensor_scalar(m_top[:, 0, :], m_top[:, 0, :], sink_col[:, 0:1], None, ALU.max)
            dve.drain()
            dve.tensor_tensor(ps, ps, m_top[:, 0, :].unsqueeze(2).to_broadcast([NH, DEC, P]), ALU.subtract)
            dve.tensor_scalar(m_top[:, 3, :], m_top[:, 0, :], -1.0, sink_col[:, 0:1], ALU.mult, ALU.add)
            dve.drain().then_inc(T["att"], 1)
            dve.wait_ge(T["att"], 3)
            dve.tensor_reduce(m_top[:, 2, :], ps, AX.X, ALU.add)
            dve.drain()
            dve.tensor_tensor(m_top[:, 2, :], m_top[:, 2, :], m_top[:, 3, :], ALU.add)
            dve.drain()
            dve.reciprocal(m_top[:, 2, :], m_top[:, 2, :])
            dve.drain()
            dve.tensor_tensor(ps, ps, m_top[:, 2, :].unsqueeze(2).to_broadcast([NH, DEC, P]), ALU.mult)
            dve.drain().then_inc(T["att"], 1)
            dve.wait_ge(T["att"], 5)
            dve.tensor_copy(ps_T[:, :, :].rearrange("p b h -> p (b h)"), bank[2][:, 0:DEC * NH]).then_inc(T["att"], 1)
            dve.wait_ge(T["att"], 7)
            for kv in range(NKV):
                r = slice(kv * HD, kv * HD + HD)
                ins = dve.tensor_copy(aT[r, :, 0:DEC], bank[3][r, 0:DEC * NH].rearrange("p (b k r) -> p k r b", b=DEC, k=NKV)[:, kv])
            ins.then_inc(T["att"], 1)
            dve.wait_ge(T["dt"], 3)
            dve.tensor_copy(st_da[:, 0:2 * DEC], bank[6][0:SH, 0:2 * DEC])
            dve.tensor_copy(st_da[:, 2 * DEC:], d_col[:, :])
            dve.tensor_copy(head_sel.rearrange("p (h d) -> p h d", h=SH), ident[0:SH, 0:SH].unsqueeze(2).to_broadcast([SH, SH, SP_]))
            dve.drain().then_inc(T["xz"], 1)
            dve.wait_ge(T["xz"], 2)
            dve.tensor_copy(st_sc[:, :, :], bank[7][:, 0:4 * (2 * DEC + 1)].rearrange("p (c n) -> p c n", c=4))
            dve.tensor_copy(st_xT[:, :, :], bank[4][:, 0:4 * DEC].rearrange("p (c n) -> p c n", c=4))
            dve.tensor_copy(st_zT[:, :, :], bank[4][:, 4 * DEC:8 * DEC].rearrange("p (c n) -> p c n", c=4))
            dve.drain()
            dve.tensor_tensor(st_dx[:, :, :], st_xT[:, :, :], st_sc[:, :, 0:DEC], ALU.mult).then_inc(T["dx"], 1)
            dve.wait_ge(T["ssmT"], 1)
            dve.tensor_copy(st_turned, bank[5][:, :].rearrange("p (c n) -> p c n", c=4)).then_inc(T["ssmC"], 1)
            for b in range(DEC):
                dve.wait_ge(T["bx"], b + 1)
                for c in range(4):
                    dve.scalar_tensor_tensor(out=st_h[:, b, c, :], in0=st_h[:, b, c, :], scalar=st_sc[:, c, DEC + b:DEC + b + 1],
                                             in1=st_bx[b % 2][:, c, :], op0=ALU.mult, op1=ALU.add)
                dve.drain()
                cb = bank[b % 2][:, 2 * P:4 * P].rearrange("p (g n) -> p g n", g=SG)
                for g in range(SG):
                    dve.tensor_tensor(st_ch[:, 2 * g:2 * g + 2, :], st_h[:, b, 2 * g:2 * g + 2, :], cb[:, g:g + 1, :].to_broadcast([P, 2, P]), ALU.mult)
                dve.drain()
                dve.tensor_reduce(st_y[:, :, b], st_ch, AX.X, ALU.add)
                dve.drain().then_inc(T["hst"], 1)
            dve.tensor_tensor(st_g2[:, :, :], st_xT[:, :, :], st_sc[:, :, 2 * DEC:].to_broadcast([P, 4, DEC]), ALU.mult)
            dve.drain()
            dve.tensor_tensor(st_y[:, :, :], st_y[:, :, :], st_g2[:, :, :], ALU.add)
            dve.drain()
            dve.tensor_tensor(st_y[:, :, :], st_y[:, :, :], st_zT[:, :, :], ALU.mult)
            dve.drain()
            dve.tensor_tensor(st_g2[:, :, :], st_y[:, :, :], st_y[:, :, :], ALU.mult)
            dve.drain().then_inc(T["norm"], 1)
            dve.wait_ge(T["norm"], 2)
            dve.tensor_copy(st_g2[:, :, :].rearrange("p a b -> p (a b)"), bank[6][:, 0:4 * DEC])
            dve.drain()
            for g in range(SG):
                ins = dve.tensor_tensor(st_n[:, g, :], st_g2[:, 2 * g, :], st_g2[:, 2 * g + 1, :], ALU.add)
            ins.then_inc(T["norm"], 1)
            dve.wait_ge(T["norm"], 4)
            for g in range(SG):
                dve.tensor_tensor(st_y[:, 2 * g:2 * g + 2, :], st_y[:, 2 * g:2 * g + 2, :], st_r[:, g:g + 1, :].to_broadcast([P, 2, DEC]), ALU.mult)
            dve.drain()
            dve.tensor_tensor(gT[:, :, 0:DEC], st_y[:, :, :], ssm_norm[:, :].unsqueeze(2).to_broadcast([P, 4, DEC]), ALU.mult).then_inc(T["norm"], 1)
            dve_residual(dve, TILES, 0, DEC)
            dve_norm2(dve, TILES, 0, DEC, (t_out[1], 8 * TILES + 16))
            sample_slot = lambda name, n: routed[name][0:n, TILES]
            dve_router(dve, TILES, DEC, sample_slot)
            dve_rank(dve, TILES, DEC, sample_slot)

            def turned_choices(done, sel, table, at, n):
                for a in range(3):
                    dve.tensor_tensor(sel[a], con[:, C_IOTA:C_IOTA + P].unsqueeze(1).to_broadcast([P, THIRD, P]),
                                      table[:, a * THIRD:(a + 1) * THIRD].unsqueeze(2).to_broadcast([P, THIRD, P]), ALU.is_equal).then_inc(T[done], 1)
                dve.wait_ge(T[done], 4)
                dve.tensor_scalar(slot_f[:, 0, 0:n], bank[1][:, 0:n], float(EMPTY), None, ALU.add)
                dve.drain()
                dve.tensor_scalar(slot_f[:, 1, 0:n], slot_f[:, 0, 0:n], float(TOKENS), -float(TOKENS), ALU.is_ge, ALU.mult)
                dve.tensor_copy(slot_tab[:, at:at + n, 1], slot_f[:, 0, 0:n])
                dve.drain()
                dve.tensor_tensor(slot_tab[:, at:at + n, 0], slot_f[:, 0, 0:n], slot_f[:, 1, 0:n], ALU.add)

            dve.wait_ge(outs, N_OUTS)
            dve.drain().then_inc(T["cnt"], 1)
            dve.tensor_tensor(chosen, flat_onehot, con[:, C_CHOICE:C_CHOICE + PAIRS].unsqueeze(2).to_broadcast([P, PAIRS, NE]), ALU.mult)
            turned_choices("slots", row_sel, flat_rank, 0, NE)
            dve.drain().then_inc(T["slots"], 1)
            dve.wait_ge(T["cnt"], 2)
            dve.tensor_copy(nt[:, 0, :], bank[0][:, 0:NE])
            dve.drain()
            dve.tensor_scalar(nt[:, 1, :], nt[:, 0, :], float(ROWS), None, ALU.is_gt)
            dve.drain()
            for j in range(2, (TOKENS + ROWS - 1) // ROWS):
                dve.scalar_tensor_tensor(out=nt[:, 1, :], in0=nt[:, 0, :], scalar=float(ROWS * j), in1=nt[:, 1, :], op0=ALU.is_gt, op1=ALU.add)
                dve.drain()
            dve.tensor_tensor_scan(nt[:, 2, :], con[:, C_ONES:C_ONES + NE], nt[:, 1, :], 0.0, ALU.mult, ALU.add)
            dve.drain()
            dve.tensor_copy(over_i[:, :], nt[0:1, 2, NE - 1:NE])
            dve.tensor_tensor(nt[:, 3, :], nt[:, 2, :], nt[:, 1, :], ALU.subtract)
            dve.tensor_tensor(ecmp, nt[0:1, 2:3, :].to_broadcast([1, OVER_TILES, NE]),
                              con[0:1, C_IOTA:C_IOTA + OVER_TILES].unsqueeze(2).to_broadcast([1, OVER_TILES, NE]), ALU.is_le)
            dve.drain()
            dve.tensor_reduce(etile, ecmp, AX.X, ALU.add)
            dve.drain()
            dve.tensor_scalar(etile, etile, float(NE - 1), None, ALU.min)
            dve.drain()
            dve.tensor_copy(etile_i[:, :], etile)
            dve.drain().then_inc(T["et"], 1)

            dve.sem_inc(E_["yd"], 1)
            dve.wait_ge(outs, N_OUTS)

            def dve_turned(j, w):
                dve.wait_ge(E_["turn"], j + 1)
                dve.tensor_copy(xgT[w % 2][:, 4:8, :].rearrange("p a b -> p (a b)"), bank[w % 2 * 2 + 1][:, :]).then_inc(E_["xd"], 1)

            def dve_expert(j, w, stored, more=True):
                u = w % 2
                dve.wait_ge(E_["sil"], j + 1)
                dve.tensor_tensor(hidT[u], sil[u], bank[4 + u][:, P:2 * P], ALU.mult).then_inc(E_["hid"], 1)
                if more:
                    dve_turned(j + 1, (w + 1) % RING)
                dve.wait_ge(E_["dn"], j + 2)
                if stored is not None:
                    dve.wait_ge(e_out[u], stored)
                dve.tensor_copy(yo[u][:, 512:D], bank[7][:, :]).then_inc(E_["yd"], 1)

            dve_turned(0, 0)
            for w in range(RING):
                dve_expert(w, w, 16 * (w // 2) if w >= 2 else None)
            with dve.Fori(1, NE // RING - 1) as group:
                for w in range(RING):
                    dve_expert(RING * group + w, w, 32 * group + 16 * (w // 2))
            for w in range(RING):
                j = NE - RING + w
                dve_expert(j, w, 16 * (j // 2), w < RING - 1)
            over = dve.value_load(over_i[0:1, 0:1], min_val=0, max_val=OVER_TILES)
            with dve.If(over > 0):
                dve.tensor_scalar(quo[:, 0, :], flat_rank, float(ROWS), None, ALU.is_ge)
                dve.drain()
                dve.tensor_tensor(quo[:, 3, :], quo[:, 0, :], con[:, C_CHOICE:C_CHOICE + PAIRS], ALU.mult)
                for j in range(2, (TOKENS + ROWS - 1) // ROWS):
                    dve.scalar_tensor_tensor(out=quo[:, 0, :], in0=flat_rank, scalar=float(ROWS * j), in1=quo[:, 0, :], op0=ALU.is_ge, op1=ALU.add)
                    dve.drain()
                dve.scalar_tensor_tensor(out=quo[:, 1, :], in0=quo[:, 0, :], scalar=-float(ROWS), in1=flat_rank, op0=ALU.mult, op1=ALU.add)
                dve.tensor_tensor(pair_prod, flat_onehot, nt[:, 3:4, :].to_broadcast([P, PAIRS, NE]), ALU.mult)
                dve.drain()
                dve.tensor_reduce(quo[:, 2, :], pair_prod, AX.X, ALU.add)
                dve.drain()
                dve.scalar_tensor_tensor(out=quo[:, 2, :], in0=quo[:, 0, :], scalar=-1.0, in1=quo[:, 2, :], op0=ALU.add, op1=ALU.add)
                dve.drain()
                over_chosen = pair_prod[:, :, 0:OVER_TILES]
                dve.tensor_tensor(over_chosen, con[:, C_IOTA:C_IOTA + OVER_TILES].unsqueeze(1).to_broadcast([P, PAIRS, OVER_TILES]),
                                  quo[:, 2, :].unsqueeze(2).to_broadcast([P, PAIRS, OVER_TILES]), ALU.is_equal)
                dve.drain()
                dve.tensor_tensor(over_chosen, over_chosen, quo[:, 3, :].unsqueeze(2).to_broadcast([P, PAIRS, OVER_TILES]), ALU.mult)
                turned_choices("over", over_sel, quo[:, 1, :], NE, OVER_TILES)
                dve.drain().then_inc(T["over"], 1)
                with dve.Fori(0, OVER_TILES) as j:
                    dve.wait_ge(V["sil"], j + 1)
                    dve.tensor_tensor(hidT[0], sil[0], bank[4][:, P:2 * P], ALU.mult).then_inc(V["hid"], 1)

            dve.wait_ge(c_in, 16 * TILES)
            for c in range(TILES + 1):
                n, w = (P if c < TILES else DEC), c % 4
                dve.wait_ge(c_in1[w], 32 * (c // 4 + 1))
                for k in range(2):
                    ins = dve.scalar_tensor_tensor(out=c_h[c][0:n, :], in0=c_y[w][k][0:n, :], scalar=gate[0:n, c, k:k + 1], in1=c_h[c][0:n, :],
                                                   op0=ALU.mult, op1=ALU.add)
                    if k == 0:
                        dve.drain()
                ins.then_inc(c_done, 1)

        def root_mean(pool, col, count, n, done):
            pool.tensor_tensor(stat[0:n, col:col + count], stat[0:n, col:col + count], eps[0:n, 0:count], ALU.add)
            pool.drain()
            pool.tensor_tensor(rstd[0:n, col:col + count], stat[0:n, col:col + count], neg_half[0:n, 0:count], ALU.pow).then_inc(S[done], 1)

        @block.gpsimd
        def _(pool):
            credit(pool, "xs qs xde xd ys hs")
            pool.memset(neg_half[:, :], -0.5)
            pool.memset(eps[:, :], EPS)
            pool.drain()

            def pool_rows(tile, n):
                now(pool, "ssq", tile)
                last(pool, "xn", tile)
                root_mean(pool, 0, 1, n, "xs")

            def pool_qk(tile, n):
                now(pool, "qsq", tile)
                last(pool, "qkr", tile)
                root_mean(pool, 1, 10, n, "qs")

            def pool_h(tile, n):
                now(pool, "hsq", tile)
                last(pool, "td", tile)
                root_mean(pool, 13, 1, n, "hs")

            def pool_tile(tile, n_next):
                pool_rows(tile + 1, n_next)
                now(pool, "xtk", tile)
                last(pool, "yf", tile)
                pool.tensor_tensor(xd[:, :, :], xtok[:, :, :], d_skip[:, :].unsqueeze(2).to_broadcast([P, SH, SP_]), ALU.mult).then_inc(S["xd"], 1)
                now(pool, "xdt ecd", tile)
                last(pool, "stm", tile)
                pool.tensor_tensor(xde[:, :, :], xdt[:, :, :], ecum[:, 1, :].unsqueeze(2).to_broadcast([P, SH, SP_]), ALU.mult).then_inc(S["xde"], 1)
                now(pool, "ysq", tile)
                last(pool, "yg", tile)
                root_mean(pool, 11, 2, P, "ys")
                pool_qk(tile + 1, n_next)
                pool_h(tile, P)

            pool_rows(0, P)
            pool_qk(0, P)
            pool.wait_ge(params, N_PARAMS)
            pool_tile(0, P)
            with pool.Fori(0, TILES // 2 - 1) as pair:
                for u in range(2):
                    pool_tile(pair * 2 + (u + 1), P)
            pool_tile(TILES - 1, DEC)
            pool.wait_ge(T["norm"], 3)
            pool.tensor_scalar(st_n[:, :, :], st_n[:, :, :], 1.0 / 256, EPS, ALU.mult, ALU.add)
            pool.drain()
            pool.tensor_tensor(st_r[:, :, :].rearrange("p a b -> p (a b)"), st_n[:, :, :].rearrange("p a b -> p (a b)"), neg_half[:, 0:SG * DEC], ALU.pow).then_inc(T["norm"], 1)
            pool_h(TILES, DEC)

            def fetch_index(idx, j, which):
                return pool.tensor_copy(idx[:, :], slot_tab[:, bass.ds(j, 1), which])

            def gather(into, idx, landed):
                pool.indirect_dma_start(into, None, t_dram, bass.IndirectOffsetOnAxis(ap=idx[:, :].bitcast(U32), axis=0),
                                        bounds_check=TOKENS - 1, oob_is_err=False).then_inc(landed, 16)

            def scatter(out, idx, landed):
                pool.indirect_dma_start(y_dram, bass.IndirectOffsetOnAxis(ap=idx[:, :].bitcast(U32), axis=0), out, None,
                                        bounds_check=CHOICES - 1, oob_is_err=False).then_inc(landed, 16)

            def pool_expert(j, w, left=NE):
                pool.wait_ge(E_["ya"], j + 2)
                pool.wait_ge(E_["yd"], j + 2)
                pool.wait_ge(E_["idx"], j + 1)
                if left > 1:
                    ins = fetch_index(idx_out[(w + 1) % RING], j + 1, 1)
                if left > RING:
                    ins = fetch_index(idx_in[w], j + RING, 0)
                if left > 1:
                    ins.then_inc(E_["idx"], 1)
                scatter(yo[w % 2], idx_out[w], e_out[w % 2])
                if left >= RING:
                    gather(xg[(w + RING - 1) % RING], idx_in[(w + RING - 1) % RING], e_x[(w + RING - 1) % RING])

            pool.wait_ge(T["slots"], 5)
            for w in range(RING):
                fetch_index(idx_in[w], w, 0)
            fetch_index(idx_out[0], 0, 1)
            pool.drain().then_inc(E_["idx"], 1)
            for u in range(2):
                pool.wait_ge(t_out[u], 16 + 16 * ((TILES + 2 - u) // 2))
                pool.wait_ge(h_out[u], 16 + 16 * ((TILES + 2 - u) // 2))
            pool.wait_ge(outs, N_OUTS)
            for w in range(RING - 1):
                gather(xg[w], idx_in[w], e_x[w])
            for w in range(RING):
                pool_expert(w, w)
            with pool.Fori(1, NE // RING - 1) as group:
                for w in range(RING):
                    pool_expert(RING * group + w, w)
            for w in range(RING):
                pool_expert(NE - RING + w, w, RING - w)
            pool.wait_ge(T["et"], 1)
            over = pool.value_load(over_i[0:1, 0:1], min_val=0, max_val=OVER_TILES)
            with pool.If(over > 0):
                pool.wait_ge(T["over"], 5)
                for u in range(2):
                    pool.wait_ge(e_out[u], 16 * NE // 2)
                with pool.Fori(0, OVER_TILES) as j:
                    pool.wait_ge(V["dn"], j + 1)
                    fetch_index(idx_in[0], j + NE, 0)
                    pool.drain()
                    gather(xg[0], idx_in[0], o_x)
                    pool.wait_ge(V["ye"], j + 2)
                    fetch_index(idx_out[0], j + NE, 1)
                    pool.drain()
                    scatter(yo[0], idx_out[0], o_out)
                    pool.wait_ge(o_out, 16 * j + 16)

        def pe_turn_x(pe, src, ids, n, banks, done):
            for k in range(KC):
                cols = src.rearrange("t (p k) -> t k p", k=KC)[:, k, :]
                ins = pe.transpose(bank[banks[k // 4]][:, (k % 4) * n:(k % 4 + 1) * n], cols, ids)
            ins.then_inc(done, 1)

        def pe_rows(pe, tile, n):
            now(pe, "xn", tile)
            last(pe, "rawc z", tile)
            pe_turn_x(pe, xn[0:n, :], ident[0:n, 0:n], n, (0, 1), S["xm"])

        def project(pe, out, n, cols, landed=()):
            for one in landed:
                pe.wait_ge(one, 16)
            for k in range(KC):
                ins = pe.matmul(out, xT[:, k, 0:n], w_in[:, k, cols], start=k == 0, stop=k == KC - 1)
            return ins

        def pe_q(pe, tile, n, landed=()):
            now(pe, "xT", tile)
            project(pe, bank[0][0:n, :], n, slice(0, Q_END), landed).then_inc(S["projq"], 1)

        def pe_kv(pe, tile, n, landed=()):
            project(pe, bank[1][0:n, 0:256], n, slice(Q_END, V_END))
            project(pe, bank[1][0:n, 256:256 + SH], n, slice(XBC_END, IN_DIM), landed).then_inc(S["projk"], 1)

        def pe_xbc(pe, tile, n, half):
            now(pe, ("qe", "qkv")[half], tile)
            if n == P:
                for c in range(4):
                    at = Z_END + (4 * half + c) * P
                    for k in range(KC):
                        ins = pe.matmul(bank[half][:, c * P:(c + 1) * P], w_in[:, k, at:at + P], xT[:, k, :], start=k == 0, stop=k == KC - 1)
            else:
                at = Z_END + 512 * half
                ins = project(pe, bank[half][0:n, :], n, slice(at, at + 512))
            ins.then_inc(S[("proja", "projc")[half]], 1)

        def pe_z(pe, tile, n, landed=()):
            now(pe, "rawa", tile)
            project(pe, bank[0][0:n, :], n, slice(V_END, Z_END), landed).then_inc(S["projz"], 1)

        def pe_out(pe, tile, n):
            for c in range(2):
                for k in range(KC):
                    lhs = aT[:, k, 0:n] if k < REP else gT[:, k - REP, 0:n]
                    ins = pe.matmul(bank[4 - c][0:n, :], lhs, w_out[:, k, 512 * c:512 * c + 512], start=k == 0, stop=k == KC - 1)
            ins.then_inc(S["wom"], 1)

        def pe_turn_t(pe, tile, n):
            now(pe, "td", tile)
            pe_turn_x(pe, t[0:n, :], ident[0:n, 0:n], n, (5, 6), S["ttm"])

        def pe_router(pe, tile, n):
            now(pe, "tt", tile)
            for k in range(KC):
                ins = pe.matmul(bank[7][0:n, 0:NG + NE], tT[:, k, 0:n], w_route[:, k, :], start=k == 0, stop=k == KC - 1)
            ins.then_inc(S["lgm"], 1)

        def pe_rank(pe, tile, n):
            now(pe, "rsel", tile)
            pe.matmul(bank[7][0:n, 0:NE], strict[0:n, 0:n], both[0:n, :], start=True, stop=False)
            pe.matmul(bank[7][0:n, 0:NE], ones[:, 0:n], counted[:, :], start=False, stop=True).then_inc(S["rankm"], 1)

        @block.tensor
        def _(pe):
            credit(pe, "xm projq projk projz proja projc cumm qkt sc0 sc1 sc2 sc3 ptm pv xtm rmm ydm stm ytm wom ttm lgm rankm")
            pe.wait_ge(first_in, 32)
            pe_rows(pe, 0, P)
            pe_q(pe, 0, P, (w_q,))
            pe_kv(pe, 0, P, (w_x,))
            pe_xbc(pe, 0, P, 0)
            pe_xbc(pe, 0, P, 1)

            def pe_keys(tile):
                now(pe, "dta", tile)
                pe.matmul(bank[7][:, 0:SH], tri, dt[:, 4, :], start=True, stop=True)
                pe.matmul(bank[7][:, SH:2 * SH], ones, dt[:, 4, :], start=True, stop=True).then_inc(S["cumm"], 1)
                now(pe, "qkr", tile)
                for r in range(REP):
                    pe.transpose(bank[2][:, r * P:(r + 1) * P], qkr[:, 2 * r:2 * r + 2, :].rearrange("p a b -> p (a b)"), ident)
                pe.transpose(bank[6][:, 0:P], qkr[:, 8:10, :].rearrange("p a b -> p (a b)"), ident).then_inc(S["qkt"], 1)

            pe_keys(0)
            pe_z(pe, 0, P, (w_z,))
            pe.wait_ge(loaded, n_loaded[0])
            pe.wait_ge(T["init"], 1)

            def pe_tile(tile, n_next, first=False):
                nxt = tile + 1
                now(pe, "qkc", tile)
                last(pe, "hres", tile)
                for i, b in enumerate((3, 4, 5, 6)):
                    if i == 2 and not first:
                        now(pe, "tt", tile - 1)
                    for j in range(2):
                        kv, r = (2 * i + j) // REP, (2 * i + j) % REP
                        rr = slice(kv * HD, kv * HD + HD)
                        ins = pe.matmul(bank[b][:, j * 256:(j + 1) * 256], qT[rr, r, :], kT[rr, :, :].rearrange("p a b -> p (a b)"),
                                        start=True, stop=True)
                    ins.then_inc(S[f"sc{i}"], 1)
                if not first:
                    pe_router(pe, tile - 1, P)
                pe_rows(pe, nxt, n_next)
                now(pe, "xcs se", tile)
                for g in range(SG):
                    pe.matmul(bank[3][:, (2 + g) * P:(3 + g) * P], xc[:, 4 + g, :], xc[:, 6 + g, :], start=True, stop=True)
                for c in (4, 5, 0, 1, 2, 3):
                    ins = pe.transpose(bank[2 + c // 4][:, (c % 4) * P:(c % 4 + 1) * P], xc[:, c, :], ident)
                ins.then_inc(S["xtm"], 1)
                for hh in range(SH):
                    ins = pe.matmul(bank[5 + hh // 4][:, (hh % 4) * P:(hh % 4 + 1) * P], dt[:, 4, hh:hh + 1].to_broadcast([P, P]), tri,
                                    start=True, stop=True)
                ins.then_inc(S["rmm"], 1)
                pe_q(pe, nxt, n_next)
                pe_kv(pe, nxt, n_next)
                if not first:
                    pe_rank(pe, tile - 1, P)
                now(pe, "prob xtk cbm", tile)
                for kv in range(NKV):
                    for blk in range(2):
                        if kv == 1 and blk == 1 and not first:
                            now(pe, "rankd", tile - 1)
                        for r in range(REP):
                            ins = pe.transpose(bank[(4, 2, 3, 7)[kv * 2 + blk]][:, r * P:(r + 1) * P], s[:, kv * REP + r, blk * P:(blk + 1) * P], ident)
                ins.then_inc(S["ptm"], 1)
                now(pe, "md xdt rmin", tile)
                last(pe, "std", tile)
                for hh in range(SH):
                    pe.matmul(bank[5][:, hh * SP_:(hh + 1) * SP_], m[:, hh, :], xdt[:, hh, :], start=True, stop=True)
                for g in range(SG):
                    ins = pe.matmul(bank[6][:, g * 256:(g + 1) * 256], xc[:, 6 + g, :], hT[:, 4 * g:4 * g + 4, :].rearrange("p a b -> p (a b)"),
                                    start=True, stop=True)
                ins.then_inc(S["ydm"], 1)
                now(pe, "pta ptb vc", tile)
                for kv in range(NKV):
                    for blk in range(2):
                        ins = pe.matmul(bank[4][kv * HD:(kv + 1) * HD, :], v[:, blk, kv * HD:(kv + 1) * HD],
                                        pT[:, kv, blk].rearrange("p a b -> p (a b)"), start=blk == 0, stop=blk == 1)
                ins.then_inc(S["pv"], 1)
                now(pe, "xde", tile)
                for g in range(SG):
                    ins = pe.matmul(bank[2][:, g * 256:(g + 1) * 256], btok[:, g, :], xde[:, 4 * g:4 * g + 4, :].rearrange("p a b -> p (a b)"),
                                    start=True, stop=True)
                ins.then_inc(S["stm"], 1)
                pe_xbc(pe, nxt, n_next, 0)
                now(pe, "yg", tile)
                for c in range(4):
                    ins = pe.transpose(bank[3][:, c * P:(c + 1) * P], y[:, 2 * c:2 * c + 2, :].rearrange("p a b -> p (a b)"), ident)
                ins.then_inc(S["ytm"], 1)
                pe_xbc(pe, nxt, n_next, 1)
                now(pe, "at gt std", tile)
                pe_out(pe, tile, P)
                if n_next == P:
                    pe_keys(nxt)
                pe_z(pe, nxt, n_next)
                if n_next == P:
                    now(pe, "qkc", nxt)
                pe_turn_t(pe, tile, P)

            pe_tile(0, P, first=True)
            with pe.Fori(0, TILES // 2 - 1) as pair:
                for u in range(2):
                    pe_tile(pair * 2 + (u + 1), P)
            pe_tile(TILES - 1, DEC)
            pe_router(pe, TILES - 1, P)
            pe_rank(pe, TILES - 1, P)
            i8 = ident[0:DEC, 0:DEC]
            now(pe, "qkr", TILES)
            last(pe, "rankd", TILES)
            for r in range(REP):
                ins = pe.transpose(bank[7][:, r * DEC:(r + 1) * DEC], qkr[0:DEC, 2 * r:2 * r + 2, :].rearrange("p a b -> p (a b)"), i8)
            ins.then_inc(T["q"], 1)
            pe.wait_ge(cache_in, 64)
            for b in range(DEC):
                ins = pe.transpose(bank[5 + b // 4][:, (b % 4) * P:(b % 4 + 1) * P], keys[:, b, :], ident)
            ins.then_inc(T["kT"], 1)
            pe.wait_ge(T["q"], 2)
            pe.wait_ge(T["kT"], 2)
            now(pe, "qkv", TILES)
            for b in range(DEC):
                ins = pe.matmul(bank[b // 4][0:NH, (b % 4) * P:(b % 4 + 1) * P], q_blk[:, b].rearrange("p k r -> p (k r)"), keysT[:, b, :],
                                start=True, stop=True)
            ins.then_inc(T["att"], 1)
            last(pe, "std", TILES)
            for c in range(4):
                ins = pe.transpose(bank[5][:, c * P:(c + 1) * P], hT[:, 2 * c:2 * c + 2, :].rearrange("p a b -> p (a b)"), ident)
            ins.then_inc(T["ssmT"], 1)
            pe.wait_ge(T["dt"], 2)
            now(pe, "z", TILES)
            pe.transpose(bank[6][0:SH, 0:DEC], dt[0:DEC, 3, :], i8)
            pe.transpose(bank[6][0:SH, DEC:2 * DEC], dt[0:DEC, 4, :], i8).then_inc(T["dt"], 1)
            pe.wait_ge(T["cv"], 2)
            pe.wait_ge(T["att"], 4)
            for b in range(DEC):
                ins = pe.transpose(bank[2][:, b * NH:(b + 1) * NH], ps[:, b, :], i8)
            ins.then_inc(T["att"], 1)
            pe.wait_ge(T["att"], 6)
            now(pe, "rawc", TILES)
            for b in range(DEC):
                ins = pe.matmul(bank[3][:, b * NH:(b + 1) * NH], vals[:, b, :], ps_T[:, b, :], start=True, stop=True)
            ins.then_inc(T["att"], 1)
            for c in range(4):
                pe.transpose(bank[4][:, c * DEC:(c + 1) * DEC], st_xc[:, c * P:(c + 1) * P], i8)
            for c in range(4):
                pe.transpose(bank[4][:, (4 + c) * DEC:(5 + c) * DEC], zs[0:DEC, c * P:(c + 1) * P], i8)
            pe.wait_ge(T["xz"], 1)
            for c in range(4):
                ins = pe.matmul(bank[7][:, c * (2 * DEC + 1):(c + 1) * (2 * DEC + 1)],
                                head_sel[:, c * P:(c + 1) * P], st_da[:, :], start=True, stop=True)
            ins.then_inc(T["xz"], 1)
            for b in range(DEC):
                if b >= 2:
                    pe.wait_ge(T["hst"], b - 1)
                pe.matmul(bank[b % 2][:, :], ident[0:DEC, b:b + 1].to_broadcast([DEC, P]), st_xc[:, 512:1024],
                          start=True, stop=True).then_inc(T["bc"], 1)
            pe.wait_ge(T["norm"], 1)
            pe.matmul(bank[6][:, 0:4 * DEC], ones, st_g2[:, :, :].rearrange("p a b -> p (a b)"), start=True, stop=True).then_inc(T["norm"], 1)
            pe.wait_ge(T["att"], 8)
            pe.wait_ge(T["norm"], 5)
            pe_out(pe, TILES, DEC)
            pe_turn_t(pe, TILES, DEC)
            pe_router(pe, TILES, DEC)
            pe_rank(pe, TILES, DEC)
            def pe_choices(done, sel, rhs):
                for i in range(PAIRS):
                    if i % THIRD == 0:
                        pe.wait_ge(T[done], i // THIRD + 1)
                    ins = pe.matmul(bank[1][:, 0:rhs.shape[2]], sel[i // THIRD][:, i % THIRD, :], rhs[:, i, :], start=i == 0, stop=i == PAIRS - 1)
                ins.then_inc(T[done], 1)

            pe.wait_ge(T["cnt"], 1)
            pe.matmul(bank[0][:, 0:NE], ones, counted[:, :], start=True, stop=True).then_inc(T["cnt"], 1)
            pe_choices("slots", row_sel, chosen)

            pe.sem_inc(E_["dn"], 1)
            pe.sem_inc(V["dn"], 1)
            pe.wait_ge(T["et"], 1)

            def expert_up(w, out, done):
                for a in range(2):
                    for k in range(KC):
                        ins = pe.matmul(out[:, a * P:(a + 1) * P], wgu[w][:, a, k, :], xgT[w % 2][:, k, :], start=k == 0, stop=k == KC - 1)
                ins.then_inc(done, 1)

            def expert_down(w, done):
                for c in range(2):
                    ins = pe.matmul(bank[6 + c][:, :], hidT[w % 2], wd[w][:, 512 * c:512 * c + 512], start=True, stop=True)
                ins.then_inc(done, 1)

            def pe_turn(j, w, gathered):
                pe.wait_ge(e_x[w], gathered)
                pe_turn_x(pe, xg[w], ident, P, (w % 2 * 2, w % 2 * 2 + 1), E_["turn"])

            def pe_expert(j, w, group, more=True):
                pe.wait_ge(E_["xa"], j + 1)
                pe.wait_ge(E_["xd"], j + 1)
                pe.wait_ge(e_w[w], 48 * group + 48)
                expert_up(w, bank[4 + w % 2], E_["up"])
                if more:
                    pe_turn(j + 1, (w + 1) % RING, 16 * group + (16 if w < RING - 1 else 32))
                pe.wait_ge(E_["hid"], j + 1)
                pe.wait_ge(E_["ya"], j + 1)
                pe.wait_ge(E_["yd"], j + 1)
                expert_down(w, E_["dn"])

            pe_turn(0, 0, 16)
            for w in range(RING):
                pe_expert(w, w, 0)
            with pe.Fori(1, NE // RING - 1) as group:
                for w in range(RING):
                    pe_expert(RING * group + w, w, group)
            for w in range(RING):
                pe_expert(NE - RING + w, w, NE // RING - 1, w < RING - 1)
            over = pe.value_load(over_i[0:1, 0:1], min_val=0, max_val=OVER_TILES)
            with pe.If(over > 0):
                pe_choices("over", over_sel, pair_prod[:, :, 0:OVER_TILES])
                pe.wait_ge(T["over"], 5)
                pe.wait_ge(E_["ya"], NE + 1)
                pe.wait_ge(E_["yd"], NE + 1)
                with pe.Fori(0, OVER_TILES) as j:
                    pe.wait_ge(o_x, 16 * j + 16)
                    pe_turn_x(pe, xg[0], ident, P, (0, 1), V["turn"])
                    pe.wait_ge(V["xe"], j + 1)
                    pe.wait_ge(o_w, 48 * j + 48)
                    expert_up(0, bank[4], V["up"])
                    pe.wait_ge(V["hid"], j + 1)
                    pe.wait_ge(V["ye"], j + 1)
                    expert_down(0, V["dn"])


OUTS = [("y_prompt", (1, SEQ, D)), ("y_sample", (DEC, 1, D)), ("win_k_prompt", (1, 1, P, NKV, HD)), ("win_v_prompt", (1, 1, P, NKV, HD)),
        ("conv_prompt", (P, CC, CK - 1)), ("ssm_prompt", (1, 1, SH, SP_, SN)), ("win_k_sample", (1, DEC, P, NKV, HD)),
        ("win_v_sample", (1, DEC, P, NKV, HD)), ("conv_sample", (1, DEC, CK - 1, CD)), ("ssm_sample", (1, DEC, SH, SP_, SN))]
N_SSM = 16 * (1 + 1 + 3 + 2 + 1 + 1)
N_OUTS = N_SSM + 16 * DEC


def kernel(**inputs):
    import concourse.bacc as bacc
    from concourse.bass_utils import run_bass_kernel_spmd

    nc = bacc.Bacc("TRN2", target_bir_lowering=False, num_devices=1)
    arrays, ins, outs = {}, {}, {}
    given = dict(inputs, constants=shape_constants(), rope=rope_table())
    given["conv_w_by_channel"] = np.asarray(inputs["conv_w"])[0].reshape(CK, CC, P).transpose(2, 1, 0)
    given["conv_b_by_channel"] = np.asarray(inputs["conv_b"])[0].reshape(CC, P).T
    given["ssm_norm_by_channel"] = np.asarray(inputs["ssm_norm"])[0].reshape(4, P).T
    for name, a in given.items():
        a = np.ascontiguousarray(a)
        arrays[f"in_{name}"] = a
        ins[name] = nc.dram_tensor(f"in_{name}", a.shape, mybir.dt.from_np(a.dtype), kind="ExternalInput").ap()
    for name, shape in OUTS:
        outs[name] = nc.dram_tensor(f"out_{name}", shape, F32, kind="ExternalOutput").ap()
    layer_kernel(nc, ins, outs)
    r = run_bass_kernel_spmd(nc, [arrays], core_ids=[0])
    got = {name: r.results[0][f"out_{name}"] for name, _ in OUTS}
    got["conv_prompt"] = got["conv_prompt"].transpose(2, 1, 0).reshape(1, 1, CK - 1, CD)
    return tuple(got[name] for name, _ in OUTS)
```

```python
from contextlib import ExitStack

import numpy as np

import concourse.bass as bass
from concourse import mybir
from concourse.alu_op_type import AluOpType as ALU

F32 = mybir.dt.float32
BF16 = mybir.dt.bfloat16
I32 = mybir.dt.int32
U32 = mybir.dt.uint32
ACT = mybir.ActivationFunctionType
AX = mybir.AxisListType

P = 128
D = 1024
KC = D // P
SEQ = 1024
TILES = SEQ // P
DEC = 8
TOKENS = SEQ + DEC
NH, NKV, HD = 8, 2, 64
REP = NH // NKV
PAST = 8192
THETA = 10000.0
SCALE = HD ** -0.5
SH, SG, SP_, SN = 8, 2, 64, 128
CK = 4
CD = SH * SP_ + 2 * SG * SN
CC = CD // P
Q_END = NH * HD
K_END = Q_END + NKV * HD
V_END = K_END + NKV * HD
Z_END = V_END + SH * SP_
XBC_END = Z_END + CD
IN_DIM = XBC_END + SH
NG, EPG = 4, 8
NE = NG * EPG
FF = D // 8
EPS = 1e-6
BIG = 1e30
CHOICES = 2 * TOKENS
ROWS = P
OVER_TILES = CHOICES // (ROWS + 1)
SLOT_TILES = NE + OVER_TILES
EMPTY = 8192
RING = 4
CREDIT = 2

C_ID, C_TRI, C_STRICT, C_ONES, C_BAND, C_IOTA, C_CHOICE = 0, 128, 256, 384, 512, 768, 896
C_END = C_CHOICE + 2 * (TILES + 1)

W_DT = V_END
W_Z = W_DT + SH
W_XBC = W_Z + SH * SP_


def shape_constants():
    c = np.zeros((P, C_END), np.float32)
    r, q = np.arange(P)[:, None], np.arange(P)[None, :]
    c[:, C_ID:C_ID + P] = r == q
    c[:, C_TRI:C_TRI + P] = r <= q
    c[:, C_STRICT:C_STRICT + P] = r < q
    c[:, C_ONES:C_ONES + P] = 1.0
    c[:, C_BAND:C_BAND + P] = np.where(q > r, 0.0, -BIG)
    c[:, C_BAND + P:C_BAND + 2 * P] = np.where(q <= r, 0.0, -BIG)
    c[:, C_IOTA:C_IOTA + P] = np.arange(P)
    i = np.arange(2 * (TILES + 1))
    c[:, C_CHOICE:C_END] = i % 2 * TOKENS + i // 2 * P + r - EMPTY
    return c


def rope_table():
    inv = np.float32(1.0) / np.power(THETA, np.arange(0, HD, 2) / HD).astype(np.float32)
    pos = np.concatenate([np.arange(SEQ), np.full(P, PAST)]).astype(np.float32)
    ang = pos[:, None] * inv[None, :]
    ang = ang.astype(np.float64)
    return np.concatenate([np.cos(ang), np.sin(ang)], axis=1).astype(np.float32)


def layer_kernel(nc, I, O):
    with ExitStack() as ctx:
        def sb(name, shape, dt=F32):
            return ctx.enter_context(nc.sbuf_tensor(name, shape, dt))

        def sem(name):
            return ctx.enter_context(nc.semaphore(name))

        bank = [ctx.enter_context(nc.psum_tensor(f"bank{n}", [P, 512], F32)) for n in range(8)]
        h_dram = nc.dram_tensor("h_dram", (TOKENS, D), F32, kind="Internal").ap()
        t_dram = nc.dram_tensor("t_dram", (TOKENS, D), F32, kind="Internal").ap()
        y_dram = nc.dram_tensor("y_dram", (CHOICES, D), F32, kind="Internal").ap()

        con = sb("con", [P, C_END])
        ident, tri, strict, ones = (con[:, c:c + P] for c in (C_ID, C_TRI, C_STRICT, C_ONES))
        w_arena = sb("w_arena", [P, KC * IN_DIM])
        w_in = w_arena[:, :].rearrange("p (k n) -> p k n", k=KC)
        w_out = sb("w_out_sb", [P, KC, D])
        w_route = sb("w_route", [P, KC, NG + NE])
        b_route = sb("b_route", [P, NG + NE])
        norm1 = sb("norm1_sb", [P, KC])
        norm2 = sb("norm2_sb", [P, D])
        qk_norm = sb("qk_norm", [P, 2, HD])
        sink = sb("sink", [P, NH])
        sink_col = sb("sink_col", [NH, 1])
        conv_w = sb("conv_w_sb", [P, CC, CK])
        conv_b = sb("conv_b_sb", [P, CC])
        dt_bias = sb("dt_bias_sb", [P, SH])
        a_neg = sb("a_neg", [P, SH])
        d_skip = sb("d_skip_sb", [P, SH])
        d_col = sb("d_col", [SH, 1])
        ssm_norm = sb("ssm_norm_sb", [P, 4])
        neg_half = sb("neg_half", [P, 16])
        eps = sb("eps", [P, 16])
        mask = sb("mask", [P, 2, P])

        x = [sb(f"x{u}", [P, D]) for u in range(2)]
        rope = [sb(f"rope{u}", [P, HD]) for u in range(2)]
        xn = sb("xn", [P, D])
        xT = sb("xT", [P, KC, P])
        junk = sb("junk", [P, D], BF16)
        stat = sb("stat", [P, 16])
        rstd = sb("rstd", [P, 16])
        qk = sb("qk", [P, 10, HD])
        qkr = sb("qkr", [P, 10, HD])
        v_new = sb("v_new", [P, P])
        v = sb("v", [P, 2, P])
        qT = sb("qT", [P, REP, P])
        kT = sb("kT", [P, 2, P])
        s = sb("s", [P, NH, 2 * P])
        top = sb("top", [P, 4, NH])
        pT = sb("pT", [P, NKV, 2, REP, P])
        aT = sb("aT", [P, REP, P])
        dt = sb("dt", [P, 5, SH])
        zs = sb("zs", [P, SH * SP_])
        raw = sb("raw", [P, CC, P + CK - 1])
        cv = sb("cv", [P, CC, P])
        xc = sb("xc", [P, CC, P])
        xtok = sb("xtok", [P, SH, SP_])
        btok = sb("btok", [P, SG, P])
        xdt = sb("xdt", [P, SH, SP_])
        xde = sb("xde", [P, SH, SP_])
        xd = sb("xd", [P, SH, SP_])
        cum = sb("cum", [P, 3, SH])
        ecum = sb("ecum", [P, 3, SH])
        cbm = sb("cbm", [P, SG, P])
        m = cv
        hT = sb("hT", [P, SH, SP_])
        y = sb("y", [P, SH, SP_])
        gT = sb("gT", [P, 4, P])
        t = sb("t", [P, D])
        tT = sb("tT", [P, KC, P])
        lg = sb("lg", [P, 8 + NE])
        le = sb("le", [P, NG, EPG])
        g8 = sb("g8", [P, 8])
        e8 = sb("e8", [P, 8])
        gi = sb("gi", [P, 8], U32)
        ei = sb("ei", [P, 8], U32)
        fi = sb("fi", [P, 16])
        gmask = sb("gmask", [P, 2, NG])
        rt = sb("rt", [P, 8])
        rexp = sb("rexp", [P, NG])
        onehot = sb("onehot", [P, TILES + 1, 2, NE])
        both = sb("both", [P, NE])
        counted = sb("counted", [P, NE])
        rankc = sb("rankc", [P, NE])
        rprod = sb("rprod", [P, 2, NE])
        rank = sb("rank", [P, TILES + 1, 2])
        gate = sb("gate", [P, TILES + 1, 2])

        keys = pT[:, 0, :, :, :].rearrange("p a b c -> p (a b) c")
        vals = pT[:, 1, :, :, :].rearrange("p a b c -> p (a b) c")
        keysT = xT
        q_blk = sb("q_blk", [P, DEC, NKV, REP])
        flat_s = s[:, :, :].rearrange("p a b -> p (a b)")
        ps = flat_s[0:NH, 0:DEC * P].rearrange("p (b s) -> p b s", b=DEC)
        ps_T = sb("ps_T", [P, DEC, NH])
        m_top = sb("m_top", [NH, 4, DEC])
        flat_raw = raw[:, :, :].rearrange("p c n -> p (c n)")
        st_conv = flat_raw[0:DEC * (CK - 1), 0:CD]
        st_raw = xn[0:DEC, :]
        st_acc = sb("st_acc", [P, CC, DEC])
        st_tmp = sb("st_tmp", [P, CC, DEC])
        st_xc = sb("st_xc", [P, CC, DEC])
        st_bc = qT[0:DEC, :, :].rearrange("p a b -> p (a b)")
        st_h = w_arena[:, 12 * CD:16 * CD].rearrange("p (b c n) -> p b c n", b=DEC, c=4)
        head_sel = w_arena[0:SH, 16 * CD:16 * CD + SH * SP_]
        flat_cv = cv[:, :, :].rearrange("p a b -> p (a b)")
        st_cs = [kT[:, :, :], cbm[:, :, :]]
        st_bx = [flat_cv[:, u * 512:(u + 1) * 512].rearrange("p (c n) -> p c n", c=4) for u in range(2)]
        st_ch = [xdt[:, :, :].rearrange("p a b -> p (a b)").rearrange("p (c n) -> p c n", c=4),
                 xde[:, :, :].rearrange("p a b -> p (a b)").rearrange("p (c n) -> p c n", c=4)]
        st_turned = y[:, :, :].rearrange("p a b -> p (a b)").rearrange("p (c n) -> p c n", c=4)
        st_xT = st_xc[:, 0:4, :]
        st_zT = sb("st_zT", [P, 4, DEC])
        st_da = sb("st_da", [SH, 2 * DEC + 1])
        st_sc = sb("st_sc", [P, 4, 2 * DEC + 1])
        st_dx = sb("st_dx", [P, 4, DEC])
        st_y = sb("st_y", [P, 4, DEC])
        st_g2 = sb("st_g2", [P, 4, DEC])
        st_n = sb("st_n", [P, SG, DEC])
        st_r = sb("st_r", [P, SG, DEC])

        PAIRS = 2 * (TILES + 1)
        slot_tab = sb("slot_tab", [P, SLOT_TILES, 2], I32)
        slot_f = sb("slot_f", [P, 2, NE])
        EARLY = 2 * TILES
        etile_i = sb("etile_i", [1, OVER_TILES], I32)
        over_i = sb("over_i", [1, 1], I32)
        flat_pT = pT[:, :, :, :, :].rearrange("p a b c d -> p (a b c d)")
        flat_xc = xc[:, :, :].rearrange("p a b -> p (a b)")
        chosen = flat_raw[:, 0:PAIRS * NE].rearrange("p (i e) -> p i e", e=NE)
        THIRD = PAIRS // 3
        row_sel = [half[:, :].rearrange("p (i r) -> p i r", r=P)
                   for half in (flat_s[:, D:2 * D], flat_xc, flat_s[:, 0:2 * P])]
        over_sel = [half[:, :].rearrange("p (i r) -> p i r", r=P)
                    for half in (flat_pT[:, 0:THIRD * P], flat_pT[:, THIRD * P:2 * THIRD * P], flat_xc[:, 0:THIRD * P])]
        flat_onehot = onehot[:, :, :, :].rearrange("p a b e -> p (a b) e")
        flat_rank = rank[:, :, :].rearrange("p a b -> p (a b)")
        flat_xd = xd[:, :, :].rearrange("p a b -> p (a b)")
        quo = flat_xd[:, 4 * NE:4 * NE + 4 * PAIRS].rearrange("p (a e) -> p a e", a=4)
        nt = flat_xd[:, 0:4 * NE].rearrange("p (a e) -> p a e", a=4)
        pair_prod = chosen
        ecmp = flat_cv[0:1, 0:OVER_TILES * NE].rearrange("p (j e) -> p j e", e=NE)
        etile = flat_cv[0:1, OVER_TILES * NE:OVER_TILES * (NE + 1)]

        def arena(at, n):
            return w_arena[:, at:at + n]
        wgu = [arena(w * 3 * D, 2 * D).rearrange("p (a k f) -> p a k f", a=2, k=KC) for w in range(RING)]
        wd = [arena(w * 3 * D + 2 * D, D) for w in range(RING)]
        xg = [x[1][:, :], xn[:, :], xT[:, :, :].rearrange("p a b -> p (a b)"), tT[:, :, :].rearrange("p a b -> p (a b)")]
        xgT = [arena((12 + u) * D, D).rearrange("p (k f) -> p k f", k=KC) for u in range(2)]
        sil = [arena(14 * D + u * P, P) for u in range(2)]
        hidT = [arena(14 * D + (2 + u) * P, P) for u in range(2)]
        yo = [flat_s[:, u * D:(u + 1) * D] for u in range(2)]
        late_wgu = [flat_pT[:, 0:2 * D].rearrange("p (a k f) -> p a k f", a=2, k=KC), arena(15 * D, 2 * D).rearrange("p (a k f) -> p a k f", a=2, k=KC)]
        late_wd = [t[:, :], arena(17 * D, D)]
        idx_in = [sb(f"idx_in{w}", [P, 1], I32) for w in range(RING)]
        idx_out = [sb(f"idx_out{w}", [P, 1], I32) for w in range(RING)]
        c_h = [w_out[:, c, :] for c in range(TILES)] + [x[0][:, :]]
        c_y = [[arena((2 * w + k) * D, D) for k in range(2)] for w in range(4)]

        loaded = sem("loaded")
        S = {}
        for name in ("ssq xs xn xm xT projq projk projz proja projc qe qkv vc rawa dtp dl dta z rawc cumm cum ecd qsq qs qkr qkt qkc sc0 sc1 sc2 sc3 "
                     "se smax pexp prob ptm pta ptb pv at convd xcs xtm xtk xdt xde xd rmm rmin rexpd cbm md ydm yf "
                     "stm std ysq ys yg ytm gt conva wom hres hsq hs td ttm tt lgm sel gex rsel rankm rankd").split():
            S[name] = sem("s_" + name)
        T = {}
        for name in "init aneg q kT att cv dt xz bcT bc bx hup ch hst norm ssmT cnt part slots et over".split():
            T[name] = sem("m_" + name)
        E_ = {}
        for name in ("turn xa xd up sil hid dn ya yd idx").split():
            E_[name] = sem("e_" + name)
        V = {}
        for name in ("turn xe up sil hid dn ye").split():
            V[name] = sem("o_" + name)
        x_in = [sem(f"x_in{u}") for u in range(2)]
        h_out = [sem(f"h_out{u}") for u in range(2)]
        t_out = [sem(f"t_out{u}") for u in range(2)]
        cache_in = sem("cache_in")
        state_in = sem("state_in")
        e_w = [sem(f"e_w{w}") for w in range(RING)]
        e_w_late = sem("e_w_late")
        e_x = [sem(f"e_x{w}") for w in range(4)]
        e_out = [sem(f"e_out{u}") for u in range(2)]
        o_w, o_x, o_out = sem("o_w"), sem("o_x"), sem("o_out")
        c_in = sem("c_in")
        c_in1 = [sem(f"c_in1{w}") for w in range(4)]
        c_done = sem("c_done")
        c_out = sem("c_out")
        kv_out = sem("kv_out")
        first_in, params, w_q, w_kv, w_z, conv_in = (sem(name) for name in ("first_in", "params", "w_q", "w_kv", "w_z", "conv_in"))
        w_x = [sem(f"w_x{half}") for half in range(2)]
        outs = sem("outs")
        block = ctx.enter_context(nc.Block())

        def now(eng, names, tile):
            for name in names.split():
                eng.wait_ge(S[name], tile + (CREDIT + 1))

        def last(eng, names, tile):
            for name in names.split():
                eng.wait_ge(S[name], tile + CREDIT)

        def credit(eng, names):
            for name in names.split():
                eng.sem_inc(S[name], CREDIT)

        flat_x = I["x_prompt"].rearrange("a s d -> (a s) d")
        n_loaded = [0]
        N_PARAMS = 16 * 11

        def row(name, n):
            return I[name].rearrange("a n -> (a n)").rearrange("(a n) -> a n", a=1).broadcast_to([n, I[name].shape[-1]])

        @block.sync
        def _(sp):
            def load(dst, src):
                sp.dma_start(dst, src).then_inc(loaded, 16)
                n_loaded[0] += 16

            w_rows = I["w_in"].rearrange("a (p k) n -> (a p) k n", k=KC)

            def weights(at, start, stop, landed):
                sp.dma_start(w_in[:, :, at:at + stop - start], w_rows[:, :, start:stop]).then_inc(landed, 16)

            def token_rows(u):
                sp.dma_start(x[u][:, :], flat_x[u * P:(u + 1) * P, :]).then_inc(x_in[u], 16)
                sp.dma_start(rope[u][:, :], I["rope"][u * P:(u + 1) * P, :]).then_inc(x_in[u], 16)

            token_rows(0)
            sp.dma_start(norm1[:, :], I["norm1"].rearrange("a (p k) -> (a p) k", k=KC)).then_inc(first_in, 16)
            sp.dma_start(con[:, :], I["constants"]).then_inc(first_in, 16)
            weights(0, 0, Q_END, w_q)
            weights(Q_END, Q_END, V_END, w_kv)
            weights(W_DT, XBC_END, IN_DIM, w_kv)
            for dst, src in (
                    (qk_norm[:, 0, :], row("q_norm", P)),
                    (qk_norm[:, 1, :], row("k_norm", P)),
                    (sink[:, :], row("sinks", P)),
                    (sink_col[:, :], I["sinks"].rearrange("a (n b) -> (a n) b", b=1)),
                    (d_col[:, :], I["d_skip"].rearrange("a (n b) -> (a n) b", b=1)),
                    (conv_w[:, :, :], I["conv_w_by_channel"]),
                    (conv_b[:, :], I["conv_b_by_channel"]),
                    (dt_bias[:, :], row("dt_bias", P)),
                    (a_neg[:, :], row("a_log", P)),
                    (d_skip[:, :], row("d_skip", P)),
                    (ssm_norm[:, :], I["ssm_norm_by_channel"]),
            ):
                sp.dma_start(dst, src).then_inc(params, 16)
            for half in range(2):
                weights(W_XBC + 512 * half, Z_END + 512 * half, Z_END + 512 * half + 512, w_x[half])
            weights(W_Z, V_END, Z_END, w_z)
            token_rows(1)
            for kv in range(NKV):
                load(w_out[kv * HD:(kv + 1) * HD, 0:REP, :],
                     I["w_out"][0, kv * REP * HD:(kv + 1) * REP * HD].rearrange("(r d) n -> d r n", d=HD))
            load(w_out[:, REP:KC, :], I["w_out"][0, NH * HD:].rearrange("(c p) n -> p c n", p=P))
            load(norm2[:, :], row("norm2", P))
            load(w_route[:, :, 0:NG], I["w_grp"].rearrange("a (p k) n -> (a p) k n", k=KC))
            load(w_route[:, :, NG:NG + NE], I["w_exp"].rearrange("a (p k) n -> (a p) k n", k=KC))
            load(b_route[:, 0:NG], row("b_grp", P))
            load(b_route[:, NG:NG + NE], row("b_exp", P))

            with sp.Fori(0, TILES // 2 - 1) as pair:
                t0 = pair * 2
                for u in range(2):
                    sp.wait_ge(first_in, 32)
                    sp.wait_ge(S["td"], t0 + (u + CREDIT + 1))
                    sp.dma_start(rope[u][:, :], I["rope"][bass.ds(t0 * P + (u + 2) * P, P), :]).then_inc(x_in[u], 16)
                    sp.wait_ge(h_out[u], 8 * t0 + 32)
                    sp.dma_start(x[u][:, :], flat_x[bass.ds(t0 * P + (u + 2) * P, P), :]).then_inc(x_in[u], 16)
            now(sp, "td", TILES - 2)
            sp.wait_ge(h_out[0], 16 + 16 * (TILES // 2))
            sp.dma_start(x[0][0:DEC, :], I["x_sample"].rearrange("b s d -> (b s) d")).then_inc(x_in[0], 16)
            sp.dma_start(rope[0][0:DEC, :], I["rope"][SEQ:SEQ + DEC, :]).then_inc(x_in[0], 16)
            now(sp, "convd", TILES - 1)
            sp.dma_start(O["conv_prompt"], raw[:, :, 0:CK - 1]).then_inc(kv_out, 16)
            now(sp, "qkr", TILES - 1)
            sp.dma_start(O["win_k_prompt"].rearrange("a b s k d -> (a b s) (k d)"), qkr[:, 8:10, :].rearrange("p a b -> p (a b)")).then_inc(kv_out, 16)
            sp.wait_ge(kv_out, 32)
            sp.dma_start(st_conv, I["state_conv"][0].rearrange("b k c -> (b k) c")).then_inc(conv_in, 16)
            last(sp, "pv", TILES)
            sp.dma_start(O["win_v_prompt"].rearrange("a b s k d -> (a b s) (k d)"), v[:, 1, :]).then_inc(outs, 16)
            ck = I["cache_win_k"].rearrange("a b s k d -> (a s) b (k d)")
            cw = I["cache_win_v"].rearrange("a b s k d -> (a s) b (k d)")
            sp.dma_start(keys[0:P - 1, :, :], ck[1:P]).then_inc(cache_in, 16)
            sp.dma_start(vals[0:P - 1, :, :], cw[1:P]).then_inc(cache_in, 16)
            for name in ("k", "v"):
                o = O[f"win_{name}_sample"].rearrange("a b s k d -> (a b) s (k d)")
                i = I[f"cache_win_{name}"].rearrange("a b s k d -> (a b) s (k d)")
                sp.dma_start(o[:, 0:P - 1, :], i[:, 1:P, :]).then_inc(outs, 16)
            sp.dma_start(O["conv_sample"][0, :, 0:CK - 2, :], I["state_conv"][0, :, 1:CK - 1, :]).then_inc(outs, 16)
            now(sp, "qkr qkv", TILES)
            new_k = qkr[0:DEC, 8:10, :].rearrange("p a b -> p (a b)")
            new_v = v_new[0:DEC, :]
            sp.dma_start(keys[P - 1:P, :, :], new_k).then_inc(cache_in, 16)
            sp.dma_start(vals[P - 1:P, :, :], new_v).then_inc(cache_in, 16)
            sp.dma_start(O["win_k_sample"].rearrange("a b s k d -> (a b) s (k d)")[:, P - 1, :], new_k).then_inc(outs, 16)
            sp.dma_start(O["win_v_sample"].rearrange("a b s k d -> (a b) s (k d)")[:, P - 1, :], new_v).then_inc(outs, 16)
            now(sp, "projz", TILES)
            for b in range(DEC):
                sp.dma_start(st_h[:, b], I["state_ssm"][0, b].rearrange("(c l) p n -> (l p) c n", l=2)).then_inc(state_in, 16)
            now(sp, "rawc", TILES)
            sp.dma_start(O["conv_sample"][0, :, CK - 2, :], st_raw).then_inc(outs, 16)
            def load_gate_up(e, gu):
                one = bass.ds(e, 1)
                return (sp.dma_start(gu[:, 0], I["w_gate"][0, one].rearrange("a (p k) f -> (a p) k f", k=KC)),
                        sp.dma_start(gu[:, 1], I["w_up"][0, one].rearrange("a (p k) f -> (a p) k f", k=KC)))

            def load_down(e, down):
                return sp.dma_start(down, I["w_down"][0, bass.ds(e, 1)].rearrange("a f n -> (a f) n"))

            def expert_weights(e, gu, down):
                return (*load_gate_up(e, gu), load_down(e, down))

            for w in range(RING):
                for one in expert_weights(w, wgu[w], wd[w]):
                    one.then_inc(e_w[w], 16)
            sp.wait_ge(T["att"], 7)
            for one in load_gate_up(NE - 2, late_wgu[0]):
                one.then_inc(e_w_late, 16)
            sp.wait_ge(T["ssmT"], 2)
            sp.dma_start(O["ssm_prompt"].rearrange("a b (c l) p n -> (a b l p) c n", l=2), st_turned).then_inc(outs, 16)
            for b in range(DEC):
                sp.wait_ge(T["hup"], b + 1)
                sp.dma_start(O["ssm_sample"][0, b].rearrange("(c l) p n -> (l p) c n", l=2), st_h[:, b]).then_inc(outs, 16)
            sp.wait_ge(outs, N_OUTS)
            for one in expert_weights(NE - 1, late_wgu[1], late_wd[1]):
                one.then_inc(e_w_late, 16)
            def load_residual(c):
                sp.dma_start(c_h[c], h_dram[c * P:(c + 1) * P, :]).then_inc(c_in, 16)

            now(sp, "wom", TILES)
            for u in range(2):
                sp.wait_ge(h_out[u], 16 + 16 * ((TILES + 1 - u) // 2))
            for c in range(TILES // 2):
                load_residual(c)
            for u in range(2):
                sp.wait_ge(t_out[u], 16 + 16 * ((TILES + 2 - u) // 2))
            now(sp, "ttm", TILES)
            for u in range(2):
                sp.wait_ge(e_x[u], 16)
            load_down(NE - 2, late_wd[0]).then_inc(e_w_late, 16)
            for c in range(TILES // 2, TILES):
                load_residual(c)
            with sp.Fori(1, NE // RING - 1) as group:
                for w in range(RING):
                    sp.wait_ge(first_in, 32)
                    sp.wait_ge(E_["dn"], RING * group + (w - RING + 2))
                    for one in expert_weights(RING * group + w, wgu[w], wd[w]):
                        one.then_inc(e_w[w], 16)
            for w in range(RING - 2):
                j = NE - RING + w
                sp.wait_ge(E_["dn"], j - RING + 2)
                for one in expert_weights(j, wgu[w], wd[w]):
                    one.then_inc(e_w[w], 16)
            sp.wait_ge(T["et"], 1)
            over = sp.value_load(over_i[0:1, 0:1], min_val=0, max_val=OVER_TILES)
            with sp.If(over > 0):
                sp.wait_ge(E_["dn"], NE + 1)
                with sp.Fori(0, OVER_TILES) as j:
                    e = sp.value_load(etile_i[0:1, bass.ds(j, 1)], min_val=0, max_val=NE - 1)
                    sp.wait_ge(T["et"], 1)
                    sp.wait_ge(V["dn"], j + 1)
                    for one in expert_weights(e, wgu[0], wd[0]):
                        one.then_inc(o_w, 16)
                sp.wait_ge(o_out, 16 * OVER_TILES)
                sp.wait_ge(V["dn"], OVER_TILES + 1)
            sp.wait_ge(E_["dn"], NE + 1)
            for u in range(2):
                sp.wait_ge(e_out[u], 16 * NE // 2)
            for c in range(TILES + 1):
                n, w = (P if c < TILES else DEC), c % 4
                if c >= 4:
                    sp.wait_ge(c_done, c - 3)
                for k in range(2):
                    at = k * TOKENS + c * P
                    sp.dma_start(c_y[w][k][0:n, :], y_dram[at:at + n, :]).then_inc(c_in1[w], 16)
            sp.wait_ge(c_out, 16 * (TILES + 1))
            sp.wait_ge(outs, N_OUTS)

        def rows(ap, n):
            return ap[0:n]

        def act_rows(act, tile, u, n, x_need):
            act.wait_ge(x_in[u], x_need)
            last(act, "xs", tile)
            act.activation(junk[0:n, :], x[u][0:n, :], ACT.Square, scale=D ** -0.5, accum_out=stat[0:n, 0:1]).then_inc(S["ssq"], 1)
            now(act, "xs", tile)
            last(act, "xm", tile)
            act.activation(xn[0:n, :], x[u][0:n, :], ACT.Copy, scale=rstd[0:n, 0:1]).then_inc(S["xn"], 1)

        def act_q(act, tile, n):
            now(act, "projq", tile)
            last(act, "qkr", tile)
            act.activation(qk[0:n, 0:8, :].rearrange("p a b -> p (a b)"), bank[0][0:n, :], ACT.Copy).then_inc(S["qe"], 1)

        def act_kv(act, tile, n):
            now(act, "projk", tile)
            last(act, "qkr dta vc", tile)
            act.activation(qk[0:n, 8:10, :].rearrange("p a b -> p (a b)"), bank[1][0:n, 0:P], ACT.Copy)
            act.activation(v_new[0:n, :], bank[1][0:n, P:2 * P], ACT.Copy)
            act.activation(dt[0:n, 0, :], bank[1][0:n, 2 * P:2 * P + SH], ACT.Copy).then_inc(S["qkv"], 1)

        def act_raw(act, tile, n, half):
            now(act, ("proja", "projc")[half], tile)
            last(act, ("conva", "convd")[half], tile)
            if n == P:
                out = raw[:, 4 * half:4 * half + 4, CK - 1:]
                act.activation(out, bank[half][:, :].rearrange("p (c n) -> p c n", c=4), ACT.Copy).then_inc(S[("rawa", "rawc")[half]], 1)
            else:
                act.activation(st_raw[:, 512 * half:512 * half + 512], bank[half][0:n, :], ACT.Copy).then_inc(S[("rawa", "rawc")[half]], 1)

        def act_softplus(act, tile, n):
            now(act, "dtp", tile)
            act.activation(dt[0:n, 2, :], dt[0:n, 1, :], ACT.Exp, scale=-1.0)
            act.drain()
            act.activation(dt[0:n, 2, :], dt[0:n, 2, :], ACT.Ln, bias=1.0).then_inc(S["dl"], 1)

        def act_z(act, tile, n):
            now(act, "projz", tile)
            last(act, "yf", tile)
            act.activation(zs[0:n, :], bank[0][0:n, :], ACT.Silu).then_inc(S["z"], 1)

        def act_residual(act, tile, u, n, dram_rows):
            now(act, "hres", tile)
            act.dma_start(h_dram[dram_rows, :], x[u][0:n, :]).then_inc(h_out[u], 16)
            act.activation(junk[0:n, :], x[u][0:n, :], ACT.Square, scale=D ** -0.5, accum_out=stat[0:n, 13:14]).then_inc(S["hsq"], 1)

        def act_store_t(act, tile, u, n, dram_rows):
            now(act, "td", tile)
            act.dma_start(t_dram[dram_rows, :], t[0:n, :]).then_inc(t_out[u], 16)

        def act_turned_t(act, tile, n):
            now(act, "ttm", tile)
            act.activation(tT[:, 0:4, 0:n], bank[5][:, 0:4 * n].rearrange("p (k n) -> p k n", k=4), ACT.Copy)
            act.activation(tT[:, 4:8, 0:n], bank[6][:, 0:4 * n].rearrange("p (k n) -> p k n", k=4), ACT.Copy).then_inc(S["tt"], 1)

        def act_conv(act, tile):
            now(act, "convd", tile)
            last(act, "ydm", tile)
            act.activation(xc[:, :, :], cv[:, :, :], ACT.Silu).then_inc(S["xcs"], 1)

        def act_router(act, tile, n):
            now(act, "sel", tile)
            act.activation(rexp[0:n, :], lg[0:n, 0:NG], ACT.Exp, bias=rt[0:n, 0:1], accum_out=rt[0:n, 1:2])
            act.activation(rt[0:n, 3:4], e8[0:n, 1:2], ACT.Exp, bias=rt[0:n, 2:3]).then_inc(S["gex"], 1)

        @block.scalar
        def _(act):
            credit(act, "ssq xn qe qkv vc dl z rawa rawc ecd pexp pta at xcs xtk rexpd ysq hsq tt gex")
            for u in range(2):
                act.sem_inc(h_out[u], 16)
                act.sem_inc(t_out[u], 16)
            act_rows(act, 0, 0, P, 32)
            act_q(act, 0, P)
            act_kv(act, 0, P)
            act.wait_ge(params, N_PARAMS)
            act.activation(a_neg[:, :], a_neg[:, :], ACT.Exp).then_inc(T["aneg"], 1)
            act_softplus(act, 0, P)
            act_raw(act, 0, P, 0)
            act_raw(act, 0, P, 1)
            act_z(act, 0, P)
            act_conv(act, 0)
            act.wait_ge(T["init"], 1)

            def act_tile(tile, u, n_next, x_need, dram_rows, first=False):
                act_rows(act, tile + 1, 1 - u, n_next, x_need)
                last(act, "pv", tile)
                act.activation(v[:, 0, :], v[:, 1, :], ACT.Copy)
                act.drain()
                act.activation(v[:, 1, :], v_new[:, :], ACT.Copy).then_inc(S["vc"], 1)
                now(act, "cum", tile)
                last(act, "yf std xde", tile)
                act.activation(ecum[:, :, :], cum[:, :, :], ACT.Exp).then_inc(S["ecd"], 1)
                now(act, "xtm", tile)
                last(act, "stm yf xd xdt", tile)
                act.activation(xtok[:, :, :].rearrange("p a b -> p (a b)"), bank[2][:, :], ACT.Copy)
                act.activation(btok[:, :, :].rearrange("p a b -> p (a b)"), bank[3][:, 0:2 * P], ACT.Copy).then_inc(S["xtk"], 1)
                now(act, "smax", tile)
                for hh in range(NH):
                    act.activation(s[:, hh, :], s[:, hh, :], ACT.Exp, bias=top[:, 1, hh:hh + 1], accum_out=top[:, 2, hh:hh + 1])
                act.activation(top[:, 3, :], top[:, 3, :], ACT.Exp).then_inc(S["pexp"], 1)
                now(act, "rmin", tile)
                act.activation(m[:, :, :], m[:, :, :], ACT.Exp).then_inc(S["rexpd"], 1)
                if not first:
                    act_router(act, tile - 1, P)
                act_q(act, tile + 1, n_next)
                act_kv(act, tile + 1, n_next)
                now(act, "ptm", tile)
                last(act, "pv", tile)
                act.activation(pT[:, 0, 0].rearrange("p a b -> p (a b)"), bank[4][:, :], ACT.Copy)
                act.activation(pT[:, 0, 1].rearrange("p a b -> p (a b)"), bank[2][:, :], ACT.Copy).then_inc(S["pta"], 1)
                now(act, "pv", tile)
                last(act, "wom", tile)
                act.activation(aT[:, :, :].rearrange("p a b -> p (a b)"), bank[4][:, :], ACT.Copy).then_inc(S["at"], 1)
                now(act, "yf", tile)
                last(act, "ys", tile)
                for g in range(SG):
                    ins = act.activation(junk[:, 256 * g:256 * g + 256], y[:, 4 * g:4 * g + 4, :].rearrange("p a b -> p (a b)"),
                                         ACT.Square, scale=256 ** -0.5, accum_out=stat[:, 11 + g:12 + g])
                ins.then_inc(S["ysq"], 1)
                act_raw(act, tile + 1, n_next, 0)
                act_softplus(act, tile + 1, n_next)
                act_raw(act, tile + 1, n_next, 1)
                act.drain()
                act_residual(act, tile, u, P, dram_rows)
                act_store_t(act, tile, u, P, dram_rows)
                act_z(act, tile + 1, n_next)
                act_turned_t(act, tile, P)
                if n_next == P:
                    act_conv(act, tile + 1)

            act_tile(0, 0, P, 32, slice(0, P), first=True)
            with act.Fori(0, TILES // 2 - 1) as pair:
                t0 = pair * 2 + 1
                for u in range(2):
                    act_tile(t0 + u, 1 - u, P, 32 * pair + 64, bass.ds(t0 * P + u * P, P))
            act_tile(TILES - 1, 1, DEC, 16 * TILES + 32, slice((TILES - 1) * P, TILES * P))
            now(act, "dta", TILES)
            act.activation(dt[0:DEC, 4, :], dt[0:DEC, 4, :], ACT.Exp).then_inc(T["dt"], 1)
            act.wait_ge(T["kT"], 1)
            act.activation(keysT[:, 0:4, :].rearrange("p a b -> p (a b)"), bank[5][:, :], ACT.Copy).then_inc(T["kT"], 1)
            act.wait_ge(T["cv"], 2)
            act.activation(st_xc[:, :, :], st_acc[:, :, :], ACT.Silu).then_inc(T["cv"], 1)
            act.wait_ge(T["att"], 2)
            for b in range(DEC):
                act.activation(ps[:, b, :], bank[b // 4][0:NH, (b % 4) * P:(b % 4 + 1) * P], ACT.Exp, scale=SCALE,
                               bias=m_top[:, 1, b:b + 1], accum_out=m_top[:, 2, b:b + 1])
            act.activation(m_top[:, 3, :], m_top[:, 3, :], ACT.Exp).then_inc(T["att"], 1)
            act.wait_ge(T["xz"], 3)
            for b in range(DEC):
                act.wait_ge(T["bc"], b + 1)
                if b >= 2:
                    act.wait_ge(T["hup"], b - 1)
                    act.wait_ge(T["ch"], b - 1)
                both_in = bank[(6, 2)[b % 2]]
                for c in range(4):
                    act.activation(st_bx[b % 2][:, c, :], both_in[:, (c // 2) * P:(c // 2 + 1) * P], ACT.Copy, scale=st_dx[:, c, b:b + 1])
                act.activation(st_cs[b % 2], both_in[:, 2 * P:4 * P].rearrange("p (g n) -> p g n", g=SG), ACT.Copy).then_inc(T["bx"], 1)
                if b == 1:
                    act_router(act, TILES - 1, P)
            act.drain()
            act_residual(act, TILES, 0, DEC, slice(SEQ, TOKENS))
            act_store_t(act, TILES, 0, DEC, slice(SEQ, TOKENS))
            act_turned_t(act, TILES, DEC)
            act_router(act, TILES, DEC)

            act.sem_inc(E_["ya"], 1)
            act.sem_inc(V["ye"], 1)
            act.wait_ge(outs, N_OUTS)

            def act_turned(j, w):
                act.wait_ge(E_["turn"], j + 1)
                act.activation(xgT[w % 2][:, 0:4, :].rearrange("p a b -> p (a b)"), bank[w % 2 * 2][:, :], ACT.Copy).then_inc(E_["xa"], 1)

            def act_expert(j, w, stored, more=True):
                u = w % 2
                act.wait_ge(E_["up"], j + 1)
                act.activation(sil[u], bank[4 + u][:, 0:P], ACT.Silu).then_inc(E_["sil"], 1)
                if more:
                    act_turned(j + 1, (w + 1) % RING)
                act.wait_ge(E_["dn"], j + 2)
                if stored is not None:
                    act.wait_ge(e_out[u], stored)
                act.activation(yo[u][:, 0:512], bank[6][:, :], ACT.Copy).then_inc(E_["ya"], 1)

            act_turned(0, 0)
            for w in range(RING):
                act_expert(w, w, 16 * (w // 2) if w >= 2 else None)
            with act.Fori(1, NE // RING - 1) as group:
                for w in range(RING):
                    act_expert(RING * group + w, w, 32 * group + 16 * (w // 2))
            for w in range(RING):
                j = NE - RING + w
                act_expert(j, w, 16 * (j // 2), w < RING - 1)
            act.wait_ge(T["et"], 1)
            over = act.value_load(over_i[0:1, 0:1], min_val=0, max_val=OVER_TILES)
            with act.If(over > 0):
                act.wait_ge(e_out[0], 16 * NE // 2)
                with act.Fori(0, OVER_TILES) as j:
                    act.wait_ge(V["turn"], j + 1)
                    act.activation(xgT[0][:, 0:4, :].rearrange("p a b -> p (a b)"), bank[0][:, :], ACT.Copy)
                    act.activation(xgT[0][:, 4:8, :].rearrange("p a b -> p (a b)"), bank[1][:, :], ACT.Copy).then_inc(V["xe"], 1)
                    act.wait_ge(V["up"], j + 1)
                    act.activation(sil[0], bank[4][:, 0:P], ACT.Silu).then_inc(V["sil"], 1)
                    act.wait_ge(V["dn"], j + 2)
                    act.activation(yo[0][:, 0:512], bank[6][:, :], ACT.Copy)
                    act.activation(yo[0][:, 512:D], bank[7][:, :], ACT.Copy).then_inc(V["ye"], 1)
            for c in range(TILES + 1):
                n = P if c < TILES else DEC
                act.wait_ge(c_done, c + 1)
                dst = O["y_prompt"][0, c * P:(c + 1) * P, :] if c < TILES else O["y_sample"].rearrange("b s d -> (b s) d")
                act.dma_start(dst, c_h[c][0:n, :]).then_inc(c_out, 16)

        def dve_xT(dve, tile, n):
            now(dve, "xm", tile)
            last(dve, "projz", tile)
            for c, b in enumerate((0, 1)):
                ins = dve.tensor_tensor(xT[:, 4 * c:4 * c + 4, 0:n], bank[b][:, 0:4 * n].rearrange("p (k n) -> p k n", k=4),
                                        norm1[:, 4 * c:4 * c + 4].unsqueeze(2).to_broadcast([P, 4, n]), ALU.mult)
            ins.then_inc(S["xT"], 1)

        def dve_front(dve, tile, u, n, x_need):
            now(dve, "qkv", tile)
            dve.tensor_tensor(dt[0:n, 0, :], dt[0:n, 0, :], dt_bias[0:n, :], ALU.add)
            dve.drain()
            dve.tensor_scalar(dt[0:n, 1, :], dt[0:n, 0, :], -1.0, None, ALU.mult)
            dve.drain()
            dve.tensor_tensor(dt[0:n, 1, :], dt[0:n, 0, :], dt[0:n, 1, :], ALU.max).then_inc(S["dtp"], 1)
            last(dve, "ptm qs", tile)
            sq = flat_s[0:n, 0:640].rearrange("p (a b) -> p a b", a=10)
            dve.scalar_tensor_tensor(out=sq, in0=qk[0:n, :, :], scalar=1.0 / HD, in1=qk[0:n, :, :], op0=ALU.mult, op1=ALU.mult)
            dve.drain()
            dve.tensor_reduce(stat[0:n, 1:11], sq, AX.X, ALU.add).then_inc(S["qsq"], 1)
            now(dve, "dl", tile)
            last(dve, "rmm xdt", tile)
            dve.tensor_scalar(dt[0:n, 0, :], dt[0:n, 0, :], 0.0, None, ALU.max)
            dve.drain()
            dve.tensor_tensor(dt[0:n, 3, :], dt[0:n, 0, :], dt[0:n, 2, :], ALU.add)
            dve.drain()
            dve.tensor_tensor(dt[0:n, 4, :], dt[0:n, 3, :], a_neg[0:n, :], ALU.mult).then_inc(S["dta"], 1)
            now(dve, "qs", tile)
            last(dve, "qkt", tile)
            dve.wait_ge(x_in[u], x_need)
            w = flat_s[0:n, 1280:1920].rearrange("p (a b) -> p a b", a=10)
            dve.tensor_tensor(w, qk[0:n, :, :], rstd[0:n, 1:11].unsqueeze(2).to_broadcast([n, 10, HD]), ALU.mult)
            dve.drain()
            dve.tensor_tensor(w[:, 0:8, :], w[:, 0:8, :], qk_norm[0:n, 0:1, :].to_broadcast([n, 8, HD]), ALU.mult)
            dve.tensor_tensor(w[:, 8:10, :], w[:, 8:10, :], qk_norm[0:n, 1:2, :].to_broadcast([n, 2, HD]), ALU.mult)
            dve.drain()
            H2 = HD // 2
            tmp = [flat_s[0:n, 320 * a:320 * a + 320].rearrange("p (a b) -> p a b", a=10) for a in range(4)]
            cos = rope[u][0:n, 0:H2].unsqueeze(1).to_broadcast([n, 10, H2])
            sin = rope[u][0:n, H2:HD].unsqueeze(1).to_broadcast([n, 10, H2])
            dve.tensor_tensor(tmp[0], w[:, :, 0:H2], cos, ALU.mult)
            dve.tensor_tensor(tmp[1], w[:, :, H2:HD], sin, ALU.mult)
            dve.tensor_tensor(tmp[2], w[:, :, H2:HD], cos, ALU.mult)
            dve.tensor_tensor(tmp[3], w[:, :, 0:H2], sin, ALU.mult)
            dve.drain()
            q_out = qkr[0:n, 0:8, :].rearrange("p (r k) d -> p k r d", k=NKV)
            for half, (a, b, op) in enumerate(((0, 1, ALU.subtract), (2, 3, ALU.add))):
                at = slice(half * H2, half * H2 + H2)
                for kv in range(NKV):
                    hs_ = slice(kv * REP, kv * REP + REP)
                    dve.tensor_tensor(q_out[:, kv, :, at], tmp[a][:, hs_, :], tmp[b][:, hs_, :], op)
                ins = dve.tensor_tensor(qkr[0:n, 8:10, at], tmp[a][:, 8:10, :], tmp[b][:, 8:10, :], op)
            ins.then_inc(S["qkr"], 1)

        def dve_residual(dve, tile, u, n):
            now(dve, "wom", tile)
            for c in range(2):
                ins = dve.tensor_tensor(x[u][0:n, 512 * c:512 * c + 512], x[u][0:n, 512 * c:512 * c + 512], bank[4 - c][0:n, :], ALU.add)
            ins.then_inc(S["hres"], 1)

        def dve_norm2(dve, tile, u, n, t_free):
            now(dve, "hs", tile)
            last(dve, "ttm", tile)
            dve.wait_ge(*t_free)
            dve.scalar_tensor_tensor(out=t[0:n, :], in0=x[u][0:n, :], scalar=rstd[0:n, 13:14], in1=norm2[0:n, :],
                                     op0=ALU.mult, op1=ALU.mult).then_inc(S["td"], 1)

        def dve_router(dve, tile, n, slot):
            now(dve, "lgm", tile)
            last(dve, "gex", tile)
            dve.tensor_tensor(lg[0:n, 0:NG], bank[7][0:n, 0:NG], b_route[0:n, 0:NG], ALU.add)
            dve.tensor_tensor(lg[0:n, 8:8 + NE], bank[7][0:n, NG:NG + NE], b_route[0:n, NG:NG + NE], ALU.add)
            dve.drain()
            dve.max(g8[0:n, :], lg[0:n, 0:8])
            dve.drain()
            dve.max_index(gi[0:n, :], g8[0:n, :], lg[0:n, 0:8])
            dve.tensor_scalar(rt[0:n, 0:1], g8[0:n, 0:1], -1.0, None, ALU.mult)
            dve.drain()
            dve.tensor_copy(fi[0:n, 0:1], gi[0:n, 0:1])
            dve.drain()
            dve.tensor_scalar(gmask[0:n, 0, :], con[0:n, C_IOTA:C_IOTA + NG], fi[0:n, 0:1], None, ALU.is_equal)
            dve.drain()
            dve.tensor_scalar(gmask[0:n, 1, :], gmask[0:n, 0, :], 1.0, BIG, ALU.subtract, ALU.mult)
            dve.tensor_tensor(le[0:n, :, :], lg[0:n, 8:8 + NE].rearrange("p (g e) -> p g e", g=NG),
                              gmask[0:n, 0, :].unsqueeze(2).to_broadcast([n, NG, EPG]), ALU.mult)
            dve.drain()
            dve.tensor_tensor(le[0:n, :, :], le[0:n, :, :], gmask[0:n, 1, :].unsqueeze(2).to_broadcast([n, NG, EPG]), ALU.add)
            dve.drain()
            fl = le[0:n, :, :].rearrange("p g e -> p (g e)")
            dve.max(e8[0:n, :], fl)
            dve.drain()
            dve.max_index(ei[0:n, :], e8[0:n, :], fl)
            dve.tensor_scalar(rt[0:n, 2:3], e8[0:n, 0:1], -1.0, None, ALU.mult).then_inc(S["sel"], 1)
            dve.drain()
            dve.tensor_copy(fi[0:n, 2:4], ei[0:n, 0:2])
            dve.drain()
            for k in range(2):
                dve.tensor_scalar(slot("onehot", n)[:, k], con[0:n, C_IOTA:C_IOTA + NE], fi[0:n, 2 + k:3 + k], None, ALU.is_equal)
            dve.drain()
            last(dve, "rankm", tile)
            dve.tensor_tensor(both[0:n, :], slot("onehot", n)[:, 0], slot("onehot", n)[:, 1], ALU.add).then_inc(S["rsel"], 1)

        def dve_rank_read(dve, tile, n):
            now(dve, "rankm", tile)
            dve.tensor_copy(rankc[0:n, :], bank[7][0:n, 0:NE]).then_inc(S["rankd"], 1)

        def dve_rank(dve, tile, n, slot):
            now(dve, "gex", tile)
            dve.tensor_scalar(rt[0:n, 4:5], rt[0:n, 3:4], 1.0, None, ALU.add)
            dve.drain()
            dve.tensor_tensor(rt[0:n, 4:5], rt[0:n, 4:5], rt[0:n, 1:2], ALU.mult)
            dve.drain()
            dve.reciprocal(slot("gate", n)[:, 0:1], rt[0:n, 4:5])
            dve.drain()
            dve.tensor_tensor(slot("gate", n)[:, 1:2], slot("gate", n)[:, 0:1], rt[0:n, 3:4], ALU.mult)
            dve.tensor_tensor(counted[0:n, :], counted[0:n, :], both[0:n, :], ALU.add)
            dve.drain()
            dve.tensor_tensor(rprod[0:n, :, :], slot("onehot", n), rankc[0:n, :].unsqueeze(1).to_broadcast([n, 2, NE]), ALU.mult)
            dve.drain()
            dve.tensor_reduce(slot("rank", n), rprod[0:n, :, :], AX.X, ALU.add)

        @block.vector
        def _(dve):
            credit(dve, "conva xT dtp qsq dta cum qkr qkc se smax prob ptb convd xdt rmin cbm md yf std yg gt hres td sel rsel rankd")
            dve.memset(v[:, :, :], 0.0)
            dve.memset(kT[:, :, :], 0.0)
            dve.memset(raw[:, :, 0:CK - 1], 0.0)
            dve.memset(hT[:, :, :], 0.0)
            dve.memset(counted[:, :], 0.0)
            dve.memset(onehot[:, TILES], 0.0)
            dve.memset(rank[:, TILES], 0.0)
            dve.memset(q_blk[:, :, :, :], 0.0)
            dve.memset(mask[:, 0, :], -BIG)
            dve.memset(lg[:, :], -BIG)
            dve.drain().then_inc(T["init"], 1)
            dve.wait_ge(first_in, 32)
            dve.tensor_copy(mask[:, 1, :], con[:, C_BAND + P:C_BAND + 2 * P])
            dve_xT(dve, 0, P)
            dve.wait_ge(params, N_PARAMS)
            dve.wait_ge(T["aneg"], 1)
            dve.tensor_scalar(a_neg[:, :], a_neg[:, :], -1.0, None, ALU.mult)
            dve.drain()
            dve_front(dve, 0, 0, P, 32)

            def dve_conv(tile, half):
                now(dve, ("rawa", "rawc")[half], tile)
                last(dve, "xcs ydm", tile)
                cc = range(4 * half, 4 * half + 4)
                for c in cc:
                    dve.tensor_scalar(cv[:, c, :], raw[:, c, 0:P], conv_w[:, c, 0:1], conv_b[:, c:c + 1], ALU.mult, ALU.add)
                for k in range(1, CK):
                    dve.drain()
                    for c in cc:
                        dve.scalar_tensor_tensor(out=cv[:, c, :], in0=raw[:, c, k:k + P], scalar=conv_w[:, c, k:k + 1],
                                                 in1=cv[:, c, :], op0=ALU.mult, op1=ALU.add)
                dve.drain()
                dve.tensor_copy(raw[:, cc[0]:cc[0] + 4, 0:CK - 1], raw[:, cc[0]:cc[0] + 4, P:P + CK - 1]).then_inc(S[("conva", "convd")[half]], 1)

            def dve_keys(tile):
                now(dve, "cumm", tile)
                last(dve, "ecd", tile)
                dve.tensor_copy(cum[:, 0, :], bank[7][:, 0:SH])
                dve.tensor_copy(cum[:, 2, :], bank[7][:, SH:2 * SH])
                dve.drain()
                dve.tensor_tensor(cum[:, 1, :], cum[:, 2, :], cum[:, 0, :], ALU.subtract).then_inc(S["cum"], 1)
                now(dve, "qkt", tile)
                last(dve, "sc3", tile)
                dve.tensor_copy(kT[:, 0, :], kT[:, 1, :])
                dve.drain()
                dve.tensor_copy(kT[:, 1, :], bank[6][:, 0:P])
                dve.tensor_copy(qT[:, :, :].rearrange("p a b -> p (a b)"), bank[2][:, :]).then_inc(S["qkc"], 1)

            dve_conv(0, 0)
            dve_conv(0, 1)
            dve_keys(0)

            def dve_tile(tile, u, n_next, x_need, t_free, slot):
                for i, b in enumerate((3, 4, 5, 6)):
                    now(dve, f"sc{i}", tile)
                    ins = dve.scalar_tensor_tensor(
                        out=s[:, 2 * i:2 * i + 2, :], in0=bank[b][:, :].rearrange("p (a b) -> p a b", a=2), scalar=SCALE,
                        in1=mask[:, :, :].rearrange("p a b -> p (a b)").unsqueeze(1).to_broadcast([P, 2, 2 * P]),
                        op0=ALU.mult, op1=ALU.add)
                ins.then_inc(S["se"], 1)
                dve_xT(dve, tile + 1, n_next)
                dve.drain()
                if slot is None:
                    dve.tensor_copy(mask[:, 0, :], con[:, C_BAND:C_BAND + P])
                dve.tensor_reduce(top[:, 0, :], s[:, :, :], AX.X, ALU.max)
                dve.drain()
                dve.tensor_tensor(top[:, 0, :], top[:, 0, :], sink[:, :], ALU.max)
                dve.drain()
                dve.tensor_scalar(top[:, 1, :], top[:, 0, :], -1.0, None, ALU.mult)
                dve.tensor_tensor(top[:, 3, :], sink[:, :], top[:, 0, :], ALU.subtract).then_inc(S["smax"], 1)
                now(dve, "rmm", tile)
                last(dve, "ydm", tile)
                for hh in range(SH):
                    ins = dve.tensor_scalar(m[:, hh, :], bank[5 + hh // 4][:, (hh % 4) * P:(hh % 4 + 1) * P],
                                            cum[:, 0, hh:hh + 1], 0.0, ALU.subtract, ALU.min)
                ins.then_inc(S["rmin"], 1)
                now(dve, "xtk", tile)
                dve.tensor_tensor(cbm[:, :, :], bank[3][:, 2 * P:4 * P].rearrange("p (g l) -> p g l", g=SG),
                                  tri.unsqueeze(1).to_broadcast([P, SG, P]), ALU.mult).then_inc(S["cbm"], 1)
                last(dve, "xde", tile)
                dve.tensor_tensor(xdt[:, :, :], xtok[:, :, :], dt[:, 3, :].unsqueeze(2).to_broadcast([P, SH, SP_]), ALU.mult).then_inc(S["xdt"], 1)
                if slot is not None:
                    dve_router(dve, tile - 1, P, slot)
                now(dve, "pexp", tile)
                dve.tensor_tensor(top[:, 2, :], top[:, 2, :], top[:, 3, :], ALU.add)
                dve.drain()
                dve.reciprocal(top[:, 2, :], top[:, 2, :])
                dve.drain()
                for hh in range(NH):
                    ins = dve.tensor_scalar(s[:, hh, :], s[:, hh, :], top[:, 2, hh:hh + 1], None, ALU.mult)
                ins.then_inc(S["prob"], 1)
                if slot is not None:
                    dve_rank_read(dve, tile - 1, P)
                now(dve, "rexpd", tile)
                for g in range(SG):
                    ins = dve.tensor_tensor(m[:, 4 * g:4 * g + 4, :], m[:, 4 * g:4 * g + 4, :],
                                            cbm[:, g:g + 1, :].to_broadcast([P, 4, P]), ALU.mult)
                ins.then_inc(S["md"], 1)
                if slot is not None:
                    dve_rank(dve, tile - 1, P, slot)
                now(dve, "ptm", tile)
                last(dve, "pv", tile)
                dve.tensor_copy(pT[:, 1, 0].rearrange("p a b -> p (a b)"), bank[3][:, :])
                dve.tensor_copy(pT[:, 1, 1].rearrange("p a b -> p (a b)"), bank[7][:, :]).then_inc(S["ptb"], 1)
                now(dve, "ydm ecd xd z", tile)
                fy = y[:, :, :].rearrange("p a b -> p (a b)")
                dve.tensor_tensor(y[:, :, :], bank[6][:, :].rearrange("p (a b) -> p a b", a=SH),
                                  ecum[:, 0, :].unsqueeze(2).to_broadcast([P, SH, SP_]), ALU.mult)
                dve.drain()
                dve.tensor_tensor(fy, fy, bank[5][:, :], ALU.add)
                dve.drain()
                dve.tensor_tensor(y[:, :, :], y[:, :, :], xd[:, :, :], ALU.add)
                dve.drain()
                dve.tensor_tensor(fy, fy, zs[:, :], ALU.mult).then_inc(S["yf"], 1)
                dve.tensor_tensor(hT[:, :, :], hT[:, :, :], ecum[:, 2, :].unsqueeze(2).to_broadcast([P, SH, SP_]), ALU.mult)
                dve.drain()
                now(dve, "stm", tile)
                dve.tensor_tensor(hT[:, :, :].rearrange("p a b -> p (a b)"), hT[:, :, :].rearrange("p a b -> p (a b)"),
                                  bank[2][:, :], ALU.add).then_inc(S["std"], 1)
                now(dve, "ys", tile)
                for g in range(SG):
                    ins = dve.tensor_scalar(y[:, 4 * g:4 * g + 4, :], y[:, 4 * g:4 * g + 4, :], rstd[:, 11 + g:12 + g], None, ALU.mult)
                ins.then_inc(S["yg"], 1)
                now(dve, "ytm", tile)
                last(dve, "wom", tile)
                dve.tensor_tensor(gT[:, :, :], bank[3][:, :].rearrange("p (c n) -> p c n", c=4),
                                  ssm_norm[:, :].unsqueeze(2).to_broadcast([P, 4, P]), ALU.mult).then_inc(S["gt"], 1)

                if n_next == DEC:
                    dve.wait_ge(kv_out, 32)
                dve_front(dve, tile + 1, 1 - u, n_next, x_need)
                if n_next == P:
                    dve_conv(tile + 1, 0)
                dve_residual(dve, tile, u, P)
                if n_next == P:
                    dve_keys(tile + 1)
                if slot is None:
                    dve.wait_ge(loaded, n_loaded[0])
                dve_norm2(dve, tile, u, P, t_free)
                if n_next == P:
                    dve_conv(tile + 1, 1)

            routed = {"onehot": onehot, "rank": rank, "gate": gate}
            dve_tile(0, 0, P, 32, (t_out[1], 16), None)
            with dve.Fori(0, TILES // 2 - 1) as pair:
                t0 = pair * 2
                for u in range(2):
                    dve_tile(t0 + (u + 1), 1 - u, P, 32 * pair + 64, (t_out[u], 16 * pair + 32),
                             lambda name, n: routed[name][0:n, bass.ds(t0 + u, 1)].squeeze(1))
            dve_tile(TILES - 1, 1, DEC, 16 * TILES + 32, (t_out[0], 8 * TILES + 16), lambda name, n: routed[name][0:n, TILES - 2])

            dve.wait_ge(T["q"], 1)
            for kv in range(NKV):
                r = slice(kv * HD, kv * HD + HD)
                ins = dve.tensor_copy(q_blk[r, :, kv, :], bank[4][r, 0:REP * DEC].rearrange("p (r b) -> p b r", b=DEC))
            ins.then_inc(T["q"], 1)
            dve.wait_ge(T["kT"], 1)
            dve.tensor_copy(keysT[:, 4:8, :].rearrange("p a b -> p (a b)"), bank[6][:, :]).then_inc(T["kT"], 1)
            dve.wait_ge(T["cv"], 1)
            new = bank[2][:, 0:CC * DEC].rearrange("p (c b) -> p c b", c=CC)
            old = bank[2][:, CC * DEC:CC * DEC * CK].rearrange("p (c b k) -> p c b k", c=CC, k=CK - 1)

            def tap(k):
                return conv_w[:, :, k:k + 1].to_broadcast([P, CC, DEC])
            dve.tensor_tensor(st_acc[:, :, :], new, tap(CK - 1), ALU.mult)
            dve.tensor_tensor(st_tmp[:, :, :], old[:, :, :, 0], tap(0), ALU.mult)
            dve.drain()
            dve.tensor_tensor(st_acc[:, :, :], st_acc[:, :, :], conv_b[:, :].unsqueeze(2).to_broadcast([P, CC, DEC]), ALU.add)
            for k in range(CK - 1):
                dve.drain()
                dve.tensor_tensor(st_acc[:, :, :], st_acc[:, :, :], st_tmp[:, :, :], ALU.add)
                if k < CK - 2:
                    dve.drain()
                    dve.tensor_tensor(st_tmp[:, :, :], old[:, :, :, k + 1], tap(k + 1), ALU.mult)
            dve.drain().then_inc(T["cv"], 1)
            now(dve, "projz", TILES)
            dve.wait_ge(T["dt"], 2)
            dve.tensor_copy(st_da[:, 0:2 * DEC], bank[3][0:SH, 0:2 * DEC])
            dve.tensor_copy(st_da[:, 2 * DEC:], d_col[:, :])
            dve.tensor_copy(head_sel.rearrange("p (h d) -> p h d", h=SH), ident[0:SH, 0:SH].unsqueeze(2).to_broadcast([SH, SH, SP_]))
            dve.drain().then_inc(T["xz"], 1)
            dve.wait_ge(T["att"], 1)
            for c in range(2):
                dve.tensor_reduce(m_top[:, 0, 4 * c:4 * c + 4], bank[c][0:NH, :].rearrange("p (b s) -> p b s", b=4), AX.X, ALU.max)
            dve.drain()
            dve.tensor_scalar(m_top[:, 0, :], m_top[:, 0, :], SCALE, sink_col[:, 0:1], ALU.mult, ALU.max)
            dve.drain()
            dve.tensor_scalar(m_top[:, 1, :], m_top[:, 0, :], -1.0, None, ALU.mult)
            dve.tensor_scalar(m_top[:, 3, :], m_top[:, 0, :], -1.0, sink_col[:, 0:1], ALU.mult, ALU.add)
            dve.drain().then_inc(T["att"], 1)
            dve.wait_ge(T["bcT"], 1)
            dve.tensor_copy(st_bc, bank[3][0:DEC, :]).then_inc(T["bcT"], 1)
            dve.tensor_copy(st_zT[:, :, :], bank[4][:, 0:4 * DEC].rearrange("p (c n) -> p c n", c=4))
            dve.wait_ge(T["xz"], 2)
            dve.tensor_copy(st_sc[:, :, :], bank[2][:, 0:4 * (2 * DEC + 1)].rearrange("p (c n) -> p c n", c=4))
            dve.drain()
            dve.tensor_tensor(st_dx[:, :, :], st_xT, st_sc[:, :, 0:DEC], ALU.mult)
            dve.drain().then_inc(T["xz"], 1)
            last_slot = lambda name, n: routed[name][0:n, TILES - 1]
            dve_router(dve, TILES - 1, P, last_slot)

            def dve_attention():
                dve.wait_ge(T["att"], 3)
                dve.tensor_tensor(m_top[:, 2, :], m_top[:, 2, :], m_top[:, 3, :], ALU.add)
                dve.drain()
                dve.reciprocal(m_top[:, 2, :], m_top[:, 2, :])
                dve.drain()
                dve.tensor_tensor(ps, ps, m_top[:, 2, :].unsqueeze(2).to_broadcast([NH, DEC, P]), ALU.mult)
                dve.drain().then_inc(T["att"], 1)

            def dve_early_choices(half):
                pairs = slice(half * EARLY // 2, (half + 1) * EARLY // 2)
                if half == 0:
                    dve.drain()
                    dve.tensor_tensor(chosen[:, 0:EARLY, :], flat_onehot[:, 0:EARLY, :],
                                      con[:, C_CHOICE:C_CHOICE + EARLY].unsqueeze(2).to_broadcast([P, EARLY, NE]), ALU.mult)
                dve.tensor_tensor(row_sel[half], con[:, C_IOTA:C_IOTA + P].unsqueeze(1).to_broadcast([P, EARLY // 2, P]),
                                  flat_rank[:, pairs].unsqueeze(2).to_broadcast([P, EARLY // 2, P]), ALU.is_equal).then_inc(T["part"], 1)

            def dve_state(b):
                if b < DEC:
                    dve.wait_ge(T["bx"], b + 1)
                    for c in range(4):
                        ins = dve.scalar_tensor_tensor(out=st_h[:, b, c, :], in0=st_h[:, b, c, :], scalar=st_sc[:, c, DEC + b:DEC + b + 1],
                                                       in1=st_bx[b % 2][:, c, :], op0=ALU.mult, op1=ALU.add)
                    ins.then_inc(T["hup"], 1)
                if b >= 1:
                    dve.wait_ge(T["ch"], b)
                    dve.tensor_reduce(st_y[:, :, b - 1], st_ch[(b - 1) % 2], AX.X, ALU.add).then_inc(T["hst"], 1)

            dve.wait_ge(state_in, 16 * DEC)
            dve_state(0)
            dve_state(1)
            dve_attention()
            dve_state(2)
            dve_rank_read(dve, TILES - 1, P)
            dve_rank(dve, TILES - 1, P, last_slot)
            dve_state(3)
            dve_state(4)
            dve.wait_ge(T["att"], 5)
            dve.tensor_copy(ps_T[:, :, :].rearrange("p b h -> p (b h)"), bank[5][:, 0:DEC * NH]).then_inc(T["att"], 1)
            dve_state(5)
            dve_state(6)
            dve.wait_ge(T["att"], 7)
            for kv in range(NKV):
                r = slice(kv * HD, kv * HD + HD)
                ins = dve.tensor_copy(aT[r, :, 0:DEC], bank[0][r, 0:DEC * NH].rearrange("p (b k r) -> p k r b", b=DEC, k=NKV)[:, kv])
            ins.then_inc(T["att"], 1)
            dve_state(7)
            dve_state(8)
            dve.drain()
            dve.tensor_tensor(st_g2[:, :, :], st_xT, st_sc[:, :, 2 * DEC:].to_broadcast([P, 4, DEC]), ALU.mult)
            dve.drain()
            dve.tensor_tensor(st_y[:, :, :], st_y[:, :, :], st_g2[:, :, :], ALU.add)
            dve.drain()
            dve.tensor_tensor(st_y[:, :, :], st_y[:, :, :], st_zT[:, :, :], ALU.mult)
            dve.drain()
            dve.tensor_tensor(st_g2[:, :, :], st_y[:, :, :], st_y[:, :, :], ALU.mult)
            dve.drain().then_inc(T["norm"], 1)
            dve.wait_ge(T["norm"], 2)
            dve.tensor_copy(st_g2[:, :, :].rearrange("p a b -> p (a b)"), bank[5][:, 0:4 * DEC])
            dve.drain()
            for g in range(SG):
                ins = dve.tensor_tensor(st_n[:, g, :], st_g2[:, 2 * g, :], st_g2[:, 2 * g + 1, :], ALU.add)
            ins.then_inc(T["norm"], 1)
            dve.wait_ge(T["ssmT"], 1)
            dve.tensor_copy(st_turned, bank[1][:, :].rearrange("p (c n) -> p c n", c=4)).then_inc(T["ssmT"], 1)
            dve_early_choices(0)
            dve_early_choices(1)
            dve.wait_ge(T["norm"], 4)
            for g in range(SG):
                dve.tensor_tensor(st_y[:, 2 * g:2 * g + 2, :], st_y[:, 2 * g:2 * g + 2, :], st_r[:, g:g + 1, :].to_broadcast([P, 2, DEC]), ALU.mult)
            dve.drain()
            dve.tensor_tensor(gT[:, :, 0:DEC], st_y[:, :, :], ssm_norm[:, :].unsqueeze(2).to_broadcast([P, 4, DEC]), ALU.mult).then_inc(T["norm"], 1)
            dve_residual(dve, TILES, 0, DEC)
            dve_norm2(dve, TILES, 0, DEC, (t_out[1], 8 * TILES + 16))
            sample_slot = lambda name, n: routed[name][0:n, TILES]
            dve_router(dve, TILES, DEC, sample_slot)
            dve_rank_read(dve, TILES, DEC)
            dve_rank(dve, TILES, DEC, sample_slot)

            def slot_table(at, n):
                dve.drain()
                dve.tensor_scalar(slot_f[:, 1, 0:n], slot_f[:, 0, 0:n], float(TOKENS), -float(TOKENS), ALU.is_ge, ALU.mult)
                dve.tensor_copy(slot_tab[:, at:at + n, 1], slot_f[:, 0, 0:n])
                dve.drain()
                dve.tensor_tensor(slot_tab[:, at:at + n, 0], slot_f[:, 0, 0:n], slot_f[:, 1, 0:n], ALU.add)
                return dve.drain()

            dve.drain().then_inc(T["cnt"], 1)
            dve.tensor_tensor(chosen[:, EARLY:PAIRS, :], flat_onehot[:, EARLY:PAIRS, :],
                              con[:, C_CHOICE + EARLY:C_CHOICE + PAIRS].unsqueeze(2).to_broadcast([P, 2, NE]), ALU.mult)
            dve.tensor_tensor(row_sel[2], con[:, C_IOTA:C_IOTA + P].unsqueeze(1).to_broadcast([P, 2, P]),
                              flat_rank[:, EARLY:PAIRS].unsqueeze(2).to_broadcast([P, 2, P]), ALU.is_equal).then_inc(T["slots"], 1)
            dve.wait_ge(T["slots"], 2)
            dve.tensor_scalar(slot_f[:, 0, :], bank[1][:, 0:NE], float(EMPTY), None, ALU.add)
            slot_table(0, NE).then_inc(T["slots"], 1)
            dve.wait_ge(T["cnt"], 2)
            dve.tensor_copy(nt[:, 0, :], bank[0][:, 0:NE])
            dve.drain()
            dve.tensor_scalar(nt[:, 1, :], nt[:, 0, :], float(ROWS), None, ALU.is_gt)
            dve.drain()
            for j in range(2, (TOKENS + ROWS - 1) // ROWS):
                dve.scalar_tensor_tensor(out=nt[:, 1, :], in0=nt[:, 0, :], scalar=float(ROWS * j), in1=nt[:, 1, :], op0=ALU.is_gt, op1=ALU.add)
                dve.drain()
            dve.tensor_tensor_scan(nt[:, 2, :], con[:, C_ONES:C_ONES + NE], nt[:, 1, :], 0.0, ALU.mult, ALU.add)
            dve.drain()
            dve.tensor_copy(over_i[:, :], nt[0:1, 2, NE - 1:NE])
            dve.tensor_tensor(nt[:, 3, :], nt[:, 2, :], nt[:, 1, :], ALU.subtract)
            dve.tensor_tensor(ecmp, nt[0:1, 2:3, :].to_broadcast([1, OVER_TILES, NE]),
                              con[0:1, C_IOTA:C_IOTA + OVER_TILES].unsqueeze(2).to_broadcast([1, OVER_TILES, NE]), ALU.is_le)
            dve.drain()
            dve.tensor_reduce(etile, ecmp, AX.X, ALU.add)
            dve.drain()
            dve.tensor_scalar(etile, etile, float(NE - 1), None, ALU.min)
            dve.drain()
            dve.tensor_copy(etile_i[:, :], etile)
            dve.drain().then_inc(T["et"], 1)

            dve.sem_inc(E_["yd"], 1)
            dve.wait_ge(outs, N_OUTS)

            def dve_turned(j, w):
                dve.wait_ge(E_["turn"], j + 1)
                dve.tensor_copy(xgT[w % 2][:, 4:8, :].rearrange("p a b -> p (a b)"), bank[w % 2 * 2 + 1][:, :]).then_inc(E_["xd"], 1)

            def dve_expert(j, w, stored, more=True):
                u = w % 2
                dve.wait_ge(E_["sil"], j + 1)
                dve.tensor_tensor(hidT[u], sil[u], bank[4 + u][:, P:2 * P], ALU.mult).then_inc(E_["hid"], 1)
                if more:
                    dve_turned(j + 1, (w + 1) % RING)
                dve.wait_ge(E_["dn"], j + 2)
                if stored is not None:
                    dve.wait_ge(e_out[u], stored)
                dve.tensor_copy(yo[u][:, 512:D], bank[7][:, :]).then_inc(E_["yd"], 1)

            dve_turned(0, 0)
            for w in range(RING):
                dve_expert(w, w, 16 * (w // 2) if w >= 2 else None)
            with dve.Fori(1, NE // RING - 1) as group:
                for w in range(RING):
                    dve_expert(RING * group + w, w, 32 * group + 16 * (w // 2))
            for w in range(RING):
                j = NE - RING + w
                dve_expert(j, w, 16 * (j // 2), w < RING - 1)
            over = dve.value_load(over_i[0:1, 0:1], min_val=0, max_val=OVER_TILES)
            with dve.If(over > 0):
                dve.tensor_scalar(quo[:, 0, :], flat_rank, float(ROWS), None, ALU.is_ge)
                dve.drain()
                dve.tensor_tensor(quo[:, 3, :], quo[:, 0, :], con[:, C_CHOICE:C_CHOICE + PAIRS], ALU.mult)
                for j in range(2, (TOKENS + ROWS - 1) // ROWS):
                    dve.scalar_tensor_tensor(out=quo[:, 0, :], in0=flat_rank, scalar=float(ROWS * j), in1=quo[:, 0, :], op0=ALU.is_ge, op1=ALU.add)
                    dve.drain()
                dve.scalar_tensor_tensor(out=quo[:, 1, :], in0=quo[:, 0, :], scalar=-float(ROWS), in1=flat_rank, op0=ALU.mult, op1=ALU.add)
                dve.tensor_tensor(pair_prod, flat_onehot, nt[:, 3:4, :].to_broadcast([P, PAIRS, NE]), ALU.mult)
                dve.drain()
                dve.tensor_reduce(quo[:, 2, :], pair_prod, AX.X, ALU.add)
                dve.drain()
                dve.scalar_tensor_tensor(out=quo[:, 2, :], in0=quo[:, 0, :], scalar=-1.0, in1=quo[:, 2, :], op0=ALU.add, op1=ALU.add)
                dve.drain()
                over_chosen = pair_prod[:, :, 0:OVER_TILES]
                dve.tensor_tensor(over_chosen, con[:, C_IOTA:C_IOTA + OVER_TILES].unsqueeze(1).to_broadcast([P, PAIRS, OVER_TILES]),
                                  quo[:, 2, :].unsqueeze(2).to_broadcast([P, PAIRS, OVER_TILES]), ALU.is_equal)
                dve.drain()
                dve.tensor_tensor(over_chosen, over_chosen, quo[:, 3, :].unsqueeze(2).to_broadcast([P, PAIRS, OVER_TILES]), ALU.mult)
                for a in range(3):
                    dve.tensor_tensor(over_sel[a], con[:, C_IOTA:C_IOTA + P].unsqueeze(1).to_broadcast([P, THIRD, P]),
                                      quo[:, 1, a * THIRD:(a + 1) * THIRD].unsqueeze(2).to_broadcast([P, THIRD, P]), ALU.is_equal).then_inc(T["over"], 1)
                dve.wait_ge(T["over"], 4)
                dve.tensor_scalar(slot_f[:, 0, 0:OVER_TILES], bank[1][:, 0:OVER_TILES], float(EMPTY), None, ALU.add)
                slot_table(NE, OVER_TILES).then_inc(T["over"], 1)
                with dve.Fori(0, OVER_TILES) as j:
                    dve.wait_ge(V["sil"], j + 1)
                    dve.tensor_tensor(hidT[0], sil[0], bank[4][:, P:2 * P], ALU.mult).then_inc(V["hid"], 1)

            dve.wait_ge(c_in, 16 * TILES)
            for c in range(TILES + 1):
                n, w = (P if c < TILES else DEC), c % 4
                dve.wait_ge(c_in1[w], 32 * (c // 4 + 1))
                for k in range(2):
                    ins = dve.scalar_tensor_tensor(out=c_h[c][0:n, :], in0=c_y[w][k][0:n, :], scalar=gate[0:n, c, k:k + 1], in1=c_h[c][0:n, :],
                                                   op0=ALU.mult, op1=ALU.add)
                    if k == 0:
                        dve.drain()
                ins.then_inc(c_done, 1)

        def root_mean(pool, col, count, n, done):
            pool.tensor_tensor(stat[0:n, col:col + count], stat[0:n, col:col + count], eps[0:n, 0:count], ALU.add)
            pool.drain()
            pool.tensor_tensor(rstd[0:n, col:col + count], stat[0:n, col:col + count], neg_half[0:n, 0:count], ALU.pow).then_inc(S[done], 1)

        @block.gpsimd
        def _(pool):
            credit(pool, "xs qs xde xd ys hs")
            pool.memset(neg_half[:, :], -0.5)
            pool.memset(eps[:, :], EPS)
            pool.drain()

            def pool_rows(tile, n):
                now(pool, "ssq", tile)
                last(pool, "xn", tile)
                root_mean(pool, 0, 1, n, "xs")

            def pool_qk(tile, n):
                now(pool, "qsq", tile)
                last(pool, "qkr", tile)
                root_mean(pool, 1, 10, n, "qs")

            def pool_h(tile, n):
                now(pool, "hsq", tile)
                last(pool, "td", tile)
                root_mean(pool, 13, 1, n, "hs")

            def pool_tile(tile, n_next):
                pool_rows(tile + 1, n_next)
                now(pool, "xtk", tile)
                last(pool, "yf", tile)
                pool.tensor_tensor(xd[:, :, :], xtok[:, :, :], d_skip[:, :].unsqueeze(2).to_broadcast([P, SH, SP_]), ALU.mult).then_inc(S["xd"], 1)
                now(pool, "xdt ecd", tile)
                last(pool, "stm", tile)
                pool.tensor_tensor(xde[:, :, :], xdt[:, :, :], ecum[:, 1, :].unsqueeze(2).to_broadcast([P, SH, SP_]), ALU.mult).then_inc(S["xde"], 1)
                now(pool, "ysq", tile)
                last(pool, "yg", tile)
                root_mean(pool, 11, 2, P, "ys")
                pool_qk(tile + 1, n_next)
                pool_h(tile, P)

            pool_rows(0, P)
            pool_qk(0, P)
            pool.wait_ge(params, N_PARAMS)
            pool_tile(0, P)
            with pool.Fori(0, TILES // 2 - 1) as pair:
                for u in range(2):
                    pool_tile(pair * 2 + (u + 1), P)
            pool_tile(TILES - 1, DEC)
            for b in range(DEC):
                pool.wait_ge(T["hup"], b + 1)
                if b >= 2:
                    pool.wait_ge(T["hst"], b - 1)
                for g in range(SG):
                    ins = pool.tensor_tensor(st_ch[b % 2][:, 2 * g:2 * g + 2, :], st_h[:, b, 2 * g:2 * g + 2, :],
                                             st_cs[b % 2][:, g:g + 1, :].to_broadcast([P, 2, P]), ALU.mult)
                ins.then_inc(T["ch"], 1)
            pool.wait_ge(T["norm"], 3)
            pool.tensor_scalar(st_n[:, :, :], st_n[:, :, :], 1.0 / 256, EPS, ALU.mult, ALU.add)
            pool.drain()
            pool.tensor_tensor(st_r[:, :, :].rearrange("p a b -> p (a b)"), st_n[:, :, :].rearrange("p a b -> p (a b)"), neg_half[:, 0:SG * DEC], ALU.pow).then_inc(T["norm"], 1)
            pool_h(TILES, DEC)

            def fetch_index(idx, j, which):
                return pool.tensor_copy(idx[:, :], slot_tab[:, bass.ds(j, 1), which])

            def gather(into, idx, landed):
                pool.indirect_dma_start(into, None, t_dram, bass.IndirectOffsetOnAxis(ap=idx[:, :].bitcast(U32), axis=0),
                                        bounds_check=TOKENS - 1, oob_is_err=False).then_inc(landed, 16)

            def scatter(out, idx, landed):
                pool.indirect_dma_start(y_dram, bass.IndirectOffsetOnAxis(ap=idx[:, :].bitcast(U32), axis=0), out, None,
                                        bounds_check=CHOICES - 1, oob_is_err=False).then_inc(landed, 16)

            def pool_expert(j, w, left=NE):
                pool.wait_ge(E_["ya"], j + 2)
                pool.wait_ge(E_["yd"], j + 2)
                pool.wait_ge(E_["idx"], j + 2)
                if left > 1:
                    ins = fetch_index(idx_out[(w + 1) % RING], j + 1, 1)
                if left > RING + 1:
                    ins = fetch_index(idx_in[(w + 1) % RING], j + RING + 1, 0)
                if left > 1:
                    ins.then_inc(E_["idx"], 1)
                scatter(yo[w % 2], idx_out[w], e_out[w % 2])
                if left > RING:
                    gather(xg[w], idx_in[w], e_x[w])

            pool.wait_ge(T["slots"], 3)
            for u in range(2):
                pool.wait_ge(t_out[u], 16 + 16 * ((TILES + 2 - u) // 2))
                pool.wait_ge(h_out[u], 16 + 16 * ((TILES + 2 - u) // 2))
            pool.wait_ge(outs, N_OUTS)
            fetch_index(idx_in[0], 0, 0)
            pool.drain()
            gather(xg[0], idx_in[0], e_x[0])
            for w in range(1, RING):
                fetch_index(idx_in[w], w, 0)
            fetch_index(idx_out[0], 0, 1).then_inc(E_["idx"], 1)
            pool.wait_ge(E_["idx"], 1)
            for w in range(1, RING):
                gather(xg[w], idx_in[w], e_x[w])
            pool.wait_ge(e_x[0], 16)
            fetch_index(idx_in[0], RING, 0).then_inc(E_["idx"], 1)
            for w in range(RING):
                pool_expert(w, w)
            with pool.Fori(1, NE // RING - 2) as group:
                for w in range(RING):
                    pool_expert(RING * group + w, w)
            for w in range(2 * RING):
                pool_expert(NE - 2 * RING + w, w % RING, 2 * RING - w)
            pool.wait_ge(T["et"], 1)
            over = pool.value_load(over_i[0:1, 0:1], min_val=0, max_val=OVER_TILES)
            with pool.If(over > 0):
                pool.wait_ge(T["over"], 5)
                for u in range(2):
                    pool.wait_ge(e_out[u], 16 * NE // 2)
                with pool.Fori(0, OVER_TILES) as j:
                    pool.wait_ge(V["dn"], j + 1)
                    fetch_index(idx_in[0], j + NE, 0)
                    pool.drain()
                    gather(xg[0], idx_in[0], o_x)
                    pool.wait_ge(V["ye"], j + 2)
                    fetch_index(idx_out[0], j + NE, 1)
                    pool.drain()
                    scatter(yo[0], idx_out[0], o_out)
                    pool.wait_ge(o_out, 16 * j + 16)

        def pe_turn_x(pe, src, ids, n, banks, done):
            for k in range(KC):
                cols = src.rearrange("t (p k) -> t k p", k=KC)[:, k, :]
                ins = pe.transpose(bank[banks[k // 4]][:, (k % 4) * n:(k % 4 + 1) * n], cols, ids)
            ins.then_inc(done, 1)

        def pe_rows(pe, tile, n):
            now(pe, "xn", tile)
            last(pe, "rawc z", tile)
            pe_turn_x(pe, xn[0:n, :], ident[0:n, 0:n], n, (0, 1), S["xm"])

        def project(pe, out, n, cols, landed=()):
            for one, count in landed:
                pe.wait_ge(one, count)
            for k in range(KC):
                ins = pe.matmul(out, xT[:, k, 0:n], w_in[:, k, cols], start=k == 0, stop=k == KC - 1)
            return ins

        def pe_q(pe, tile, n, landed=()):
            now(pe, "xT", tile)
            project(pe, bank[0][0:n, :], n, slice(0, Q_END), landed).then_inc(S["projq"], 1)

        def pe_kv(pe, tile, n, landed=()):
            project(pe, bank[1][0:n, 0:W_Z - Q_END], n, slice(Q_END, W_Z), landed).then_inc(S["projk"], 1)

        def pe_xbc(pe, tile, n, half):
            now(pe, ("qe", "qkv")[half], tile)
            if n == P:
                for c in range(4):
                    at = W_XBC + (4 * half + c) * P
                    for k in range(KC):
                        ins = pe.matmul(bank[half][:, c * P:(c + 1) * P], w_in[:, k, at:at + P], xT[:, k, :], start=k == 0, stop=k == KC - 1)
            else:
                at = W_XBC + 512 * half
                ins = project(pe, bank[half][0:n, :], n, slice(at, at + 512))
            ins.then_inc(S[("proja", "projc")[half]], 1)

        def pe_z(pe, tile, n, landed=()):
            now(pe, "rawa", tile)
            project(pe, bank[0][0:n, :], n, slice(W_Z, W_XBC), landed).then_inc(S["projz"], 1)

        def pe_out(pe, tile, n):
            for c in range(2):
                for k in range(KC):
                    lhs = aT[:, k, 0:n] if k < REP else gT[:, k - REP, 0:n]
                    ins = pe.matmul(bank[4 - c][0:n, :], lhs, w_out[:, k, 512 * c:512 * c + 512], start=k == 0, stop=k == KC - 1)
            ins.then_inc(S["wom"], 1)

        def pe_out_half(pe, n, half, columns):
            for c in columns:
                for k in range(half * REP, half * REP + REP):
                    lhs = gT[:, k - REP, 0:n] if half else aT[:, k, 0:n]
                    ins = pe.matmul(bank[4 - c][0:n, :], lhs, w_out[:, k, 512 * c:512 * c + 512], start=k == 0, stop=k == KC - 1)
            return ins

        def pe_turn_t(pe, tile, n):
            now(pe, "td", tile)
            pe_turn_x(pe, t[0:n, :], ident[0:n, 0:n], n, (5, 6), S["ttm"])

        def pe_router(pe, tile, n):
            now(pe, "tt", tile)
            for k in range(KC):
                ins = pe.matmul(bank[7][0:n, 0:NG + NE], tT[:, k, 0:n], w_route[:, k, :], start=k == 0, stop=k == KC - 1)
            ins.then_inc(S["lgm"], 1)

        def pe_rank(pe, tile, n):
            now(pe, "rsel", tile)
            pe.matmul(bank[7][0:n, 0:NE], strict[0:n, 0:n], both[0:n, :], start=True, stop=False)
            pe.matmul(bank[7][0:n, 0:NE], ones[:, 0:n], counted[:, :], start=False, stop=True).then_inc(S["rankm"], 1)

        @block.tensor
        def _(pe):
            credit(pe, "xm projq projk projz proja projc cumm qkt sc0 sc1 sc2 sc3 ptm pv xtm rmm ydm stm ytm wom ttm lgm rankm")
            pe.wait_ge(first_in, 32)
            pe_rows(pe, 0, P)
            pe_q(pe, 0, P, ((w_q, 16),))
            pe_kv(pe, 0, P, ((w_kv, 32),))
            for half in range(2):
                pe.wait_ge(w_x[half], 16)
                pe_xbc(pe, 0, P, half)

            def pe_keys(tile):
                now(pe, "dta", tile)
                pe.matmul(bank[7][:, 0:SH], tri, dt[:, 4, :], start=True, stop=True)
                pe.matmul(bank[7][:, SH:2 * SH], ones, dt[:, 4, :], start=True, stop=True).then_inc(S["cumm"], 1)
                now(pe, "qkr", tile)
                for r in range(REP):
                    pe.transpose(bank[2][:, r * P:(r + 1) * P], qkr[:, 2 * r:2 * r + 2, :].rearrange("p a b -> p (a b)"), ident)
                pe.transpose(bank[6][:, 0:P], qkr[:, 8:10, :].rearrange("p a b -> p (a b)"), ident).then_inc(S["qkt"], 1)

            pe_z(pe, 0, P, ((w_z, 16),))
            pe_keys(0)
            pe.wait_ge(T["init"], 1)

            def pe_tile(tile, n_next, first=False):
                nxt = tile + 1
                now(pe, "qkc", tile)
                last(pe, "hres", tile)
                for i, b in enumerate((3, 4, 5, 6)):
                    if i == 2 and not first:
                        now(pe, "tt", tile - 1)
                    for j in range(2):
                        kv, r = (2 * i + j) // REP, (2 * i + j) % REP
                        rr = slice(kv * HD, kv * HD + HD)
                        ins = pe.matmul(bank[b][:, j * 256:(j + 1) * 256], qT[rr, r, :], kT[rr, :, :].rearrange("p a b -> p (a b)"),
                                        start=True, stop=True)
                    ins.then_inc(S[f"sc{i}"], 1)
                if not first:
                    pe_router(pe, tile - 1, P)
                pe_rows(pe, nxt, n_next)
                now(pe, "xcs se", tile)
                for g in range(SG):
                    pe.matmul(bank[3][:, (2 + g) * P:(3 + g) * P], xc[:, 4 + g, :], xc[:, 6 + g, :], start=True, stop=True)
                for c in (4, 5, 0, 1, 2, 3):
                    ins = pe.transpose(bank[2 + c // 4][:, (c % 4) * P:(c % 4 + 1) * P], xc[:, c, :], ident)
                ins.then_inc(S["xtm"], 1)
                for hh in range(SH):
                    ins = pe.matmul(bank[5 + hh // 4][:, (hh % 4) * P:(hh % 4 + 1) * P], dt[:, 4, hh:hh + 1].to_broadcast([P, P]), tri,
                                    start=True, stop=True)
                ins.then_inc(S["rmm"], 1)
                pe_q(pe, nxt, n_next)
                pe_kv(pe, nxt, n_next)
                if not first:
                    pe_rank(pe, tile - 1, P)
                now(pe, "prob xtk cbm", tile)
                for kv in range(NKV):
                    for blk in range(2):
                        if kv == 1 and blk == 1 and not first:
                            now(pe, "rankd", tile - 1)
                        for r in range(REP):
                            ins = pe.transpose(bank[(4, 2, 3, 7)[kv * 2 + blk]][:, r * P:(r + 1) * P], s[:, kv * REP + r, blk * P:(blk + 1) * P], ident)
                ins.then_inc(S["ptm"], 1)
                now(pe, "md xdt rmin", tile)
                last(pe, "std", tile)
                for hh in range(SH):
                    pe.matmul(bank[5][:, hh * SP_:(hh + 1) * SP_], m[:, hh, :], xdt[:, hh, :], start=True, stop=True)
                for g in range(SG):
                    ins = pe.matmul(bank[6][:, g * 256:(g + 1) * 256], xc[:, 6 + g, :], hT[:, 4 * g:4 * g + 4, :].rearrange("p a b -> p (a b)"),
                                    start=True, stop=True)
                ins.then_inc(S["ydm"], 1)
                now(pe, "pta ptb vc", tile)
                for kv in range(NKV):
                    for blk in range(2):
                        ins = pe.matmul(bank[4][kv * HD:(kv + 1) * HD, :], v[:, blk, kv * HD:(kv + 1) * HD],
                                        pT[:, kv, blk].rearrange("p a b -> p (a b)"), start=blk == 0, stop=blk == 1)
                ins.then_inc(S["pv"], 1)
                now(pe, "xde", tile)
                for g in range(SG):
                    ins = pe.matmul(bank[2][:, g * 256:(g + 1) * 256], btok[:, g, :], xde[:, 4 * g:4 * g + 4, :].rearrange("p a b -> p (a b)"),
                                    start=True, stop=True)
                ins.then_inc(S["stm"], 1)
                pe_xbc(pe, nxt, n_next, 0)
                now(pe, "yg", tile)
                for c in range(4):
                    ins = pe.transpose(bank[3][:, c * P:(c + 1) * P], y[:, 2 * c:2 * c + 2, :].rearrange("p a b -> p (a b)"), ident)
                ins.then_inc(S["ytm"], 1)
                pe_xbc(pe, nxt, n_next, 1)
                if first:
                    pe.wait_ge(loaded, n_loaded[0])
                now(pe, "at gt std", tile)
                pe_out(pe, tile, P)
                if n_next == P:
                    pe_keys(nxt)
                pe_z(pe, nxt, n_next)
                if n_next == P:
                    now(pe, "qkc", nxt)
                pe_turn_t(pe, tile, P)

            pe_tile(0, P, first=True)
            with pe.Fori(0, TILES // 2 - 1) as pair:
                for u in range(2):
                    pe_tile(pair * 2 + (u + 1), P)
            pe_tile(TILES - 1, DEC)
            i8 = ident[0:DEC, 0:DEC]
            now(pe, "rawc", TILES)
            for c in range(CC):
                pe.transpose(bank[2][:, c * DEC:(c + 1) * DEC], st_raw[:, c * P:(c + 1) * P], i8)
            pe.wait_ge(conv_in, 16)
            rows3 = DEC * (CK - 1)
            for c in range(CC):
                at = CC * DEC + c * rows3
                ins = pe.transpose(bank[2][:, at:at + rows3], st_conv[:, c * P:(c + 1) * P], ident[0:rows3, 0:rows3])
            ins.then_inc(T["cv"], 1)
            now(pe, "qkr", TILES)
            last(pe, "hres", TILES)
            for r in range(REP):
                ins = pe.transpose(bank[4][:, r * DEC:(r + 1) * DEC], qkr[0:DEC, 2 * r:2 * r + 2, :].rearrange("p a b -> p (a b)"), i8)
            ins.then_inc(T["q"], 1)
            now(pe, "tt", TILES - 1)
            pe.wait_ge(cache_in, 64)
            for b in range(DEC):
                ins = pe.transpose(bank[5 + b // 4][:, (b % 4) * P:(b % 4 + 1) * P], keys[:, b, :], ident)
            ins.then_inc(T["kT"], 1)
            pe_router(pe, TILES - 1, P)
            pe.wait_ge(T["dt"], 1)
            pe.transpose(bank[3][0:SH, 0:DEC], dt[0:DEC, 3, :], i8)
            pe.transpose(bank[3][0:SH, DEC:2 * DEC], dt[0:DEC, 4, :], i8).then_inc(T["dt"], 1)
            pe.wait_ge(T["q"], 2)
            pe.wait_ge(T["kT"], 3)
            now(pe, "qkv z", TILES)
            for b in range(DEC):
                ins = pe.matmul(bank[b // 4][0:NH, (b % 4) * P:(b % 4 + 1) * P], q_blk[:, b].rearrange("p k r -> p (k r)"), keysT[:, b, :],
                                start=True, stop=True)
            ins.then_inc(T["att"], 1)
            pe.wait_ge(T["xz"], 1)
            for c in range(4):
                ins = pe.matmul(bank[2][:, c * (2 * DEC + 1):(c + 1) * (2 * DEC + 1)],
                                head_sel[:, c * P:(c + 1) * P], st_da[:, :], start=True, stop=True)
            ins.then_inc(T["xz"], 1)
            pe.wait_ge(T["cv"], 3)
            for c in range(4):
                pe.transpose(bank[3][0:DEC, c * P:(c + 1) * P], st_xc[:, 4 + c, :], ident)
            for c in range(4):
                ins = pe.transpose(bank[4][:, c * DEC:(c + 1) * DEC], zs[0:DEC, c * P:(c + 1) * P], i8)
            ins.then_inc(T["bcT"], 1)
            pe.wait_ge(T["bcT"], 2)
            pe.wait_ge(T["xz"], 3)

            def pe_choices(pairs, sel, rhs, start=True, stop=True):
                for i in pairs:
                    lhs, at = sel(i)
                    ins = pe.matmul(bank[1][:, 0:rhs.shape[2]], lhs[:, at, :], rhs[:, i, :], start=start and i == pairs[0], stop=stop and i == pairs[-1])
                return ins

            half = EARLY // 2

            def early(i):
                return row_sel[i // half], i % half

            for b in range(DEC):
                if b >= 2:
                    pe.wait_ge(T["bx"], b - 1)
                pe.matmul(bank[(6, 2)[b % 2]][:, :], ident[0:DEC, b:b + 1].to_broadcast([DEC, P]), st_bc,
                          start=True, stop=True).then_inc(T["bc"], 1)
                if b == 2:
                    pe_rank(pe, TILES - 1, P)
                if b == 4:
                    pe.wait_ge(T["att"], 4)
                    for q in range(DEC):
                        ins = pe.transpose(bank[5][:, q * NH:(q + 1) * NH], ps[:, q, :], i8)
                    ins.then_inc(T["att"], 1)
                if b == 6:
                    pe.wait_ge(T["att"], 6)
                    for q in range(DEC):
                        ins = pe.matmul(bank[0][:, q * NH:(q + 1) * NH], vals[:, q, :], ps_T[:, q, :], start=True, stop=True)
                    ins.then_inc(T["att"], 1)
                if b == 7:
                    for c in range(4):
                        ins = pe.transpose(bank[1][:, c * P:(c + 1) * P], hT[:, 2 * c:2 * c + 2, :].rearrange("p a b -> p (a b)"), ident)
                    ins.then_inc(T["ssmT"], 1)
            pe.wait_ge(T["att"], 8)
            pe_out_half(pe, DEC, 0, (0,))
            pe.wait_ge(T["norm"], 1)
            pe.matmul(bank[5][:, 0:4 * DEC], ones, st_g2[:, :, :].rearrange("p a b -> p (a b)"), start=True, stop=True).then_inc(T["norm"], 1)
            pe_out_half(pe, DEC, 0, (1,))
            pe.wait_ge(T["norm"], 5)
            pe_out_half(pe, DEC, 1, (0, 1)).then_inc(S["wom"], 1)
            pe.wait_ge(T["part"], 2)
            pe.wait_ge(T["ssmT"], 2)
            pe_choices(range(0, half), early, chosen, stop=False)
            pe_turn_t(pe, TILES, DEC)
            pe_router(pe, TILES, DEC)
            pe_choices(range(half, EARLY), early, chosen, start=False, stop=False)
            pe_rank(pe, TILES, DEC)
            pe.wait_ge(T["cnt"], 1)
            pe.matmul(bank[0][:, 0:NE], ones, counted[:, :], start=True, stop=True).then_inc(T["cnt"], 1)
            pe.wait_ge(T["slots"], 1)
            pe_choices(range(EARLY, PAIRS), lambda i: (row_sel[2], i - EARLY), chosen, start=False).then_inc(T["slots"], 1)

            pe.sem_inc(E_["dn"], 1)
            pe.sem_inc(V["dn"], 1)
            pe.wait_ge(T["et"], 1)

            def expert_up(w, out, done, gu=None):
                gu = wgu[w] if gu is None else gu
                for a in range(2):
                    for k in range(KC):
                        ins = pe.matmul(out[:, a * P:(a + 1) * P], gu[:, a, k, :], xgT[w % 2][:, k, :], start=k == 0, stop=k == KC - 1)
                ins.then_inc(done, 1)

            def expert_down(w, done, down=None):
                down = wd[w] if down is None else down
                for c in range(2):
                    ins = pe.matmul(bank[6 + c][:, :], hidT[w % 2], down[:, 512 * c:512 * c + 512], start=True, stop=True)
                ins.then_inc(done, 1)

            def pe_turn(j, w, gathered):
                pe.wait_ge(e_x[w], gathered)
                pe_turn_x(pe, xg[w], ident, P, (w % 2 * 2, w % 2 * 2 + 1), E_["turn"])

            def pe_expert(j, w, group, more=True, late=None):
                pe.wait_ge(E_["xa"], j + 1)
                pe.wait_ge(E_["xd"], j + 1)
                if late is None:
                    pe.wait_ge(e_w[w], 48 * group + 48)
                else:
                    pe.wait_ge(e_w_late, 96)
                expert_up(w, bank[4 + w % 2], E_["up"], None if late is None else late_wgu[late])
                if more:
                    pe_turn(j + 1, (w + 1) % RING, 16 * group + (16 if w < RING - 1 else 32))
                pe.wait_ge(E_["hid"], j + 1)
                pe.wait_ge(E_["ya"], j + 1)
                pe.wait_ge(E_["yd"], j + 1)
                expert_down(w, E_["dn"], None if late is None else late_wd[late])

            pe_turn(0, 0, 16)
            for w in range(RING):
                pe_expert(w, w, 0)
            with pe.Fori(1, NE // RING - 1) as group:
                for w in range(RING):
                    pe_expert(RING * group + w, w, group)
            for w in range(RING):
                pe_expert(NE - RING + w, w, NE // RING - 1, w < RING - 1, w - (RING - 2) if w >= RING - 2 else None)
            over = pe.value_load(over_i[0:1, 0:1], min_val=0, max_val=OVER_TILES)
            with pe.If(over > 0):
                pe.wait_ge(T["over"], 3)
                pe_choices(range(PAIRS), lambda i: (over_sel[i // THIRD], i % THIRD), pair_prod[:, :, 0:OVER_TILES]).then_inc(T["over"], 1)
                pe.wait_ge(T["over"], 5)
                pe.wait_ge(E_["ya"], NE + 1)
                pe.wait_ge(E_["yd"], NE + 1)
                with pe.Fori(0, OVER_TILES) as j:
                    pe.wait_ge(o_x, 16 * j + 16)
                    pe_turn_x(pe, xg[0], ident, P, (0, 1), V["turn"])
                    pe.wait_ge(V["xe"], j + 1)
                    pe.wait_ge(o_w, 48 * j + 48)
                    expert_up(0, bank[4], V["up"])
                    pe.wait_ge(V["hid"], j + 1)
                    pe.wait_ge(V["ye"], j + 1)
                    expert_down(0, V["dn"])


OUTS = [("y_prompt", (1, SEQ, D)), ("y_sample", (DEC, 1, D)), ("win_k_prompt", (1, 1, P, NKV, HD)), ("win_v_prompt", (1, 1, P, NKV, HD)),
        ("conv_prompt", (P, CC, CK - 1)), ("ssm_prompt", (1, 1, SH, SP_, SN)), ("win_k_sample", (1, DEC, P, NKV, HD)),
        ("win_v_sample", (1, DEC, P, NKV, HD)), ("conv_sample", (1, DEC, CK - 1, CD)), ("ssm_sample", (1, DEC, SH, SP_, SN))]
N_OUTS = 16 * (1 + 2 + 2 + 2 + 1 + DEC)


def kernel(**inputs):
    import concourse.bacc as bacc
    from concourse.bass_utils import run_bass_kernel_spmd

    nc = bacc.Bacc("TRN2", target_bir_lowering=False, num_devices=1)
    arrays, ins, outs = {}, {}, {}
    given = dict(inputs, constants=shape_constants(), rope=rope_table())
    given["conv_w_by_channel"] = np.asarray(inputs["conv_w"])[0].reshape(CK, CC, P).transpose(2, 1, 0)
    given["conv_b_by_channel"] = np.asarray(inputs["conv_b"])[0].reshape(CC, P).T
    given["ssm_norm_by_channel"] = np.asarray(inputs["ssm_norm"])[0].reshape(4, P).T
    for name, a in given.items():
        a = np.ascontiguousarray(a)
        arrays[f"in_{name}"] = a
        ins[name] = nc.dram_tensor(f"in_{name}", a.shape, mybir.dt.from_np(a.dtype), kind="ExternalInput").ap()
    for name, shape in OUTS:
        outs[name] = nc.dram_tensor(f"out_{name}", shape, F32, kind="ExternalOutput").ap()
    layer_kernel(nc, ins, outs)
    r = run_bass_kernel_spmd(nc, [arrays], core_ids=[0])
    got = {name: r.results[0][f"out_{name}"] for name, _ in OUTS}
    got["conv_prompt"] = got["conv_prompt"].transpose(2, 1, 0).reshape(1, 1, CK - 1, CD)
    return tuple(got[name] for name, _ in OUTS)
```
